# Optimizing a Trainium2 kernel written in Bass

```python
import math
import jax, jax.numpy as jnp
from jax import lax
import numpy as np

D_MODEL = 1024
BATCH = 1
SEQ = 512
DEPTH = 2

N_EVEN = (DEPTH + 1) // 2
N_ODD = DEPTH // 2
ALPHA = (2 * DEPTH) ** 0.25
BETA = (8 * DEPTH) ** -0.25
LN_EPS = 1e-5

SC_WIDTH = D_MODEL
SC_KERNEL = 3

SSM_INNER = D_MODEL
SSM_HEADDIM = 64
SSM_HEADS = SSM_INNER // SSM_HEADDIM
SSM_GROUPS = 2
SSM_STATE = 128
SSM_CONV = 4
SSM_CHUNK = 128
SSM_XBC = SSM_INNER + 2 * SSM_GROUPS * SSM_STATE
MIX0_IN = 3 * SC_WIDTH + SSM_INNER + SSM_XBC + SSM_HEADS
MIX0_OUT = SC_WIDTH + SSM_INNER

FOX_HEADS = 16
FOX_HEADDIM = D_MODEL // FOX_HEADS
FOX_WIDTH = FOX_HEADS * FOX_HEADDIM
FOX_IN = 3 * FOX_WIDTH + FOX_HEADS
FOX_BLOCK = 128

D_FF = 2816
FFN_KERNEL = 3


def _split(h, sizes):
    idx = np.cumsum(sizes)[:-1].tolist()
    return jnp.split(h, idx, axis=-1)

def causal_dwconv(x, w, b=None):
    k, c = w.shape
    y = lax.conv_general_dilated(x, w[:, None, :].astype(x.dtype), window_strides=(1,), padding=[(k - 1, 0)], dimension_numbers=('NWC', 'WIO', 'NWC'), feature_group_count=c)
    return y if b is None else y + b.astype(y.dtype)

def layer_norm(x, g, b):
    xf = x.astype(jnp.float32)
    mu = jnp.mean(xf, -1, keepdims=True)
    var = jnp.mean(jnp.square(xf - mu), -1, keepdims=True)
    return ((xf - mu) * lax.rsqrt(var + LN_EPS) * g + b).astype(x.dtype)

def gated_rmsnorm(y, z, g):
    bsz, l, _ = y.shape
    u = (y.astype(jnp.float32) * jax.nn.silu(z.astype(jnp.float32))).reshape(bsz, l, SSM_GROUPS, -1)
    u = u * lax.rsqrt(jnp.mean(jnp.square(u), -1, keepdims=True) + LN_EPS)
    return (u.reshape(bsz, l, SSM_INNER) * g).astype(y.dtype)

def ssd_chunked(xs, dt, a, bm, cm):
    bsz, l = xs.shape[:2]
    nc, q, r = l // SSM_CHUNK, SSM_CHUNK, SSM_HEADS // SSM_GROUPS
    x = xs.astype(jnp.float32).reshape(bsz, nc, q, SSM_GROUPS, r, SSM_HEADDIM)
    dtc = dt.reshape(bsz, nc, q, SSM_GROUPS, r)
    xdt = x * dtc[..., None]
    bc = bm.astype(jnp.float32).reshape(bsz, nc, q, SSM_GROUPS, SSM_STATE)
    cc = cm.astype(jnp.float32).reshape(bsz, nc, q, SSM_GROUPS, SSM_STATE)
    a_cs = jnp.cumsum((dtc * a.reshape(SSM_GROUPS, r)).transpose(0, 1, 3, 4, 2), axis=-1)
    causal = jnp.tril(jnp.ones((q, q), dtype=bool))
    seg = jnp.exp(jnp.where(causal, a_cs[..., :, None] - a_cs[..., None, :], -jnp.inf))
    cb = jnp.einsum('bctgn,bcsgn->bcgts', cc, bc)
    y_diag = jnp.einsum('bcgts,bcgrts,bcsgrp->bctgrp', cb, seg, xdt)
    decay_to_end = jnp.exp(a_cs[..., -1:] - a_cs)
    chunk_states = jnp.einsum('bcsgn,bcgrs,bcsgrp->bcgrpn', bc, decay_to_end, xdt)
    chunk_decay = jnp.exp(a_cs[..., -1])

    def step(h, inp):
        st, dec = inp
        return h * dec[..., None, None] + st, h

    h0 = jnp.zeros((bsz, SSM_GROUPS, r, SSM_HEADDIM, SSM_STATE), jnp.float32)
    _, prev = lax.scan(step, h0, (jnp.moveaxis(chunk_states, 1, 0), jnp.moveaxis(chunk_decay, 1, 0)))
    prev = jnp.moveaxis(prev, 0, 1)
    y_off = jnp.einsum('bctgn,bcgrpn,bcgrt->bctgrp', cc, prev, jnp.exp(a_cs))
    return (y_diag + y_off).reshape(bsz, l, SSM_HEADS, SSM_HEADDIM)

def sconv_ssd_mixer(x, w_in, sc_conv_w, ssm_conv_w, ssm_conv_b, dt_bias, a_log, d_skip, norm_g, w_out):
    bsz, l, _ = x.shape
    h = x @ w_in
    sc_b, sc_c, sc_h, z, xbc, dt_raw = _split(h, [SC_WIDTH, SC_WIDTH, SC_WIDTH, SSM_INNER, SSM_XBC, SSM_HEADS])
    y_a = sc_b * causal_dwconv(sc_c * sc_h, sc_conv_w)
    xbc = jax.nn.silu(causal_dwconv(xbc, ssm_conv_w, ssm_conv_b))
    xs, bm, cm = _split(xbc, [SSM_INNER, SSM_GROUPS * SSM_STATE, SSM_GROUPS * SSM_STATE])
    xs = xs.reshape(bsz, l, SSM_HEADS, SSM_HEADDIM)
    dt = jax.nn.softplus(dt_raw.astype(jnp.float32) + dt_bias.astype(jnp.float32))
    a = -jnp.exp(a_log.astype(jnp.float32))
    y = ssd_chunked(xs, dt, a, bm.reshape(bsz, l, SSM_GROUPS, SSM_STATE), cm.reshape(bsz, l, SSM_GROUPS, SSM_STATE))
    y = y + d_skip.astype(jnp.float32)[:, None] * xs.astype(jnp.float32)
    y_b = gated_rmsnorm(y.reshape(bsz, l, SSM_INNER).astype(x.dtype), z, norm_g)
    return jnp.concatenate([y_a, y_b], axis=-1) @ w_out

def fox_mixer(x, w_in, b_f, w_out):
    bsz, l, _ = x.shape
    nb = l // FOX_BLOCK
    h = x @ w_in
    q, k, v, f_logit = _split(h, [FOX_WIDTH, FOX_WIDTH, FOX_WIDTH, FOX_HEADS])
    heads = lambda t: t.reshape(bsz, l, FOX_HEADS, FOX_HEADDIM).transpose(0, 2, 1, 3)
    q, k, v = heads(q), heads(k), heads(v)
    log_f = jax.nn.log_sigmoid(f_logit.astype(jnp.float32) + b_f.astype(jnp.float32))
    cum = jnp.cumsum(log_f, axis=1).transpose(0, 2, 1)
    scale = FOX_HEADDIM ** -0.5
    key_pos = jnp.arange(l)

    def block(args):
        q_blk, cum_blk, i = args
        qpos = i * FOX_BLOCK + jnp.arange(FOX_BLOCK)
        s = jnp.einsum('bhqd,bhkd->bhqk', q_blk, k).astype(jnp.float32) * scale + cum_blk[..., None] - cum[:, :, None, :]
        s = jnp.where(key_pos[None, :] <= qpos[:, None], s, -jnp.inf)
        p = jax.nn.softmax(s, axis=-1)
        return jnp.einsum('bhqk,bhkd->bhqd', p.astype(v.dtype), v)

    q_blocks = q.reshape(bsz, FOX_HEADS, nb, FOX_BLOCK, FOX_HEADDIM).transpose(2, 0, 1, 3, 4)
    cum_blocks = cum.reshape(bsz, FOX_HEADS, nb, FOX_BLOCK).transpose(2, 0, 1, 3)
    o = lax.map(block, (q_blocks, cum_blocks, jnp.arange(nb)))
    o = o.transpose(1, 0, 3, 2, 4).reshape(bsz, l, FOX_WIDTH)
    return o @ w_out

def conv_ffn(x, w_up, conv_w, conv_b, w_down):
    h = causal_dwconv(x @ w_up, conv_w, conv_b)
    u, g = _split(h, [D_FF, D_FF])
    return (u * jax.nn.silu(g)) @ w_down

def first_inputs(seed: int = 0) -> dict:
    key = jax.random.key(seed)
    ks = jax.random.split(key, 21)
    f32 = jnp.float32

    def nrm(k, shape, scale):
        return jax.random.normal(k, shape, f32) * scale

    x = nrm(ks[0], (BATCH, SEQ, D_MODEL), 1.0)
    sc_ssm_w_in = nrm(ks[1], (N_EVEN, D_MODEL, MIX0_IN), D_MODEL ** -0.5)
    sc_conv_w = nrm(ks[2], (N_EVEN, SC_KERNEL, SC_WIDTH), SC_KERNEL ** -0.5)
    ssm_conv_w = nrm(ks[3], (N_EVEN, SSM_CONV, SSM_XBC), SSM_CONV ** -0.5)
    ssm_conv_b = nrm(ks[4], (N_EVEN, SSM_XBC), 0.02)
    dt0 = jnp.exp(jax.random.uniform(ks[5], (N_EVEN, SSM_HEADS), f32, minval=math.log(1e-3), maxval=math.log(1e-1)))
    ssm_dt_bias = dt0 + jnp.log(-jnp.expm1(-dt0))
    ssm_a_log = jnp.log(jax.random.uniform(ks[6], (N_EVEN, SSM_HEADS), f32, minval=1.0, maxval=16.0))
    ssm_d = 1.0 + nrm(ks[7], (N_EVEN, SSM_HEADS), 0.1)
    ssm_norm_g = 1.0 + nrm(ks[8], (N_EVEN, SSM_INNER), 0.02)
    sc_ssm_w_out = nrm(ks[9], (N_EVEN, MIX0_OUT, D_MODEL), BETA * MIX0_OUT ** -0.5)
    col_scale = jnp.concatenate([jnp.ones((2 * FOX_WIDTH,), f32), jnp.full((FOX_WIDTH,), BETA, f32), jnp.ones((FOX_HEADS,), f32)])
    fox_w_in = nrm(ks[10], (N_ODD, D_MODEL, FOX_IN), D_MODEL ** -0.5) * col_scale
    fox_b_f = jax.random.uniform(ks[11], (N_ODD, FOX_HEADS), f32, minval=1.0, maxval=4.0)
    fox_w_out = nrm(ks[12], (N_ODD, FOX_WIDTH, D_MODEL), BETA * FOX_WIDTH ** -0.5)
    ffn_w_up = nrm(ks[13], (DEPTH, D_MODEL, 2 * D_FF), BETA * D_MODEL ** -0.5)
    ffn_conv_w = nrm(ks[14], (DEPTH, FFN_KERNEL, 2 * D_FF), FFN_KERNEL ** -0.5)
    ffn_conv_b = nrm(ks[15], (DEPTH, 2 * D_FF), 0.02)
    ffn_w_down = nrm(ks[16], (DEPTH, D_FF, D_MODEL), BETA * D_FF ** -0.5)
    ln_mix_g = 1.0 + nrm(ks[17], (DEPTH, D_MODEL), 0.02)
    ln_mix_b = nrm(ks[18], (DEPTH, D_MODEL), 0.02)
    ln_ffn_g = 1.0 + nrm(ks[19], (DEPTH, D_MODEL), 0.02)
    ln_ffn_b = nrm(ks[20], (DEPTH, D_MODEL), 0.02)
    return {'x': x, 'sc_ssm_w_in': sc_ssm_w_in, 'sc_conv_w': sc_conv_w, 'ssm_conv_w': ssm_conv_w, 'ssm_conv_b': ssm_conv_b, 'ssm_dt_bias': ssm_dt_bias, 'ssm_a_log': ssm_a_log, 'ssm_d': ssm_d, 'ssm_norm_g': ssm_norm_g, 'sc_ssm_w_out': sc_ssm_w_out, 'fox_w_in': fox_w_in, 'fox_b_f': fox_b_f, 'fox_w_out': fox_w_out, 'ffn_w_up': ffn_w_up, 'ffn_conv_w': ffn_conv_w, 'ffn_conv_b': ffn_conv_b, 'ffn_w_down': ffn_w_down, 'ln_mix_g': ln_mix_g, 'ln_mix_b': ln_mix_b, 'ln_ffn_g': ln_ffn_g, 'ln_ffn_b': ln_ffn_b}

def first_block(x, sc_ssm_w_in, sc_conv_w, ssm_conv_w, ssm_conv_b, ssm_dt_bias, ssm_a_log, ssm_d, ssm_norm_g, sc_ssm_w_out, fox_w_in, fox_b_f, fox_w_out, ffn_w_up, ffn_conv_w, ffn_conv_b, ffn_w_down, ln_mix_g, ln_mix_b, ln_ffn_g, ln_ffn_b):
    for i in range(DEPTH):
        j = i // 2
        if i % 2 == 0:
            mix = sconv_ssd_mixer(x, sc_ssm_w_in[j], sc_conv_w[j], ssm_conv_w[j], ssm_conv_b[j], ssm_dt_bias[j], ssm_a_log[j], ssm_d[j], ssm_norm_g[j], sc_ssm_w_out[j])
        else:
            mix = fox_mixer(x, fox_w_in[j], fox_b_f[j], fox_w_out[j])
        x = layer_norm(ALPHA * x + mix, ln_mix_g[i], ln_mix_b[i])
        x = layer_norm(ALPHA * x + conv_ffn(x, ffn_w_up[i], ffn_conv_w[i], ffn_conv_b[i], ffn_w_down[i]), ln_ffn_g[i], ln_ffn_b[i])
    return x


DEPTH_2 = 1

HEAD_DIM = 64
DIFF_HEADS = 8
DIFF_VDIM = 2 * HEAD_DIM
NSA_HEADS = 16
NSA_GROUPS = 4
NSA_HPG = NSA_HEADS // NSA_GROUPS
CMP_BLOCK = 32
CMP_STRIDE = 16
CMP_HIDDEN = 256
SEL_BLOCK = 64
SEL_TOP = 16
WINDOW = 512
FORCED_SCORE = 1e4
D_FF_2 = 4 * D_MODEL
ROPE_THETA = 10000.0
EPS = 1e-6
Q_BLOCK = 128

DIFF_QK = DIFF_HEADS * 2 * HEAD_DIM
DIFF_V = DIFF_HEADS * DIFF_VDIM
NSA_Q = NSA_HEADS * HEAD_DIM
NSA_KV = NSA_GROUPS * HEAD_DIM
NSA_GATE = NSA_HEADS * 3
MERGE_GATE = 2 * D_MODEL
COLUMN_SPLITS = (DIFF_QK, DIFF_QK, DIFF_V, NSA_Q, NSA_KV, NSA_KV, NSA_KV, NSA_KV, NSA_KV, NSA_KV, NSA_GATE, MERGE_GATE)
D_IN = DIFF_QK * 2 + DIFF_V + NSA_Q + 6 * NSA_KV + NSA_GATE + MERGE_GATE


def rmsnorm(x, g):
    xf = x.astype(jnp.float32)
    y = xf * lax.rsqrt(jnp.mean(xf * xf, axis=-1, keepdims=True) + EPS)
    return (y * g.astype(jnp.float32)).astype(x.dtype)

def rope(x, pos):
    half = x.shape[-1] // 2
    inv_freq = ROPE_THETA ** (-jnp.arange(half, dtype=jnp.float32) / half)
    ang = pos.astype(jnp.float32)[:, None] * inv_freq[None, :]
    bshape = (1, ang.shape[0]) + (1,) * (x.ndim - 3) + (half,)
    cos = jnp.cos(ang).reshape(bshape)
    sin = jnp.sin(ang).reshape(bshape)
    xf = x.astype(jnp.float32)
    x1, x2 = xf[..., :half], xf[..., half:]
    return jnp.concatenate([x1 * cos - x2 * sin, x2 * cos + x1 * sin], axis=-1).astype(x.dtype)

def masked_softmax(s, mask):
    s = jnp.where(mask, s.astype(jnp.float32), -jnp.inf)
    m = jnp.max(s, axis=-1, keepdims=True)
    m = jnp.where(jnp.isfinite(m), m, 0.0)
    e = jnp.where(mask, jnp.exp(s - m), 0.0)
    return e / jnp.maximum(jnp.sum(e, axis=-1, keepdims=True), 1e-30)

def diff_attention(q, k, v, lam, lambda_init, subln_g):
    B, S, H, _, Dh = q.shape
    scale = Dh ** -0.5
    kpos = jnp.arange(S)

    def block(i):
        q0 = i * Q_BLOCK
        qb = lax.dynamic_slice_in_dim(q, q0, Q_BLOCK, axis=1)
        s = jnp.einsum('bqhcd,bkhcd->bhcqk', qb, k).astype(jnp.float32) * scale
        qpos = q0 + jnp.arange(Q_BLOCK)
        causal = kpos[None, :] <= qpos[:, None]
        p = jax.nn.softmax(jnp.where(causal, s, -jnp.inf), axis=-1)
        a = p[:, :, 0] - lam * p[:, :, 1]
        return jnp.einsum('bhqk,bkhe->bqhe', a.astype(v.dtype), v)

    o = lax.map(block, jnp.arange(S // Q_BLOCK))
    o = o.transpose(1, 0, 2, 3, 4).reshape(B, S, H, -1)
    o = rmsnorm(o, subln_g) * (1.0 - lambda_init)
    return o.reshape(B, S, H * o.shape[-1])

def compress(kv, pos_emb, w1, w2):
    B, S, G, Dh = kv.shape
    n_cmp = (S - CMP_BLOCK) // CMP_STRIDE + 1
    idx = jnp.arange(n_cmp)[:, None] * CMP_STRIDE + jnp.arange(CMP_BLOCK)[None, :]
    blocks = kv[:, idx] + pos_emb[None, None, :, None, :]
    blocks = blocks.transpose(0, 1, 3, 2, 4).reshape(B, n_cmp, G, CMP_BLOCK * Dh)
    return jax.nn.gelu(blocks @ w1) @ w2

def nsa_attention(q, k_cmp, v_cmp, k_slc, v_slc, k_win, v_win, gates):
    B, S, Hq, Dh = q.shape
    G, Hg = NSA_GROUPS, NSA_HPG
    scale = Dh ** -0.5
    dt = v_slc.dtype
    n_cmp = k_cmp.shape[1]
    n_sel = S // SEL_BLOCK
    n_top = min(SEL_TOP, n_sel)
    cmp_start = jnp.arange(n_cmp) * CMP_STRIDE
    cmp_end = cmp_start + CMP_BLOCK - 1
    sel_start = jnp.arange(n_sel) * SEL_BLOCK
    sel_ids = jnp.arange(n_sel)
    overlap = ((cmp_start[:, None] < sel_start[None, :] + SEL_BLOCK)
               & (cmp_end[:, None] >= sel_start[None, :])).astype(jnp.float32)
    k_blk = k_slc.reshape(B, n_sel, SEL_BLOCK, G, Dh).transpose(0, 3, 1, 2, 4)
    v_blk = v_slc.reshape(B, n_sel, SEL_BLOCK, G, Dh).transpose(0, 3, 1, 2, 4)
    kw_pad = jnp.pad(k_win, ((0, 0), (WINDOW, 0), (0, 0), (0, 0)))
    vw_pad = jnp.pad(v_win, ((0, 0), (WINDOW, 0), (0, 0), (0, 0)))
    b_idx = jnp.arange(B)[:, None, None, None]
    g_idx = jnp.arange(G)[None, :, None, None]

    def block(i):
        q0 = i * Q_BLOCK
        qpos = q0 + jnp.arange(Q_BLOCK)
        qb = lax.dynamic_slice_in_dim(q, q0, Q_BLOCK, axis=1).reshape(B, Q_BLOCK, G, Hg, Dh)
        gb = lax.dynamic_slice_in_dim(gates, q0, Q_BLOCK, axis=1)
        s = jnp.einsum('bqghd,bngd->bghqn', qb, k_cmp) * scale
        p_cmp = masked_softmax(s, cmp_end[None, :] <= qpos[:, None])
        o_cmp = jnp.einsum('bghqn,bngd->bqghd', p_cmp.astype(dt), v_cmp)
        imp = jnp.einsum('bghqn,nj->bgqj', p_cmp, overlap)
        cur = qpos // SEL_BLOCK
        forced = (sel_ids[None, :] == 0) | (sel_ids[None, :] == cur[:, None]) | (sel_ids[None, :] == cur[:, None] - 1)
        imp = jnp.where(forced, FORCED_SCORE, imp)
        imp = jnp.where(sel_start[None, :] <= qpos[:, None], imp, -jnp.inf)
        top_val, top_idx = lax.top_k(imp, n_top)
        sel_ok = jnp.isfinite(top_val)
        ks = k_blk[b_idx, g_idx, top_idx]
        vs = v_blk[b_idx, g_idx, top_idx]
        s = jnp.einsum('bqghd,bgqnld->bghqnl', qb, ks) * scale
        tok_pos = top_idx[..., None] * SEL_BLOCK + jnp.arange(SEL_BLOCK)
        m = sel_ok[..., None] & (tok_pos <= qpos[None, None, :, None, None])
        p = masked_softmax(s.reshape(B, G, Hg, Q_BLOCK, n_top * SEL_BLOCK),
                           m.reshape(B, G, 1, Q_BLOCK, n_top * SEL_BLOCK))
        p = p.reshape(B, G, Hg, Q_BLOCK, n_top, SEL_BLOCK)
        o_slc = jnp.einsum('bghqnl,bgqnld->bqghd', p.astype(dt), vs)
        kw = lax.dynamic_slice_in_dim(kw_pad, q0, WINDOW + Q_BLOCK, axis=1)
        vw = lax.dynamic_slice_in_dim(vw_pad, q0, WINDOW + Q_BLOCK, axis=1)
        kwpos = q0 - WINDOW + jnp.arange(WINDOW + Q_BLOCK)
        dist = qpos[:, None] - kwpos[None, :]
        s = jnp.einsum('bqghd,bkgd->bghqk', qb, kw) * scale
        p = masked_softmax(s, (dist >= 0) & (dist < WINDOW) & (kwpos[None, :] >= 0))
        o_win = jnp.einsum('bghqk,bkgd->bqghd', p.astype(dt), vw)
        shp = (B, Q_BLOCK, Hq, Dh)
        return (gb[..., 0:1] * o_cmp.reshape(shp) + gb[..., 1:2] * o_slc.reshape(shp)
                + gb[..., 2:3] * o_win.reshape(shp))

    o = lax.map(block, jnp.arange(S // Q_BLOCK))
    return o.transpose(1, 0, 2, 3, 4).reshape(B, S, Hq * Dh)

def second_inputs(seed: int = 0) -> dict:
    key = jax.random.key(seed)
    k = jax.random.split(key, 26)
    f32 = jnp.float32
    nrm = lambda kk, shape, sc: jax.random.normal(kk, shape, f32) * sc
    gain = lambda kk, shape: 1.0 + 0.02 * jax.random.normal(kk, shape, f32)
    L = DEPTH_2
    return {
        "x": jax.random.normal(k[0], (BATCH, SEQ, D_MODEL), f32),
        "ln_mix_g": gain(k[1], (L, D_MODEL)),
        "w_in": nrm(k[2], (L, D_MODEL, D_IN), D_MODEL ** -0.5),
        "diff_q_norm_g": gain(k[3], (L, HEAD_DIM)),
        "diff_k_norm_g": gain(k[4], (L, HEAD_DIM)),
        "diff_lambda_q1": nrm(k[5], (L, HEAD_DIM), 0.1),
        "diff_lambda_k1": nrm(k[6], (L, HEAD_DIM), 0.1),
        "diff_lambda_q2": nrm(k[7], (L, HEAD_DIM), 0.1),
        "diff_lambda_k2": nrm(k[8], (L, HEAD_DIM), 0.1),
        "diff_subln_g": gain(k[9], (L, DIFF_VDIM)),
        "nsa_q_norm_g": gain(k[10], (L, HEAD_DIM)),
        "nsa_k_norm_g": gain(k[11], (L, 3, HEAD_DIM)),
        "cmp_pos_k": nrm(k[12], (L, CMP_BLOCK, HEAD_DIM), 0.1),
        "cmp_pos_v": nrm(k[13], (L, CMP_BLOCK, HEAD_DIM), 0.1),
        "cmp_k_w1": nrm(k[14], (L, CMP_BLOCK * HEAD_DIM, CMP_HIDDEN), (CMP_BLOCK * HEAD_DIM) ** -0.5),
        "cmp_k_w2": nrm(k[15], (L, CMP_HIDDEN, HEAD_DIM), CMP_HIDDEN ** -0.5),
        "cmp_v_w1": nrm(k[16], (L, CMP_BLOCK * HEAD_DIM, CMP_HIDDEN), (CMP_BLOCK * HEAD_DIM) ** -0.5),
        "cmp_v_w2": nrm(k[17], (L, CMP_HIDDEN, HEAD_DIM), CMP_HIDDEN ** -0.5),
        "w_proj_diff": nrm(k[18], (L, DIFF_V, D_MODEL), DIFF_V ** -0.5),
        "w_proj_nsa": nrm(k[19], (L, NSA_Q, D_MODEL), NSA_Q ** -0.5),
        "w_out": nrm(k[20], (L, D_MODEL, D_MODEL), D_MODEL ** -0.5),
        "ln_mlp_g": gain(k[21], (L, D_MODEL)),
        "w_mlp_up": nrm(k[22], (L, D_MODEL, D_FF_2), D_MODEL ** -0.5),
        "w_mlp_down": nrm(k[23], (L, D_FF_2, D_MODEL), D_FF_2 ** -0.5),
    }

def second_block(x, ln_mix_g, w_in, diff_q_norm_g, diff_k_norm_g, diff_lambda_q1, diff_lambda_k1,
              diff_lambda_q2, diff_lambda_k2, diff_subln_g, nsa_q_norm_g, nsa_k_norm_g,
              cmp_pos_k, cmp_pos_v, cmp_k_w1, cmp_k_w2, cmp_v_w1, cmp_v_w2,
              w_proj_diff, w_proj_nsa, w_out, ln_mlp_g, w_mlp_up, w_mlp_down):
    B, S, D = x.shape
    G = NSA_GROUPS
    pos = jnp.arange(S)
    n_cmp = (S - CMP_BLOCK) // CMP_STRIDE + 1
    cmp_center = jnp.arange(n_cmp) * CMP_STRIDE + (CMP_BLOCK - 1) / 2.0
    split_at = [int(c) for c in np.cumsum(COLUMN_SPLITS)[:-1]]
    for l in range(DEPTH_2):
        h = rmsnorm(x, ln_mix_g[l])
        proj = h @ w_in[l]
        (dq, dk, dv, nq, kc, vc, ksl, vsl, kwn, vwn, ng, mg) = jnp.split(proj, split_at, axis=-1)
        dq = rope(rmsnorm(dq.reshape(B, S, DIFF_HEADS, 2, HEAD_DIM), diff_q_norm_g[l]), pos)
        dk = rope(rmsnorm(dk.reshape(B, S, DIFF_HEADS, 2, HEAD_DIM), diff_k_norm_g[l]), pos)
        dv = dv.reshape(B, S, DIFF_HEADS, DIFF_VDIM)
        lambda_init = 0.8 - 0.6 * math.exp(-0.3 * l)
        lam = (jnp.exp(jnp.sum(diff_lambda_q1[l].astype(jnp.float32) * diff_lambda_k1[l].astype(jnp.float32)))
               - jnp.exp(jnp.sum(diff_lambda_q2[l].astype(jnp.float32) * diff_lambda_k2[l].astype(jnp.float32)))
               + lambda_init)
        y_diff = diff_attention(dq, dk, dv, lam, lambda_init, diff_subln_g[l])
        nq = rope(rmsnorm(nq.reshape(B, S, NSA_HEADS, HEAD_DIM), nsa_q_norm_g[l]), pos)
        k_cmp = compress(kc.reshape(B, S, G, HEAD_DIM), cmp_pos_k[l], cmp_k_w1[l], cmp_k_w2[l])
        k_cmp = rope(rmsnorm(k_cmp, nsa_k_norm_g[l, 0]), cmp_center)
        v_cmp = compress(vc.reshape(B, S, G, HEAD_DIM), cmp_pos_v[l], cmp_v_w1[l], cmp_v_w2[l])
        k_slc = rope(rmsnorm(ksl.reshape(B, S, G, HEAD_DIM), nsa_k_norm_g[l, 1]), pos)
        k_win = rope(rmsnorm(kwn.reshape(B, S, G, HEAD_DIM), nsa_k_norm_g[l, 2]), pos)
        nsa_gates = jax.nn.sigmoid(ng).reshape(B, S, NSA_HEADS, 3)
        y_nsa = nsa_attention(nq, k_cmp, v_cmp, k_slc, vsl.reshape(B, S, G, HEAD_DIM), k_win,
                              vwn.reshape(B, S, G, HEAD_DIM), nsa_gates)
        merge = jax.nn.sigmoid(mg).reshape(B, S, 2, D)
        mixed = merge[:, :, 0] * (y_diff @ w_proj_diff[l]) + merge[:, :, 1] * (y_nsa @ w_proj_nsa[l])
        x = x + mixed @ w_out[l]
        h = rmsnorm(x, ln_mlp_g[l])
        x = x + jnp.square(jax.nn.relu(h @ w_mlp_up[l])) @ w_mlp_down[l]
    return x


def setup_inputs(seed=0):
    out = dict(first_inputs(seed))
    for name, value in second_inputs(seed + 1).items():
        if name != "x":
            out[name + "_2"] = value
    return out


def reference(
    x, sc_ssm_w_in, sc_conv_w, ssm_conv_w, ssm_conv_b, ssm_dt_bias, ssm_a_log, ssm_d,
    ssm_norm_g, sc_ssm_w_out, fox_w_in, fox_b_f, fox_w_out, ffn_w_up, ffn_conv_w, ffn_conv_b,
    ffn_w_down, ln_mix_g, ln_mix_b, ln_ffn_g, ln_ffn_b, ln_mix_g_2, w_in_2, diff_q_norm_g_2,
    diff_k_norm_g_2, diff_lambda_q1_2, diff_lambda_k1_2, diff_lambda_q2_2, diff_lambda_k2_2,
    diff_subln_g_2, nsa_q_norm_g_2, nsa_k_norm_g_2, cmp_pos_k_2, cmp_pos_v_2, cmp_k_w1_2,
    cmp_k_w2_2, cmp_v_w1_2, cmp_v_w2_2, w_proj_diff_2, w_proj_nsa_2, w_out_2, ln_mlp_g_2,
    w_mlp_up_2, w_mlp_down_2,
):
    x = first_block(
        x, sc_ssm_w_in, sc_conv_w, ssm_conv_w, ssm_conv_b, ssm_dt_bias, ssm_a_log, ssm_d,
        ssm_norm_g, sc_ssm_w_out, fox_w_in, fox_b_f, fox_w_out, ffn_w_up, ffn_conv_w,
        ffn_conv_b, ffn_w_down, ln_mix_g, ln_mix_b, ln_ffn_g, ln_ffn_b,
    )
    return second_block(
        x, ln_mix_g_2, w_in_2, diff_q_norm_g_2, diff_k_norm_g_2, diff_lambda_q1_2,
        diff_lambda_k1_2, diff_lambda_q2_2, diff_lambda_k2_2, diff_subln_g_2, nsa_q_norm_g_2,
        nsa_k_norm_g_2, cmp_pos_k_2, cmp_pos_v_2, cmp_k_w1_2, cmp_k_w2_2, cmp_v_w1_2,
        cmp_v_w2_2, w_proj_diff_2, w_proj_nsa_2, w_out_2, ln_mlp_g_2, w_mlp_up_2, w_mlp_down_2,
    )


_drawn_inputs = setup_inputs


def setup_inputs(seed=0):
    import zlib

    import numpy as np

    out = dict(_drawn_inputs(seed))
    spreads = {}
    factors = {'ssm_conv_b': 5.913,
     'ssm_d': 2.97,
     'ssm_norm_g': 8.0,
     'ffn_conv_b': 8.0,
     'ln_mix_g_2': 3.545,
     'diff_q_norm_g_2': 6.493,
     'diff_k_norm_g_2': 6.451,
     'diff_lambda_q1_2': 7.604,
     'diff_lambda_k1_2': 6.443,
     'diff_lambda_q2_2': 3.028,
     'diff_subln_g_2': 7.355,
     'nsa_q_norm_g_2': 8.0,
     'nsa_k_norm_g_2': 8.0,
     'cmp_pos_k_2': 8.0,
     'cmp_pos_v_2': 3.751,
     'ln_mlp_g_2': 3.297}
    for name, (base, spread) in spreads.items():
        noise = np.random.default_rng([zlib.crc32(name.encode()), seed]).standard_normal(out[name].shape)
        drawn = base * np.exp(spread * noise) if base else spread * noise
        out[name] = __import__('jax').numpy.asarray(drawn.astype(out[name].dtype))
    for name, factor in factors.items():
        out[name] = (out[name] * factor).astype(out[name].dtype)
    return out
```

```python
import math
from collections import namedtuple
from contextlib import ExitStack

import numpy as np
import concourse.bass as bass
from concourse import mybir

F32, F32R, BF16 = mybir.dt.float32, mybir.dt.float32r, mybir.dt.bfloat16
ALU = mybir.AluOpType
ACT = mybir.ActivationFunctionType
AX = mybir.AxisListType.X

P = 128
SEQ, DM = 512, 1024
NC_ = SEQ // P
KT = DM // P
DEPTH = 2
ALPHA = (2 * DEPTH) ** 0.25
LN_EPS, RMS_EPS = 1e-5, 1e-6
HEADS, HD = 16, 64
SCALE = HD ** -0.5
STATE, GROUPS = 128, 2
DFF = 2816
FT = DFF // P
DFF2 = 4096
FT2 = DFF2 // P
CMP_BLOCK, CMP_STRIDE, CMP_HIDDEN = 32, 16, 256
NCMP = (SEQ - CMP_BLOCK) // CMP_STRIDE + 1
NSA_G = 4
HPG = HEADS // NSA_G
MASKED = -1e30
LAMBDA_INIT = 0.8 - 0.6 * math.exp(0.0)
ds = bass.ds


def build(nc, A, out):
    ctx = ExitStack()
    base = (nc.sbuf_base + 63) // 64 * 64
    cursor = [base]

    def place(name, shape, dt=F32, at=None):
        size = int(np.prod(shape[1:])) * (2 if dt == BF16 else 4)
        if at is None:
            at = cursor[0]
            cursor[0] += (size + 31) // 32 * 32
        return nc.alloc_sbuf_tensor_at(name, shape, dt, offset=at)

    def sem(name):
        return ctx.enter_context(nc.semaphore(name))

    def sems(prefix, names):
        return namedtuple(prefix, names)(*[sem(f"{prefix}_{n}") for n in names.split()])

    def shared(prefix, names):
        return (namedtuple(prefix, names + " at"), namedtuple(prefix + "_at", names),
                {n: sem(f"{prefix}_{n}") for n in names.split()}, {n: 0 for n in names.split()})

    def turn(sh_, **counts):
        view, view_at, the_sems, so_far = sh_
        s = view(**the_sems, at=view_at(**so_far))
        for name, n in counts.items():
            so_far[name] += n
        return s

    RAW = place("RAW", [P, 2, 1024])
    WH = place("WH", [P, 2, 1024], F32R)
    WL = place("WL", [P, 2, 1024], F32R)
    X = place("X", [P, KT, SEQ])
    XH = place("XH", [P, KT, SEQ], F32R)
    XL = place("XL", [P, KT, SEQ], F32R)
    IDF = place("IDF", [P, P])
    ONES = place("ONES", [P, P])
    IDB = place("IDB", [P, P], BF16)
    MROW = place("MROW", [P, P], BF16)
    MCOL = place("MCOL", [P, P], BF16)
    PCOL = place("PCOL", [P, 608])
    BCP = place("BCP", [P, 768])
    narrow1 = cursor[0]
    SW = [(place("SWH1", [P, KT, 32], F32R), place("SWL1", [P, KT, 32], F32R)),
          (place("SWH2", [P, KT, 48], F32R), place("SWL2", [P, KT, 48], F32R))]
    TINY = place("TINY", [P, 512])
    EPS = place("EPS", [P, 2])
    NM = place("NM", [P, 16])
    RS = place("RS", [P, 16])
    RW = place("RW", [P, 16])
    LAM = place("LAM", [P, 8])
    CW2 = [place("CW2K", [P, 2, HD], at=narrow1), place("CW2V", [P, 2, HD], at=narrow1 + 512)]
    CPOS = place("CPOS", [P, 2, 16], at=narrow1 + 1024)
    TABK = place("TABK", [P, 2, HD], at=narrow1 + 1152)
    GT = place("GT", [P, NC_, 48])
    kcf_at = cursor[0]
    KCF = place("KCF", [P, NSA_G, 32])
    CPROW = place("CPROW", [32, P], at=kcf_at)
    arena = cursor[0]

    def a_(name, kb, shape, dt=F32):
        size = int(np.prod(shape[1:])) * (2 if dt == BF16 else 4)
        assert arena + kb * 1024 + size <= nc.sbuf_usable_end, (name, (nc.sbuf_usable_end - arena) / 1024)
        return place(name, shape, dt, at=arena + int(kb * 1024))

    PS = ctx.enter_context(nc.psum_tensor("PS", [P, 8, 512], F32))

    C_SC, C_SSM, C_SSMB, C_NG, C_MG2, C_ML2, C_SUB = 0, 24, 72, 84, 92, 100, 108
    C_LMG, C_LMB, C_LFG, C_LFB = 128, 144, 160, 176
    C_FW, C_FB = 256, 520
    B_DTB, B_ALOG, B_D, B_BF = 0, 16, 32, 48
    B_GAIN = {"dq": 64, "dk": 128, "nq": 192, "kc": 256, "ks": 320, "kw": 384}
    B_LAM = 448

    raw_loaded = [sem("raw_loaded0"), sem("raw_loaded1")]
    hi_ready, lo_ready, unit_done = sem("hi_ready"), sem("lo_ready"), sem("unit_done")

    def hi(act, b, U, i, u):
        slot = u % 2
        act.wait_ge(raw_loaded[slot], 16 * ((b + u) // 2 + 2) + 8 * U * i)
        act.wait_ge(unit_done, b + u + 1 + U * i)
        act.activation(WH[:, slot, :], RAW[:, slot, :], ACT.Copy).then_inc(hi_ready, 1)

    def lo(dve, b, U, i, u):
        slot = u % 2
        dve.wait_ge(hi_ready, b + u + 3 + U * i)
        dve.tensor_tensor(WL[:, slot, :], RAW[:, slot, :], WH[:, slot, :], ALU.subtract).then_inc(lo_ready, 1)

    def mm3(pe, o, wh, wl, ah, al, first, last, rhs_is_weight=False):
        if rhs_is_weight:
            pe.matmul(o, ah, wh, start=first, stop=False)
            pe.matmul(o, al, wh, start=False, stop=False)
            return pe.matmul(o, ah, wl, start=False, stop=last)
        pe.matmul(o, wh, ah, start=first, stop=False)
        pe.matmul(o, wh, al, start=False, stop=False)
        return pe.matmul(o, wl, ah, start=False, stop=last)

    def unit_fm(pe, b, U, i, u, o, ah, al):
        slot = u % 2
        pe.wait_ge(lo_ready, b + u + 1 + U * i)
        for k in range(KT):
            last = mm3(pe, o, WH[:, slot, k * P:(k + 1) * P], WL[:, slot, k * P:(k + 1) * P],
                       ah[:, k, :], al[:, k, :], k == 0, k == KT - 1)
        last.then_inc(unit_done, 1)

    def unit_tm(pe, b, U, i, u, banks, k0, before=None):
        slot = u % 2
        pe.wait_ge(lo_ready, b + u + 1 + U * i)
        for k in range(2):
            w = slice(k * 512, (k + 1) * 512)
            for c in range(NC_):
                if k0 + k == 0 and before is not None:
                    before(c)
                last = mm3(pe, banks(c), WH[:, slot, w], WL[:, slot, w],
                           XH[:, k0 + k, c * P:(c + 1) * P], XL[:, k0 + k, c * P:(c + 1) * P],
                           k0 + k == 0, k0 + k == KT - 1, rhs_is_weight=True)
        last.then_inc(unit_done, 1)

    def flat(ap):
        return ap.rearrange("p a b -> p (a b)")

    def rows(w):
        return w.rearrange("(k p) c -> p k c", p=P)

    def fm_src(w, col):
        return lambda i, u: rows(w)[:, :, ds(col(i, u), P)]

    w0 = A["sc_ssm_w_in"][0]
    wf = A["fox_w_in"][0]
    w2 = A["w_in_2"][0]

    def kmajor_src(w, tile0=0):
        def src(i, u):
            return rows(w)[:, tile0:tile0 + w.shape[0] // P, :][:, ds(2 * i, 2), u * 512:(u + 1) * 512] if tile0 == 0 \
                else rows(w)[:, tile0:, :][:, ds(2 * i, 2), u * 512:(u + 1) * 512]
        return src

    def tm_src(w, col0):
        def src(i, u):
            return rows(w)[:, 2 * u:2 * u + 2, ds(col0 + 512 * i, 512)]
        return src

    def ffn_src(l):
        return fm_src(A["ffn_w_up"][l], lambda i, u: 256 * i + (u // 2) * P + (u % 2) * DFF)

    def merge_src(i, u):
        if u < 2:
            return rows(A[("w_proj_diff_2", "w_proj_nsa_2")[u]][0])[:, :, ds(P * i, P)]
        return rows(w2)[:, :, ds(5680 + (u - 2) * DM + P * i, P)]

    STREAM = [
        ("gate", 6, 4, fm_src(w0, lambda i, u: (0, DM, 2 * DM)[u % 3] + 256 * i + (u // 3) * P)),
        ("xbc", 2, 6, fm_src(w0, lambda i, u: 4 * DM + 256 * i + u * P)),
        ("z", 4, 2, tm_src(w0, 3 * DM)),
        ("out0", 2, 8, kmajor_src(A["sc_ssm_w_out"][0])),
        ("up0", 4, FT // 2, ffn_src(0)),
        ("down0", 2, FT // 2, kmajor_src(A["ffn_w_down"][0])),
        ("foxqk", 2, 8, fm_src(wf, lambda i, u: 256 * i + u * P)),
        ("foxv", 4, 2, tm_src(wf, 2 * DM)),
        ("foxout", 2, 4, kmajor_src(A["fox_w_out"][0])),
        ("up1", 4, FT // 2, ffn_src(1)),
        ("down1", 2, FT // 2, kmajor_src(A["ffn_w_down"][1])),
        ("dq", 4, 2, tm_src(w2, 0)),
        ("dk", 4, 2, tm_src(w2, DM)),
        ("dv", 4, 2, tm_src(w2, 2 * DM)),
        ("nq", 4, 2, tm_src(w2, 3 * DM)),
        ("nkv", 4, 3, tm_src(w2, 4 * DM)),
        ("merge", 4, 8, merge_src),
        ("out2", 2, 4, kmajor_src(A["w_out_2"][0])),
        ("mupa", 2, FT2 // 4, fm_src(A["w_mlp_up_2"][0], lambda i, u: 256 * i + u * P)),
        ("mdna", 2, FT2 // 4, kmajor_src(A["w_mlp_down_2"][0])),
        ("mupb", 2, FT2 // 4, fm_src(A["w_mlp_up_2"][0], lambda i, u: DFF2 // 2 + 256 * i + u * P)),
        ("mdnb", 2, FT2 // 4, kmajor_src(A["w_mlp_down_2"][0], FT2 // 2)),
    ]
    first, total = {}, 0
    for name, U, bodies, _ in STREAM:
        first[name] = total
        total += U * bodies
    size = {name: (U, bodies) for name, U, bodies, _ in STREAM}
    final = STREAM[-1][0]

    def ring_step(fn, e, name, i, u):
        U, bodies = size[name]
        if name == final and isinstance(i, int) and U * i + u + 2 >= U * bodies:
            return
        fn(e, first[name], U, i, u)

    def loop(e, name, body, peel=0, peel_last=False):
        U, n = size[name]
        cut = n - 1 if (name == final or peel_last) else n
        for i in range(peel):
            body(i)
        if cut > peel:
            with e.Fori(peel, cut) as i:
                body(i)
        if cut < n and cut >= peel:
            body(n - 1)

    stage_end = sem("stage_end")
    passed = {}

    def barrier(e, key):
        passed[key] = passed.get(key, 0) + 1
        e.drain().then_inc(stage_end, 1)
        e.wait_ge(stage_end, 4 * passed[key])

    XT = a_("XT", 0, [P, NC_, DM])
    PROW = a_("PROW", 16, [P, 5, P])
    SWR = a_("SWR", 20, [P, KT, 80])
    su = sems("su", "x par bc small ident tr ev split zero")
    PARAM_ROWS = [
        (0, C_SC, A["sc_conv_w"].rearrange("a t (n p) -> (a t n) p", p=P), 24),
        (0, C_SSM, A["ssm_conv_w"].rearrange("a t (n p) -> (a t n) p", p=P), 48),
        (0, C_SSMB, A["ssm_conv_b"].rearrange("a (n p) -> (a n) p", p=P), 12),
        (0, C_NG, A["ssm_norm_g"].rearrange("a (n p) -> (a n) p", p=P), 8),
        (0, C_MG2, A["ln_mix_g_2"].rearrange("a (n p) -> (a n) p", p=P), 8),
        (0, C_ML2, A["ln_mlp_g_2"].rearrange("a (n p) -> (a n) p", p=P), 8),
        (0, C_SUB, A["diff_subln_g_2"], 1),
        (1, 0, A["ln_mix_g"].rearrange("a (n p) -> (a n) p", p=P), 16),
        (1, 16, A["ln_mix_b"].rearrange("a (n p) -> (a n) p", p=P), 16),
        (1, 32, A["ln_ffn_g"].rearrange("a (n p) -> (a n) p", p=P), 16),
        (1, 48, A["ln_ffn_b"].rearrange("a (n p) -> (a n) p", p=P), 16),
    ]
    fw = A["ffn_conv_w"].rearrange("a t (n p) -> (a t n) p", p=P)
    PARAM_ROWS += [(2, 0, fw[0:128, :], 128), (3, 0, fw[128:256, :], 128), (4, 0, fw[256:264, :], 8),
                   (4, 8, A["ffn_conv_b"].rearrange("a (n p) -> (a n) p", p=P), 88)]
    ROWS_OF = [109, 64, 128, 128, 96]
    COL_OF = [0, 128, 256, 384, 512]
    nk = A["nsa_k_norm_g_2"][0]
    BCAST = [(B_DTB, A["ssm_dt_bias"], 16), (B_ALOG, A["ssm_a_log"], 16), (B_D, A["ssm_d"], 16),
             (B_BF, A["fox_b_f"], 16), (B_GAIN["dq"], A["diff_q_norm_g_2"], HD),
             (B_GAIN["dk"], A["diff_k_norm_g_2"], HD), (B_GAIN["nq"], A["nsa_q_norm_g_2"], HD),
             (B_GAIN["kc"], nk[0:1, :], HD), (B_GAIN["ks"], nk[1:2, :], HD), (B_GAIN["kw"], nk[2:3, :], HD),
             (B_LAM, A["diff_lambda_q1_2"], HD), (B_LAM + 64, A["diff_lambda_k1_2"], HD),
             (B_LAM + 128, A["diff_lambda_q2_2"], HD), (B_LAM + 192, A["diff_lambda_k2_2"], HD)]

    def setup_dma(act):
        act.dma_start(XT[:, :, :], A["x"][0].rearrange("(c p) f -> p c f", p=P)).then_inc(su.x, 16)
        for g, r, src, n in PARAM_ROWS:
            act.dma_start(PROW[r:r + n, g, :], src).then_inc(su.par, 16)
        for c, src, n in BCAST:
            act.dma_start(BCP[:, c:c + n], src[0, :].partition_broadcast(P)).then_inc(su.bc, 16)
        act.dma_start(SWR[:, :, 0:16], rows(w0)[:, :, 5632:5648]).then_inc(su.small, 16)
        act.dma_start(SWR[:, :, 16:32], rows(wf)[:, :, 3072:3088]).then_inc(su.small, 16)
        act.dma_start(SWR[:, :, 32:80], rows(w2)[:, :, 5632:5680]).then_inc(su.small, 16)

    def setup_pool(pool):
        pool.memset(IDF[:, :], 0.0)
        pool.memset(ONES[:, :], 1.0)
        pool.memset(IDB[:, :], 0.0)
        pool.memset(MROW[:, :], 0.0)
        pool.memset(MCOL[:, :], 0.0)
        pool.memset(EPS[:, 0:1], LN_EPS)
        pool.memset(EPS[:, 1:2], RMS_EPS)
        pool.drain().then_inc(su.zero, 1)
        pool.wait_ge(su.zero, 1)
        for m in (IDF, IDB):
            pool.affine_select(out=m[:, :], in_=m[:, :], compare_op=ALU.not_equal, fill=1.0,
                               base=0, pattern=[[-1, P]], channel_multiplier=1)
        pool.affine_select(out=MROW[:, :], in_=MROW[:, :], compare_op=ALU.is_ge, fill=MASKED,
                           base=0, pattern=[[-1, P]], channel_multiplier=1)
        pool.affine_select(out=MCOL[:, :], in_=MCOL[:, :], compare_op=ALU.is_ge, fill=MASKED,
                           base=0, pattern=[[1, P]], channel_multiplier=-1)
        pool.drain().then_inc(su.ident, 1)

    def setup_pe(pe):
        pe.wait_ge(su.ident, 1)
        pe.wait_ge(su.par, 16 * len(PARAM_ROWS))
        for g in range(5):
            last = pe.transpose(PS[:, g // 4, (g % 4) * P:(g % 4) * P + ROWS_OF[g]], PROW[0:ROWS_OF[g], g, :],
                                IDF[0:ROWS_OF[g], 0:ROWS_OF[g]])
        last.then_inc(su.tr, 1)
        pe.wait_ge(su.x, 16)
        for f in range(KT):
            if f >= 4:
                pe.wait_ge(su.ev, f - 3)
            for c in range(NC_):
                last = pe.transpose(PS[:, 2 + f % 4, c * P:(c + 1) * P], XT[:, c, f * P:(f + 1) * P], IDF[:, :])
            last.then_inc(su.tr, 1)

    def setup_act(act):
        for u in range(2):
            act.wait_ge(raw_loaded[u], 16)
            act.activation(WH[:, u, :], RAW[:, u, :], ACT.Copy).then_inc(hi_ready, 1)
        act.wait_ge(su.small, 48)
        act.activation(SW[0][0][:, :, :], SWR[:, :, 0:32], ACT.Copy)
        act.activation(SW[1][0][:, :, :], SWR[:, :, 32:80], ACT.Copy)
        act.drain().then_inc(su.split, 1)
        for f in range(KT):
            act.wait_ge(su.ev, f + 1)
            act.activation(XH[:, f, :], X[:, f, :], ACT.Copy).then_inc(su.split, 1)

    def setup_dve(dve):
        for u in range(2):
            dve.wait_ge(hi_ready, u + 1)
            dve.tensor_tensor(WL[:, u, :], RAW[:, u, :], WH[:, u, :], ALU.subtract).then_inc(lo_ready, 1)
        dve.wait_ge(su.tr, 1)
        for g in range(5):
            dve.tensor_copy(PCOL[:, COL_OF[g]:COL_OF[g] + ROWS_OF[g]],
                            PS[:, g // 4, (g % 4) * P:(g % 4) * P + ROWS_OF[g]])
        dve.wait_ge(su.split, 1)
        dve.tensor_tensor(SW[0][1][:, :, :], SWR[:, :, 0:32], SW[0][0][:, :, :], ALU.subtract)
        dve.tensor_tensor(SW[1][1][:, :, :], SWR[:, :, 32:80], SW[1][0][:, :, :], ALU.subtract)
        for f in range(KT):
            dve.wait_ge(su.tr, f + 2)
            dve.tensor_copy(X[:, f, :], PS[:, 2 + f % 4, :]).then_inc(su.ev, 1)
        for f in range(KT):
            dve.wait_ge(su.split, f + 2)
            dve.tensor_tensor(XL[:, f, :], X[:, f, :], XH[:, f, :], ALU.subtract)
        dve.wait_ge(su.bc, 16 * len(BCAST))

    YH = a_("YH", 0, [P, 16, SEQ], F32R)
    YL = a_("YL", 32, [P, 16, SEQ], F32R)
    CSB = a_("CSB", 64, [P, 2, SEQ])
    CHP = a_("CHP", 68, [P, 2, SEQ + 8])
    CT = a_("CT", 73, [P, 2, SEQ])
    CY = a_("CY", 77, [P, 2, SEQ])
    ga = sems("ga", "copied y hi lo free")

    def gate_pe(pe):
        def body(i):
            for u in range(6):
                jj = u // 3
                if u % 3 == 0:
                    pe.wait_ge(ga.free, 2 * i + jj + 1)
                unit_fm(pe, first["gate"], 6, i, u, PS[:, 4 * jj + u % 3, :], XH, XL)
        loop(pe, "gate", body)

    def gate_act(act):
        def body(i):
            for u in range(6):
                ring_step(hi, act, "gate", i, u)
                jj = u // 3
                if u % 3 == 1:
                    act.wait_ge(ga.free, 2 * i + jj + 1)
                    act.activation(CSB[:, jj, :], PS[:, 4 * jj + 1, :], ACT.Copy).then_inc(ga.copied, 1)
                if u % 3 == 2:
                    act.wait_ge(ga.y, 2 * i + jj + 1)
                    act.activation(YH[:, ds(2 * i + jj, 1), :], CY[:, jj:jj + 1, :], ACT.Copy).then_inc(ga.hi, 1)
        loop(act, "gate", body)

    def gate_dve(dve):
        dve.memset(CHP[:, :, 0:2], 0.0)
        dve.drain().then_inc(ga.free, 2)

        def body(i):
            for u in range(6):
                ring_step(lo, dve, "gate", i, u)
                jj = u // 3
                if u % 3 != 2:
                    continue
                j = 2 * i + jj
                ch = CHP[:, jj, 2:2 + SEQ]
                dve.wait_ge(ga.copied, j + 1)
                dve.wait_ge(unit_done, first["gate"] + 6 * i + u + 1)
                dve.tensor_tensor(ch, CSB[:, jj, :], PS[:, 4 * jj + 2, :], ALU.mult)
                dve.drain()
                tap = [PCOL[:, ds(C_SC + 8 * t + j, 1)] for t in range(3)]
                dve.tensor_scalar(CT[:, jj, :], CHP[:, jj, 0:SEQ], tap[0], None, ALU.mult)
                dve.drain()
                for t in (1, 2):
                    dve.scalar_tensor_tensor(out=CT[:, jj, :], in0=CHP[:, jj, t:t + SEQ], scalar=tap[t],
                                             in1=CT[:, jj, :], op0=ALU.mult, op1=ALU.add)
                    dve.drain()
                dve.tensor_tensor(CY[:, jj, :], CT[:, jj, :], PS[:, 4 * jj, :], ALU.mult).then_inc(ga.y, 1)
                dve.wait_ge(ga.hi, j + 1)
                dve.tensor_tensor(YL[:, ds(j, 1), :], CY[:, jj:jj + 1, :], YH[:, ds(j, 1), :],
                                  ALU.subtract)
                dve.drain().then_inc(ga.free, 1)
        loop(dve, "gate", body)

    XSF = a_("XSF", 16, [P, 8, SEQ])
    BF = a_("BF", 80, [P, 2, SEQ])
    CF = a_("CF", 96, [P, 2, SEQ])
    XP = a_("XP", 64, [P, 2, SEQ + 8])
    XQ = a_("XQ", 69, [P, 2, SEQ])
    xb = sems("xb", "copied conv free")

    def xbc_dst(i, u):
        if isinstance(i, int):
            if i == 4:
                return BF[:, u:u + 1, :]
            if i == 5:
                return CF[:, u:u + 1, :]
        return XSF[:, ds(2 * i + u, 1), :]

    def xbc_loop(e, body):
        with e.Fori(0, 4) as i:
            body(i)
        body(4)
        body(5)

    def xbc_pe(pe):
        def body(i):
            for u in range(2):
                pe.wait_ge(xb.copied, 2 * i + u + 1)
                unit_fm(pe, first["xbc"], 2, i, u, PS[:, u, :], XH, XL)
        xbc_loop(pe, body)

    def xbc_act(act):
        act.drain().then_inc(xb.copied, 2)
        act.drain().then_inc(xb.free, 2)

        def body(i):
            for u in range(2):
                hi(act, first["xbc"], 2, i, u)
                act.wait_ge(xb.conv, 2 * i + u + 1)
                act.activation(XP[:, u, 3:3 + SEQ], PS[:, u, :], ACT.Copy).then_inc(xb.copied, 1)
                act.wait_ge(xb.conv, 2 * i + u + 3)
                act.activation(xbc_dst(i, u), XQ[:, u:u + 1, :], ACT.Silu).then_inc(xb.free, 1)
        xbc_loop(act, body)

    def xbc_dve(dve):
        dve.memset(XP[:, :, 0:3], 0.0)
        dve.drain().then_inc(xb.conv, 2)
        dve.drain()

        def body(i):
            for u in range(2):
                lo(dve, first["xbc"], 2, i, u)
                j = 2 * i + u
                dve.wait_ge(xb.copied, j + 3)
                dve.wait_ge(xb.free, j + 1)
                tap = [PCOL[:, ds(C_SSM + 12 * t + j, 1)] for t in range(4)]
                dve.tensor_scalar(XQ[:, u, :], XP[:, u, 0:SEQ], tap[0], PCOL[:, ds(C_SSMB + j, 1)],
                                  ALU.mult, ALU.add)
                dve.drain()
                for t in (1, 2, 3):
                    last = dve.scalar_tensor_tensor(out=XQ[:, u, :], in0=XP[:, u, t:t + SEQ], scalar=tap[t],
                                                    in1=XQ[:, u, :], op0=ALU.mult, op1=ALU.add)
                    if t < 3:
                        dve.drain()
                last.then_inc(xb.conv, 1)
        xbc_loop(dve, body)

    LT = a_("LT", 104, [P, 7, SEQ])

    norm_s = shared("norm", "res sum cent sq ssq std tmp hi")

    def norm_turn():
        return turn(norm_s, res=KT, sum=1, cent=KT, sq=KT, ssq=KT, std=1, tmp=KT, hi=KT)

    def ln_pe(pe, s):
        for m in range(KT):
            pe.wait_ge(s.res, s.at.res + m + 1)
            last = pe.matmul(PS[:, 0, :], ONES[:, :], X[:, m, :], start=m == 0, stop=m == KT - 1)
        last.then_inc(s.sum, 1)
        ssq_pe(pe, s)

    def ssq_pe(pe, s):
        for m in range(KT):
            pe.wait_ge(s.sq, s.at.sq + m + 1)
            pe.matmul(PS[:, 1, :], ONES[:, :], LT[:, m % 2, :], start=m == 0, stop=m == KT - 1).then_inc(s.ssq, 1)

    def square_act(act, s):
        for m in range(KT):
            act.wait_ge(s.cent, s.at.cent + m + 1)
            if m >= 2:
                act.wait_ge(s.ssq, s.at.ssq + m - 1)
            act.activation(LT[:, m % 2, :], X[:, m, :], ACT.Square).then_inc(s.sq, 1)

    def ln_act(act, s, g, b):
        square_act(act, s)
        act.wait_ge(s.ssq, s.at.ssq + KT)
        act.activation(LT[:, 3, :], PS[:, 1, :], ACT.Sqrt, bias=EPS[:, 0:1], scale=1.0 / DM).then_inc(s.std, 1)
        for m in range(KT):
            act.wait_ge(s.tmp, s.at.tmp + m + 1)
            act.activation(XH[:, m, :], LT[:, 5 + m % 2, :], ACT.Identity, bias=PCOL[:, b + m:b + m + 1],
                           scale=PCOL[:, g + m:g + m + 1]).then_inc(s.hi, 1)

    def ln_dve(dve, s, g, b):
        for m in range(KT):
            dve.scalar_tensor_tensor(out=X[:, m, :], in0=X[:, m, :], scalar=ALPHA, in1=PS[:, m, :],
                                     op0=ALU.mult, op1=ALU.add).then_inc(s.res, 1)
        dve.wait_ge(s.sum, s.at.sum + 1)
        dve.tensor_scalar(LT[:, 2, :], PS[:, 0, :], 1.0 / DM, None, ALU.mult)
        dve.drain()
        for m in range(KT):
            dve.tensor_tensor(X[:, m, :], X[:, m, :], LT[:, 2, :], ALU.subtract).then_inc(s.cent, 1)
        dve.wait_ge(s.std, s.at.std + 1)
        dve.reciprocal(LT[:, 4, :], LT[:, 3, :])
        dve.drain()
        for m in range(KT):
            if m >= 2:
                dve.wait_ge(s.hi, s.at.hi + m - 1)
            dve.tensor_tensor(LT[:, 5 + m % 2, :], X[:, m, :], LT[:, 4, :], ALU.mult).then_inc(s.tmp, 1)
            dve.drain()
            dve.tensor_scalar(X[:, m, :], LT[:, 5 + m % 2, :], PCOL[:, g + m:g + m + 1], PCOL[:, b + m:b + m + 1],
                              ALU.mult, ALU.add)
            dve.drain()
            dve.wait_ge(s.hi, s.at.hi + m + 1)
            dve.tensor_tensor(XL[:, m, :], X[:, m, :], XH[:, m, :], ALU.subtract)

    def rms_act(act, s, g):
        square_act(act, s)
        act.wait_ge(s.ssq, s.at.ssq + KT)
        act.activation(LT[:, 3, :], PS[:, 1, :], ACT.Sqrt, bias=EPS[:, 1:2], scale=1.0 / DM).then_inc(s.std, 1)
        for m in range(KT):
            act.wait_ge(s.tmp, s.at.tmp + m + 1)
            act.activation(XH[:, m, :], LT[:, 5 + m % 2, :], ACT.Copy,
                           scale=PCOL[:, g + m:g + m + 1]).then_inc(s.hi, 1)

    def rms_dve(dve, s, g, residual):
        for m in range(KT):
            if residual:
                dve.tensor_tensor(X[:, m, :], X[:, m, :], PS[:, m, :], ALU.add)
        dve.drain().then_inc(s.cent, KT)
        dve.wait_ge(s.std, s.at.std + 1)
        dve.reciprocal(LT[:, 4, :], LT[:, 3, :])
        dve.drain()
        for m in range(KT):
            if m >= 2:
                dve.wait_ge(s.hi, s.at.hi + m - 1)
            dve.tensor_tensor(LT[:, 5 + m % 2, :], X[:, m, :], LT[:, 4, :], ALU.mult).then_inc(s.tmp, 1)
            dve.drain()
            dve.wait_ge(s.hi, s.at.hi + m + 1)
            dve.scalar_tensor_tensor(out=XL[:, m, :], in0=LT[:, 5 + m % 2, :], scalar=PCOL[:, g + m:g + m + 1],
                                     in1=XH[:, m, :], op0=ALU.mult, op1=ALU.subtract)

    def kmajor_pe(pe, name, ah, al):
        U, n = size[name]

        def body(i):
            for u in range(2):
                slot = u % 2
                pe.wait_ge(lo_ready, first[name] + u + 1 + 2 * i)
                for k in range(2):
                    for m in range(4):
                        w = slice(k * 512 + m * P, k * 512 + (m + 1) * P)
                        a = (flat(ah[:, ds(2 * i + k, 1), :]), flat(al[:, ds(2 * i + k, 1), :]))
                        begin = isinstance(i, int) and i == 0 and k == 0
                        end = isinstance(i, int) and i == n - 1 and k == 1
                        last = mm3(pe, PS[:, 4 * u + m, :], WH[:, slot, w], WL[:, slot, w], *a, begin, end)
                last.then_inc(unit_done, 1)
        loop(pe, name, body, peel=1, peel_last=True)

    def split_only(fn, e, name):
        def body(i):
            for u in range(size[name][0]):
                ring_step(fn, e, name, i, u)
        loop(e, name, body)

    FH = a_("FH", 0, [P, FT, SEQ], F32R)
    FL = a_("FL", 44, [P, FT, SEQ], F32R)
    UP = a_("UP", 88, [P, 4, SEQ + 8])
    UT = a_("UT", 97, [P, 4, SEQ])
    FY = a_("FY", 105, [P, 2, SEQ])

    ffn_s = shared("ffn", "copied conv silu y hi")

    def ffn_turn():
        return turn(ffn_s, copied=4 + 2 * FT, conv=4 + 2 * FT, silu=2 + FT, y=FT, hi=2 + FT)

    def ffn_up_pe(pe, l, s):
        name = f"up{l}"

        def body(i):
            for u in range(4):
                pe.wait_ge(s.copied, s.at.copied + 4 * i + u + 1)
                unit_fm(pe, first[name], 4, i, u, PS[:, u, :], XH, XL)
        loop(pe, name, body)

    def ffn_up_act(act, l, s):
        name = f"up{l}"
        act.drain().then_inc(s.copied, 4)
        act.drain().then_inc(s.silu, 2)
        act.drain().then_inc(s.hi, 2)

        def body(i):
            for u in range(4):
                ring_step(hi, act, name, i, u)
                act.wait_ge(s.conv, s.at.conv + 4 * i + u + 1)
                act.activation(UP[:, u, 2:2 + SEQ], PS[:, u, :], ACT.Copy).then_inc(s.copied, 1)
                if u % 2:
                    jj = u // 2
                    act.wait_ge(s.conv, s.at.conv + 4 * i + u + 5)
                    act.activation(UT[:, u, :], UT[:, u, :], ACT.Silu).then_inc(s.silu, 1)
                    act.wait_ge(s.y, s.at.y + 2 * i + jj + 1)
                    act.activation(FH[:, ds(2 * i + jj, 1), :], FY[:, jj:jj + 1, :], ACT.Copy).then_inc(s.hi, 1)
        loop(act, name, body)

    def ffn_up_dve(dve, l, s):
        name = f"up{l}"
        dve.memset(UP[:, :, 0:2], 0.0)
        dve.drain().then_inc(s.conv, 4)

        def body(i):
            for u in range(4):
                ring_step(lo, dve, name, i, u)
                jj = u // 2
                j = 2 * i + jj
                col = C_FW + l * 132 + (u % 2) * FT + j
                dve.wait_ge(s.copied, s.at.copied + 4 * i + u + 5)
                tap = [PCOL[:, ds(col + 44 * t, 1)] for t in range(3)]
                bias = PCOL[:, ds(C_FB + l * 44 + (u % 2) * FT + j, 1)]
                dve.tensor_scalar(UT[:, u, :], UP[:, u, 0:SEQ], tap[0], bias, ALU.mult, ALU.add)
                dve.drain()
                dve.scalar_tensor_tensor(out=UT[:, u, :], in0=UP[:, u, 1:1 + SEQ], scalar=tap[1],
                                         in1=UT[:, u, :], op0=ALU.mult, op1=ALU.add)
                dve.drain()
                dve.scalar_tensor_tensor(out=UT[:, u, :], in0=UP[:, u, 2:2 + SEQ], scalar=tap[2],
                                         in1=UT[:, u, :], op0=ALU.mult, op1=ALU.add).then_inc(s.conv, 1)
                if u % 2:
                    dve.wait_ge(s.silu, s.at.silu + j + 3)
                    dve.tensor_tensor(FY[:, jj, :], UT[:, u - 1, :], UT[:, u, :], ALU.mult).then_inc(s.y, 1)
                    dve.wait_ge(s.hi, s.at.hi + j + 3)
                    dve.tensor_tensor(FL[:, ds(j, 1), :], FY[:, jj:jj + 1, :], FH[:, ds(j, 1), :], ALU.subtract)
                    dve.drain()
        loop(dve, name, body)


    XS = a_("XS", 64, [P, NC_, DM])
    YB = a_("YB", 80, [P, NC_, DM])
    BT = a_("BT", 100, [P, NC_, GROUPS * STATE])
    XDT = a_("XDT", 104, [P, NC_, DM])
    XDEC = a_("XDEC", 16, [P, NC_, DM])
    EM = a_("EM", 48, [P, 2, SEQ])
    CBT = a_("CBT", 52, [P, GROUPS, SEQ])
    HS = a_("HS", 56, [P, DM])
    ACST = a_("ACST", 60, [HEADS, SEQ])
    SELB = a_("SELB", 62, [HEADS, 2, P])
    Z = a_("Z", 16, [P, NC_, DM])
    t64 = [TINY[:, 64 * k:64 * (k + 1)] for k in range(8)]

    def heads4(ap):
        return ap.rearrange("p (c h) -> p c h", c=NC_)

    def small_gemm_pe(pe, bank, sw, c0, c1):
        n = c1 - c0
        for c in range(NC_):
            for k in range(KT):
                last = mm3(pe, PS[:, bank, c * n:(c + 1) * n], sw[0][:, k, c0:c1], sw[1][:, k, c0:c1],
                           XH[:, k, c * P:(c + 1) * P], XL[:, k, c * P:(c + 1) * P], k == 0, k == KT - 1,
                           rhs_is_weight=True)
        return last

    def softplus_dve_b(dve, v, e, w, r, q):
        dve.tensor_scalar(w, e, 1.0, None, ALU.add)
        dve.drain()
        dve.tensor_scalar(r, w, -1.0, None, ALU.add)
        dve.reciprocal(q, w)
        dve.drain()
        dve.tensor_tensor(r, e, r, ALU.subtract)
        dve.drain()
        dve.tensor_tensor(r, r, q, ALU.mult)
        dve.drain()
        dve.tensor_scalar(q, v, 0.0, None, ALU.max)
        dve.drain()
        dve.tensor_tensor(r, r, q, ALU.add)

    sd = sems("sd", "tr ev dt e w ln dta t1 scan t2 tot acs exps cb xdec st h yo ydone")
    V_, E_, W_, R_, Q_, LN_, DTA, DTV = t64
    DEC = a_("DEC", 63, [P, 4, 64])

    def ssd_pe(pe):
        small_gemm_pe(pe, 4, SW[0], 0, 16).then_inc(sd.dt, 1)
        pe.wait_ge(sd.dta, 1)
        for c in range(NC_):
            last = pe.transpose(PS[0:16, 5, c * P:(c + 1) * P], DTA[:, c * 16:(c + 1) * 16], IDF[:, :])
        last.then_inc(sd.t1, 1)
        pe.matmul(PS[:, 7, 0:64], ONES[:, :], DTA, start=True, stop=True).then_inc(sd.tot, 1)
        for j in range(10):
            if j >= 4:
                pe.wait_ge(sd.ev, j - 3)
            for c in range(NC_):
                src = XSF[:, j, c * P:(c + 1) * P] if j < 8 else BF[:, j - 8, c * P:(c + 1) * P]
                last = pe.transpose(PS[:, j % 4, c * P:(c + 1) * P], src, IDF[:, :])
            last.then_inc(sd.tr, 1)
        pe.wait_ge(sd.scan, 1)
        for c in range(NC_):
            last = pe.transpose(PS[:, 6, c * 16:(c + 1) * 16], ACST[0:16, c * P:(c + 1) * P], IDF[0:16, 0:16])
        last.then_inc(sd.t2, 1)
        pe.wait_ge(sd.ev, 10)
        for g in range(GROUPS):
            for c in range(NC_):
                last = pe.matmul(PS[:, g, c * P:(c + 1) * P], BF[:, g, c * P:(c + 1) * P],
                                 CF[:, g, c * P:(c + 1) * P], start=True, stop=True)
        last.then_inc(sd.cb, 1)
        pe.wait_ge(sd.xdec, 1)
        for c in range(NC_):
            if c < NC_ - 1:
                if c:
                    pe.wait_ge(sd.h, c)
                for g in range(GROUPS):
                    last = pe.matmul(PS[:, 2 + g, :], BT[:, c, g * STATE:(g + 1) * STATE],
                                     XDEC[:, c, g * 512:(g + 1) * 512], start=True, stop=True)
                last.then_inc(sd.st, 1)
            if c:
                pe.wait_ge(sd.h, c)
                if c > 1:
                    pe.wait_ge(sd.ydone, c)
                for g in range(GROUPS):
                    last = pe.matmul(PS[:, 4 + g, :], CF[:, g, c * P:(c + 1) * P],
                                     HS[:, g * 512:(g + 1) * 512], start=True, stop=True)
                last.then_inc(sd.yo, 1)

    def ssd_act(act):
        act.wait_ge(sd.e, 1)
        act.activation(E_, V_, ACT.Abs)
        act.drain()
        act.activation(E_, E_, ACT.Exp, scale=-1.0)
        act.activation(BCP[:, 752:768], BCP[:, B_ALOG:B_ALOG + 16], ACT.Exp)
        act.drain().then_inc(sd.w, 1)
        act.wait_ge(sd.ln, 1)
        act.activation(LN_, W_, ACT.Ln).then_inc(sd.ln, 1)
        act.wait_ge(sd.acs, 1)
        for k in range(3):
            last = act.activation(DEC[:, k, :], DEC[:, k, :], ACT.Exp)
        last.then_inc(sd.exps, 1)

    def ssd_dve(dve):
        dve.wait_ge(sd.dt, 1)
        dve.tensor_tensor(heads4(V_), heads4(PS[:, 4, 0:64]),
                          BCP[:, B_DTB:B_DTB + 16].unsqueeze(1).to_broadcast([P, NC_, 16]), ALU.add)
        dve.drain()
        dve.drain().then_inc(sd.e, 1)
        dve.wait_ge(sd.w, 1)
        dve.tensor_copy(BCP[:, B_ALOG:B_ALOG + 16], BCP[:, 752:768])
        softplus_dve_b(dve, V_, E_, W_, R_, Q_)
        dve.drain().then_inc(sd.ln, 1)
        dve.wait_ge(sd.ln, 2)
        dve.tensor_tensor(DTV, R_, LN_, ALU.add)
        dve.drain()
        dve.scalar_tensor_tensor(out=heads4(DTA), in0=heads4(DTV), scalar=-1.0,
                                 in1=BCP[:, B_ALOG:B_ALOG + 16].unsqueeze(1).to_broadcast([P, NC_, 16]),
                                 op0=ALU.mult, op1=ALU.mult)
        dve.drain().then_inc(sd.dta, 1)
        dve.wait_ge(sd.t1, 1)
        for c in range(NC_):
            dve.tensor_tensor_scan(ACST[0:16, c * P:(c + 1) * P], ONES[0:16, :], PS[0:16, 5, c * P:(c + 1) * P],
                                   0.0, ALU.mult, ALU.add)
        dve.drain().then_inc(sd.scan, 1)
        for j in range(10):
            dve.wait_ge(sd.tr, j + 1)
            dst = XS[:, :, j * P:(j + 1) * P] if j < 8 else BT[:, :, (j - 8) * P:(j - 7) * P]
            dve.tensor_copy(dst, PS[:, j % 4, :].rearrange("p (c t) -> p c t", c=NC_)).then_inc(sd.ev, 1)
        dve.wait_ge(sd.t2, 1)
        dve.wait_ge(sd.tot, 1)
        dve.tensor_copy(DEC[:, 2, :], PS[:, 6, 0:64])
        dve.tensor_copy(DEC[:, 1, :], PS[:, 7, 0:64])
        dve.drain()
        dve.tensor_scalar(DEC[:, 3, :], DEC[:, 2, :], -1.0, None, ALU.mult)
        dve.tensor_tensor(DEC[:, 0, :], DEC[:, 1, :], DEC[:, 2, :], ALU.subtract)
        dve.drain().then_inc(sd.acs, 1)

        def per_head(ap):
            return ap.unsqueeze(2).to_broadcast([P, HEADS, HD])

        def by_head(ap):
            return ap.rearrange("p (h d) -> p h d", h=HEADS)

        for c in range(NC_):
            dve.tensor_tensor(by_head(XDT[:, c, :]), by_head(XS[:, c, :]), per_head(DTV[:, c * 16:(c + 1) * 16]),
                              ALU.mult)
        dve.wait_ge(sd.exps, 1)
        dve.wait_ge(sd.cb, 1)
        for g in range(GROUPS):
            dve.tensor_copy(CBT[:, g, :], PS[:, g, :])
        dve.drain()
        for c in range(NC_):
            dve.tensor_tensor(by_head(XDEC[:, c, :]), by_head(XDT[:, c, :]),
                              per_head(DEC[:, 0, c * 16:(c + 1) * 16]), ALU.mult)
            dve.tensor_tensor(by_head(YB[:, c, :]), by_head(XS[:, c, :]), per_head(BCP[:, B_D:B_D + 16]), ALU.mult)
        dve.drain().then_inc(sd.xdec, 1)
        for c in range(NC_):
            if c:
                dve.wait_ge(sd.yo, c)
                for g in range(GROUPS):
                    half = XS[:, c, g * 512:(g + 1) * 512]
                    dve.tensor_tensor(half.rearrange("p (h d) -> p h d", h=8),
                                      PS[:, 4 + g, :].rearrange("p (h d) -> p h d", h=8),
                                      DEC[:, 2, c * 16 + 8 * g:c * 16 + 8 * g + 8].unsqueeze(2)
                                      .to_broadcast([P, 8, HD]), ALU.mult)
                dve.drain().then_inc(sd.ydone, 2 if c == 1 else 1)
                dve.tensor_tensor(YB[:, c, :], YB[:, c, :], XS[:, c, :], ALU.add)
            if c < NC_ - 1:
                dve.wait_ge(sd.st, c + 1)
                new = PS[:, 2:4, :].rearrange("p a b -> p (a b)")
                if c == 0:
                    dve.tensor_copy(HS[:, :], new)
                else:
                    dve.tensor_tensor(by_head(HS[:, :]), by_head(HS[:, :]),
                                      per_head(DEC[:, 1, c * 16:(c + 1) * 16]), ALU.mult)
                    dve.drain()
                    dve.tensor_tensor(HS[:, :], HS[:, :], new, ALU.add)
                dve.drain().then_inc(sd.h, 1)

    def heads_loop(e, body):
        for g in range(GROUPS):
            with e.Fori(0, 4) as i:
                body(g, i)

    sh = sems("sh", "sel bc e m y yd")

    def ssdh_pe(pe):
        def body(g, i):
            n = 8 * g + 2 * i
            for hh in range(2):
                pe.wait_ge(sh.sel, n + hh + 1)
                pe.wait_ge(sh.e, n + hh + 1)
                pe.matmul(PS[:, hh, :], SELB[:, hh, :], ACST[:, :], start=True, stop=False)
                for c in range(NC_):
                    last = pe.matmul(PS[:, hh, c * P:(c + 1) * P], IDB[:, :], MCOL[:, :], start=False,
                                     stop=c == NC_ - 1)
                last.then_inc(sh.bc, 1)
            for hh in range(2):
                pe.wait_ge(sh.m, n + hh + 1)
                pe.wait_ge(sh.yd, n + hh + 1)
                for c in range(NC_):
                    last = pe.matmul(PS[:, 2 + hh, c * HD:(c + 1) * HD], EM[:, hh, c * P:(c + 1) * P],
                                     XDT[:, c, ds((n + hh) * HD, HD)], start=True, stop=True)
                last.then_inc(sh.y, 1)
        heads_loop(pe, body)

    def ssdh_act(act):
        act.drain().then_inc(sh.e, 2)

        def body(g, i):
            n = 8 * g + 2 * i
            for hh in range(2):
                act.wait_ge(sh.bc, n + hh + 1)
                act.wait_ge(sh.yd, n + hh + 1)
                for c in range(NC_):
                    last = act.activation(EM[:, hh, c * P:(c + 1) * P], PS[:, hh, c * P:(c + 1) * P], ACT.Exp,
                                          bias=DEC[:, 3, ds(c * 16 + n + hh, 1)])
                last.then_inc(sh.e, 1)
        heads_loop(act, body)

    def ssdh_dve(dve):
        dve.drain().then_inc(sh.yd, 2)

        def body(g, i):
            n = 8 * g + 2 * i
            for hh in range(2):
                dve.tensor_copy(SELB[:, hh, :], IDF[0:16, ds(n + hh, 1)].to_broadcast([HEADS, P])).then_inc(sh.sel, 1)
            for hh in range(2):
                dve.wait_ge(sh.e, n + hh + 3)
                dve.tensor_tensor(EM[:, hh, :], EM[:, hh, :], CBT[:, g, :], ALU.mult).then_inc(sh.m, 1)
            for hh in range(2):
                dve.wait_ge(sh.y, n + hh + 1)
                y = YB[:, :, ds((n + hh) * HD, HD)]
                dve.tensor_tensor(y, y, PS[:, 2 + hh, 0:256].rearrange("p (c d) -> p c d", c=NC_),
                                  ALU.add)
                dve.drain().then_inc(sh.yd, 1)
        heads_loop(dve, body)

    def tm_pe(pe, name, s, groups_before=0):
        def body(i):
            def free(c):
                pe.wait_ge(s.left, s.at.left + 4 * (i + groups_before) + c + 1)
            for u in range(4):
                unit_tm(pe, first[name], 4, i, u, lambda c: PS[:, c, :], 2 * u, free)
        loop(pe, name, body)

    def tm_act(act, name, s, dst, func=ACT.Copy, credit=True):
        if credit:
            act.drain().then_inc(s.left, 4)

        def body(i):
            for u in range(4):
                ring_step(hi, act, name, i, u)
            act.wait_ge(unit_done, first[name] + 4 * i + 4)
            for c in range(NC_):
                act.activation(dst(i, c), PS[:, c, :], func).then_inc(s.left, 1)
        loop(act, name, body)

    left_s = shared("left", "left")
    zs = turn(left_s, left=4 + 8)
    gn = sems("gn", "u ss std n tr hi lo")

    def gnorm_pe(pe):
        for f in range(KT):
            pe.wait_ge(gn.n, f // 4 + 1)
            if f >= 4:
                pe.wait_ge(gn.lo, f - 3)
            for c in range(NC_):
                last = pe.transpose(PS[:, f % 4, c * P:(c + 1) * P], YB[:, c, f * P:(f + 1) * P], IDF[:, :])
            last.then_inc(gn.tr, 1)

    def gnorm_act(act):
        for g in range(GROUPS):
            for c in range(NC_):
                act.wait_ge(gn.u, g * NC_ + c + 1)
                act.activation(XS[:, c, g * 512:(g + 1) * 512], YB[:, c, g * 512:(g + 1) * 512], ACT.Square,
                               accum_out=TINY[:, g * NC_ + c:g * NC_ + c + 1])
        act.drain()
        act.activation(TINY[:, 8:16], TINY[:, 0:8], ACT.Sqrt, bias=EPS[:, 0:1], scale=1.0 / 512).then_inc(gn.std, 1)
        for f in range(KT):
            act.wait_ge(gn.tr, f + 1)
            act.activation(YH[:, 8 + f, :], PS[:, f % 4, :], ACT.Copy,
                           scale=PCOL[:, C_NG + f:C_NG + f + 1]).then_inc(gn.hi, 1)

    def gnorm_dve(dve):
        for g in range(GROUPS):
            for c in range(NC_):
                seg = YB[:, c, g * 512:(g + 1) * 512]
                dve.tensor_tensor(seg, seg, Z[:, c, g * 512:(g + 1) * 512], ALU.mult).then_inc(gn.u, 1)
        dve.wait_ge(gn.std, 1)
        dve.reciprocal(TINY[:, 16:24], TINY[:, 8:16])
        dve.drain()
        for g in range(GROUPS):
            for c in range(NC_):
                seg = YB[:, c, g * 512:(g + 1) * 512]
                dve.tensor_scalar(seg, seg, TINY[:, 16 + g * NC_ + c:17 + g * NC_ + c], None, ALU.mult)
            dve.drain().then_inc(gn.n, 1)
        for f in range(KT):
            dve.wait_ge(gn.hi, f + 1)
            dve.scalar_tensor_tensor(out=YL[:, 8 + f, :], in0=PS[:, f % 4, :], scalar=PCOL[:, C_NG + f:C_NG + f + 1],
                                     in1=YH[:, 8 + f, :], op0=ALU.mult, op1=ALU.subtract).then_inc(gn.lo, 1)

    def fm_pe(pe, name, s):
        def body(i):
            for u in range(2):
                pe.wait_ge(s.left, s.at.left + 2 * i + u + 1)
                unit_fm(pe, first[name], 2, i, u, PS[:, u, :], XH, XL)
        loop(pe, name, body)

    attn_s = shared("attn", "qz sc mx ex cb tr pt pv ov")

    def attn_turn(steps, cb=0):
        return turn(attn_s, qz=8, sc=steps, mx=steps, ex=steps + 2, cb=cb, tr=steps + 2, pt=steps + 2,
                    pv=steps + 2, ov=steps + 2)

    def scores_pe(pe, bank, q, k, qb):
        n = (qb + 1) * P
        pe.matmul(PS[:, bank, 0:n], q, k(n), start=True, stop=False)
        return pe.matmul(PS[:, bank, qb * P:n], IDB[:, :], MROW[:, :], start=False, stop=True)

    def attn_pe_body(pe, s, idx, n, qb_of, scores, value, ready, width, nsub=1):
        B = idx * n
        for t in range(n + 2):
            if t < n:
                pe.wait_ge(s.ex, s.at.ex + B + t + 1)
                scores(t).then_inc(s.sc, 1)
            if 1 <= t <= n:
                k = t - 1
                pe.wait_ge(ready[0], ready[1] + B + k + 3)
                pe.wait_ge(s.pt, s.at.pt + B + k + 1)
                for b in range(qb_of(k) + 1):
                    last = pe.transpose(PS[:, 4 + k % 2, b * P:(b + 1) * P],
                                        PB[:, nsub * (k % 2), b * P:(b + 1) * P], IDF[:, :])
                last.then_inc(s.tr, 1)
            if t >= 2:
                k = t - 2
                pe.wait_ge(s.pt, s.at.pt + B + k + 3)
                pe.wait_ge(s.ov, s.at.ov + B + k + 1)
                for b in range(qb_of(k) + 1):
                    last = pe.matmul(PS[:, 6 + k % 2, 0:width], PT[:, k % 2, b * P:(b + 1) * P], value(k, b),
                                     start=b == 0, stop=b == qb_of(k))
                last.then_inc(s.pv, 1)

    def attn_act_body(act, s, idx, n, qb_of, exps):
        B = idx * n
        for t in range(n + 1):
            if t < n:
                act.wait_ge(s.mx, s.at.mx + B + t + 1)
                act.wait_ge(s.tr, s.at.tr + B + t + 1)
                exps(t).then_inc(s.ex, 1)
            if t >= 1:
                k = t - 1
                act.wait_ge(s.tr, s.at.tr + B + k + 3)
                act.wait_ge(s.pv, s.at.pv + B + k + 1)
                w = (qb_of(k) + 1) * P
                act.activation(PT[:, k % 2, 0:w], PS[:, 4 + k % 2, 0:w], ACT.Copy).then_inc(s.pt, 1)

    QK = a_("QK", 0, [P, 16, SEQ])
    VT = a_("VT", 32, [P, NC_, DM])
    OB = a_("OB", 48, [P, NC_, DM])
    QZ = a_("QZ", 64, [P, 2, SEQ])
    NBS = a_("NBS", 68, [P, 2, SEQ])
    PB = a_("PB", 72, [P, 4, SEQ])
    PT = a_("PT", 80, [P, 2, SEQ])
    NCUM = a_("NCUM", 84, [HEADS, SEQ])
    SELF = a_("SELF", 86, [HEADS, 2, P])
    fq = turn(left_s, left=2 + 16)
    fv = turn(left_s, left=4 + 8)
    fg = sems("fg", "f w ln sp t1")
    fa = attn_turn(64)
    fnb = sems("fnb", "sel bc nb")

    def foxqk_act(act):
        act.drain().then_inc(fq.left, 2)

        def part(lo_, hi_, scale):
            def body(i):
                for u in range(2):
                    ring_step(hi, act, "foxqk", i, u)
                    act.wait_ge(unit_done, first["foxqk"] + 2 * i + u + 1)
                    act.activation(QK[:, ds(2 * i + u, 1), :], PS[:, u:u + 1, :], ACT.Copy,
                                   scale=scale).then_inc(fq.left, 1)
            return body
        with act.Fori(0, 4) as i:
            part(0, 4, SCALE)(i)
        with act.Fori(4, 8) as i:
            part(4, 8, 1.0)(i)

    def forget_pe(pe):
        small_gemm_pe(pe, 4, SW[0], 16, 32).then_inc(fg.f, 1)
        pe.wait_ge(fg.sp, 1)
        for c in range(NC_):
            last = pe.transpose(PS[0:16, 5, c * P:(c + 1) * P], DTA[:, c * 16:(c + 1) * 16], IDF[:, :])
        last.then_inc(fg.t1, 1)

    def forget_act(act):
        act.wait_ge(fg.w, 1)
        act.activation(E_, V_, ACT.Abs)
        act.drain()
        act.activation(E_, E_, ACT.Exp, scale=-1.0).then_inc(fg.ln, 1)
        act.wait_ge(fg.w, 2)
        act.activation(LN_, W_, ACT.Ln).then_inc(fg.ln, 1)

    def forget_dve(dve):
        dve.wait_ge(fg.f, 1)
        dve.tensor_tensor(heads4(V_), heads4(PS[:, 4, 0:64]),
                          BCP[:, B_BF:B_BF + 16].unsqueeze(1).to_broadcast([P, NC_, 16]), ALU.add)
        dve.drain()
        dve.tensor_scalar(V_, V_, -1.0, None, ALU.mult)
        dve.drain().then_inc(fg.w, 1)
        dve.wait_ge(fg.ln, 1)
        softplus_dve_b(dve, V_, E_, W_, R_, Q_)
        dve.drain().then_inc(fg.w, 1)
        dve.wait_ge(fg.ln, 2)
        dve.tensor_tensor(DTA, R_, LN_, ALU.add).then_inc(fg.sp, 1)
        dve.wait_ge(fg.t1, 1)
        dve.memset(NBS[0:16, 0, :], 1.0)
        dve.drain()
        dve.tensor_tensor_scan(NCUM[:, :], NBS[0:16, 0, :], PS[0:16, 5, :], 0.0, ALU.mult, ALU.add)

    def zero_qz(pool):
        pool.memset(QZ[64:128, 0, :], 0.0)
        pool.memset(QZ[0:64, 1, :], 0.0)

    def fox_pe(pe):
        pe.drain().then_inc(fa.tr, 2)
        pe.drain().then_inc(fa.pv, 2)
        with pe.Fori(0, 8) as i:
            for hh in range(2):
                pe.wait_ge(fnb.sel, 2 * i + hh + 1)
                pe.matmul(PS[:, 2 + hh, :], SELF[:, hh, :], NCUM[:, :], start=True, stop=True).then_inc(fnb.bc, 1)
            pe.wait_ge(fa.qz, fa.at.qz + i + 1)
            attn_pe_body(
                pe, fa, i, 8, lambda t: t % 4,
                lambda t: scores_pe(pe, t % 2, QZ[:, t // 4, (t % 4) * P:(t % 4 + 1) * P],
                                    lambda n: flat(QK[:, ds(8 + i, 1), 0:n]), t % 4),
                lambda k, b: VT[:, b, ds(i * P + (k // 4) * HD, HD)], (fa.ex, fa.at.ex), HD)

    def copy_queries(act, src, i, s):
        for hh in range(2):
            half = slice(hh * HD, (hh + 1) * HD)
            last = act.activation(QZ[half, hh:hh + 1, :], src[half, ds(i, 1), :], ACT.Copy)
        last.then_inc(s.qz, 1)

    def fox_act(act):
        act.drain().then_inc(fa.ex, 2)
        act.drain().then_inc(fa.pt, 2)
        with act.Fori(0, 8) as i:
            for hh in range(2):
                act.wait_ge(fnb.bc, 2 * i + hh + 1)
                act.activation(NBS[:, hh, :], PS[:, 2 + hh, :], ACT.Copy).then_inc(fnb.nb, 1)
            copy_queries(act, QK, i, fa)

            def exps(t):
                w = (t % 4 + 1) * P
                return act.activation(PB[:, t % 2, 0:w], PB[:, t % 2, 0:w], ACT.Exp, bias=NM[:, t % 4:t % 4 + 1],
                                      accum_out=RS[:, t % 4:t % 4 + 1])
            attn_act_body(act, fa, i, 8, lambda t: t % 4, exps)

    def fox_dve(dve):
        dve.drain().then_inc(fa.ov, 2)
        with dve.Fori(0, 8) as i:
            for hh in range(2):
                dve.tensor_copy(SELF[:, hh, :],
                                IDF[0:16, ds(2 * i + hh, 1)].to_broadcast([HEADS, P])).then_inc(fnb.sel, 1)
            for t in range(10):
                if t < 8:
                    w = (t % 4 + 1) * P
                    if t % 4 == 0:
                        dve.wait_ge(fnb.nb, 2 * i + t // 4 + 1)
                    dve.wait_ge(fa.sc, fa.at.sc + 8 * i + t + 1)
                    dve.wait_ge(fa.tr, fa.at.tr + 8 * i + t + 1)
                    dve.memset(RW[:, t % 4:t % 4 + 1], 0.0)
                    dve.drain()
                    dve.tensor_tensor_reduce(out=PB[:, t % 2, 0:w], in0=PS[:, t % 2, 0:w], in1=NBS[:, t // 4, 0:w],
                                             scale=1.0, scalar=-3e38, op0=ALU.add, op1=ALU.max,
                                             accum_out=RW[:, t % 4:t % 4 + 1])
                    dve.drain()
                    dve.tensor_scalar(NM[:, t % 4:t % 4 + 1], RW[:, t % 4:t % 4 + 1], -1.0, None,
                                      ALU.mult).then_inc(fa.mx, 1)
                if t >= 2:
                    k = t - 2
                    dve.wait_ge(fa.pv, fa.at.pv + 8 * i + k + 3)
                    dve.reciprocal(RW[:, 8 + k % 4:9 + k % 4], RS[:, k % 4:k % 4 + 1])
                    dve.drain()
                    dve.tensor_scalar(OB[:, k % 4, ds(i * P + (k // 4) * HD, HD)], PS[:, 6 + k % 2, 0:HD],
                                      RW[:, 8 + k % 4:9 + k % 4], None, ALU.mult).then_inc(fa.ov, 1)

    split_s = shared("split", "tr hi lo")

    def split_fm(src, dh, dl, gain=None, const=1.0):
        s = turn(split_s, tr=KT, hi=KT, lo=KT)

        def f_pe(pe):
            for f in range(KT):
                if f >= 4:
                    pe.wait_ge(s.lo, s.at.lo + f - 3)
                for c in range(NC_):
                    last = pe.transpose(PS[:, f % 4, c * P:(c + 1) * P], src[:, c, f * P:(f + 1) * P], IDF[:, :])
                last.then_inc(s.tr, 1)

        def f_act(act):
            for f in range(KT):
                act.wait_ge(s.tr, s.at.tr + f + 1)
                act.activation(dh[:, f, :], PS[:, f % 4, :], ACT.Copy,
                               scale=const if gain is None else gain).then_inc(s.hi, 1)

        def f_dve(dve):
            for f in range(KT):
                dve.wait_ge(s.hi, s.at.hi + f + 1)
                dve.scalar_tensor_tensor(out=dl[:, f, :], in0=PS[:, f % 4, :],
                                         scalar=const if gain is None else gain,
                                         in1=dh[:, f, :], op0=ALU.mult, op1=ALU.subtract).then_inc(s.lo, 1)
        return f_pe, f_act, f_dve, None

    OH = a_("OH", 0, [P, KT, SEQ], F32R)
    OL = a_("OL", 16, [P, KT, SEQ], F32R)

    def rope_tables_pool(pool, RAB, TABC, gain, s):
        g = BCP[:, gain:gain + HD]
        h = HD // 2
        for c in range(NC_):
            pool.tensor_tensor(RAB[:, c, 0, :], TABC[:, c, 0, :], g, ALU.mult)
            pool.tensor_tensor(RAB[:, c, 1, 0:h], TABC[:, c, 1, 0:h], g[:, h:HD], ALU.mult)
            pool.tensor_tensor(RAB[:, c, 1, h:HD], TABC[:, c, 1, h:HD], g[:, 0:h], ALU.mult)
        pool.drain().then_inc(s, 1)

    def rope_dve(dve, T, out, nh, RAB, SS, TMP):
        h = HD // 2
        for c in range(NC_):
            t = T(c)
            tmp = TMP[:, 0:nh * HD].rearrange("p (h d) -> p h d", h=nh)
            dve.tensor_tensor(t, t, SS[:, c * nh:(c + 1) * nh].unsqueeze(2).to_broadcast([P, nh, HD]), ALU.mult)
            dve.drain()
            for a, b in ((0, h), (h, 0)):
                dve.tensor_tensor(tmp[:, :, a:a + h], t[:, :, b:b + h],
                                  RAB[:, c, 1, a:a + h].unsqueeze(1).to_broadcast([P, nh, h]), ALU.mult)
            dve.drain()
            dve.tensor_tensor(t, t, RAB[:, c, 0, :].unsqueeze(1).to_broadcast([P, nh, HD]), ALU.mult)
            dve.drain()
            dve.tensor_tensor(out(c), t, tmp, ALU.add)
            dve.drain()

    def head_ss_dve(dve, T, nh, SS, TMP):
        for c in range(NC_):
            t = T(c)
            w = t.shape[2]
            tmp = TMP[:, 0:nh * w].rearrange("p (h d) -> p h d", h=nh)
            dve.tensor_tensor(tmp, t, t, ALU.mult)
            dve.drain()
            dve.tensor_reduce(SS[:, c * nh:(c + 1) * nh], tmp, AX, ALU.add)
            dve.drain()

    rope_s = shared("rope", "tab ss rt")

    def rope_stage(items, TABC, TMP, tabs_at, load=False):
        s = turn(rope_s, tab=len(items), ss=1, rt=1)
        at = [0]
        for it in items:
            at.append(at[-1] + NC_ * it[2])

        def f_pool(pool):
            pool.wait_ge(tabs, tabs_at)
            for _, _, _, RAB, gain in items:
                rope_tables_pool(pool, RAB, TABC, gain, s.tab)

        def f_act(act):
            if load:
                act.dma_start(TABC[:, :, :, :], A["rope_tok"]).then_inc(tabs, 16)
            act.wait_ge(s.ss, s.at.ss + 1)
            act.activation(TINY[:, 256:256 + at[-1]], TINY[:, 0:at[-1]], ACT.Sqrt, bias=EPS[:, 1:2],
                           scale=1.0 / HD).then_inc(s.rt, 1)

        def f_dve(dve):
            for k, (T, _, nh, _, _) in enumerate(items):
                head_ss_dve(dve, T, nh, TINY[:, at[k]:at[k + 1]], TMP)
            dve.drain().then_inc(s.ss, 1)
            dve.wait_ge(s.rt, s.at.rt + 1)
            dve.reciprocal(TINY[:, 0:at[-1]], TINY[:, 256:256 + at[-1]])
            dve.wait_ge(s.tab, s.at.tab + len(items))
            dve.drain()
            for k, (T, out_, nh, RAB, _) in enumerate(items):
                rope_dve(dve, T, out_, nh, RAB, TINY[:, at[k]:at[k + 1]], TMP)
        return None, f_act, f_dve, f_pool

    fm_s = shared("fm", "tr ev")

    def to_fm(items):
        s = turn(fm_s, tr=len(items), ev=len(items))

        def f_pe(pe):
            for k, (src, _, _) in enumerate(items):
                if k >= 4:
                    pe.wait_ge(s.ev, s.at.ev + k - 3)
                for c in range(NC_):
                    last = pe.transpose(PS[:, k % 4, c * P:(c + 1) * P], src(c), IDF[:, :])
                last.then_inc(s.tr, 1)

        def f_act(act):
            for k, (_, dst, scale) in enumerate(items):
                act.wait_ge(s.tr, s.at.tr + k + 1)
                if isinstance(dst, tuple):
                    for h, d in enumerate(dst):
                        for half in (0, HD):
                            last = act.activation(d[half:half + HD, :], PS[h * HD:(h + 1) * HD, k % 4, :], ACT.Copy)
                    last.then_inc(s.ev, 1)
                else:
                    act.activation(dst, PS[:, k % 4, :], ACT.Copy, scale=scale).then_inc(s.ev, 1)
        return f_pe, f_act, None, None

    def per(ap, n):
        return ap.rearrange("p (h d) -> p h d", h=n)

    tabs = sem("tabs")
    TQ = a_("TQ", 0, [P, NC_, DM])
    TK = a_("TK", 16, [P, NC_, DM])
    DV = a_("DV", 32, [P, NC_, DM])
    DQF = a_("DQF", 48, [P, KT, SEQ])
    DKF = a_("DKF", 64, [P, KT, SEQ])
    OD = a_("OD", 0, [P, NC_, DM])
    TABD = a_("TABD", 80, [P, NC_, 2, HD])
    RABQ = a_("RABQ", 82, [P, NC_, 2, HD])
    RABK = a_("RABK", 84, [P, NC_, 2, HD])
    TMPD = a_("TMPD", 86, [P, DM])
    QZD = a_("QZD", 80, [P, 2, SEQ])
    PBD = PB2 = a_("PBD", 84, [P, 4, SEQ])
    PTD = a_("PTD", 92, [P, 2, SEQ])
    YDH = a_("YDH", 88, [P, KT, SEQ], F32R)
    YDL = a_("YDL", 104, [P, KT, SEQ], F32R)
    dq, dk, dvs = (turn(left_s, left=4 + 8) for _ in range(3))
    dl = sems("dl", "a b")
    da = attn_turn(32, cb=34)

    def lam_dve(dve):
        for k in range(2):
            dve.tensor_tensor(TMPD[:, 64 * k:64 * k + 64], BCP[:, B_LAM + 128 * k:B_LAM + 128 * k + 64],
                              BCP[:, B_LAM + 128 * k + 64:B_LAM + 128 * k + 128], ALU.mult)
        dve.drain()
        dve.tensor_reduce(LAM[:, 1:3], TMPD[:, 0:128].rearrange("p (k d) -> p k d", k=2), AX, ALU.add)
        dve.drain().then_inc(dl.a, 1)
        dve.wait_ge(dl.b, 1)
        dve.tensor_tensor(LAM[:, 0:1], LAM[:, 4:5], LAM[:, 3:4], ALU.subtract)
        dve.drain()
        dve.tensor_scalar(LAM[:, 0:1], LAM[:, 0:1], -LAMBDA_INIT, None, ALU.add)
        dve.drain()

    def lam_act(act):
        act.wait_ge(dl.a, 1)
        act.activation(LAM[:, 3:5], LAM[:, 1:3], ACT.Exp).then_inc(dl.b, 1)

    def ring_attn_bodies(PBx, PTx):
        def pe_body(pe, s, idx, n, qb_of, scores, value, ready, width, nsub=1):
            B = idx * n
            for t in range(n + 2):
                if t < n:
                    pe.wait_ge(s.ex, s.at.ex + B + t + 1)
                    scores(t).then_inc(s.sc, 1)
                if 1 <= t <= n:
                    k = t - 1
                    pe.wait_ge(ready[0], ready[1] + B + k + 3)
                    pe.wait_ge(s.pt, s.at.pt + B + k + 1)
                    for b in range(qb_of(k) + 1):
                        last = pe.transpose(PS[:, 4 + k % 2, b * P:(b + 1) * P],
                                            PBx[:, nsub * (k % 2), b * P:(b + 1) * P], IDF[:, :])
                    last.then_inc(s.tr, 1)
                if t >= 2:
                    k = t - 2
                    pe.wait_ge(s.pt, s.at.pt + B + k + 3)
                    pe.wait_ge(s.ov, s.at.ov + B + k + 1)
                    for b in range(qb_of(k) + 1):
                        last = pe.matmul(PS[:, 6 + k % 2, 0:width], PTx[:, k % 2, b * P:(b + 1) * P], value(k, b),
                                         start=b == 0, stop=b == qb_of(k))
                    last.then_inc(s.pv, 1)

        def act_body(act, s, idx, n, qb_of, exps):
            B = idx * n
            for t in range(n + 1):
                if t < n:
                    act.wait_ge(s.mx, s.at.mx + B + t + 1)
                    act.wait_ge(s.tr, s.at.tr + B + t + 1)
                    exps(t).then_inc(s.ex, 1)
                if t >= 1:
                    k = t - 1
                    act.wait_ge(s.tr, s.at.tr + B + k + 3)
                    act.wait_ge(s.pv, s.at.pv + B + k + 1)
                    w = (qb_of(k) + 1) * P
                    act.activation(PTx[:, k % 2, 0:w], PS[:, 4 + k % 2, 0:w], ACT.Copy).then_inc(s.pt, 1)
        return pe_body, act_body

    dpe_body, dact_body = ring_attn_bodies(PBD, PTD)

    def zero_halves(QZx):
        def f(pool):
            pool.memset(QZx[64:128, 0, :], 0.0)
            pool.memset(QZx[0:64, 1, :], 0.0)
        return f

    def queries_into(act, QZx, src, i, s):
        for hh in range(2):
            half = slice(hh * HD, (hh + 1) * HD)
            last = act.activation(QZx[half, hh:hh + 1, :], src[half, ds(i, 1), :], ACT.Copy)
        last.then_inc(s.qz, 1)

    def diff_pe(pe):
        pe.drain().then_inc(da.tr, 2)
        pe.drain().then_inc(da.pv, 2)
        with pe.Fori(0, 8) as i:
            pe.wait_ge(da.qz, da.at.qz + i + 1)

            def both(t):
                for hh in range(2):
                    last = scores_pe(pe, 2 * (t % 2) + hh, QZD[:, hh, t * P:(t + 1) * P],
                                     lambda n: flat(DKF[:, ds(i, 1), 0:n]), t)
                return last
            dpe_body(pe, da, i, 4, lambda t: t, both, lambda k, b: DV[:, b, ds(i * P, P)], (da.cb, da.at.cb), P, nsub=2)

    def diff_act(act):
        act.drain().then_inc(da.ex, 2)
        act.drain().then_inc(da.pt, 2)
        with act.Fori(0, 8) as i:
            queries_into(act, QZD, DQF, i, da)

            def exps(t):
                w = (t + 1) * P
                for hh in range(2):
                    r = 2 * (t % 2) + hh
                    last = act.activation(PBD[:, r, 0:w], PS[:, r, 0:w], ACT.Exp, bias=NM[:, r:r + 1],
                                          accum_out=RS[:, r:r + 1])
                return last
            dact_body(act, da, i, 4, lambda t: t, exps)

    def diff_dve(dve):
        dve.drain().then_inc(da.ov, 2)
        dve.drain().then_inc(da.cb, 2)
        with dve.Fori(0, 8) as i:
            for t in range(6):
                if t < 4:
                    w = (t + 1) * P
                    r = 2 * (t % 2)
                    dve.wait_ge(da.sc, da.at.sc + 4 * i + t + 1)
                    for hh in range(2):
                        last = dve.tensor_reduce(NM[:, r + hh:r + hh + 1], PS[:, r + hh, 0:w], AX, ALU.max,
                                                 negate=True)
                    last.then_inc(da.mx, 1)
                    dve.wait_ge(da.ex, da.at.ex + 4 * i + t + 3)
                    dve.reciprocal(RW[:, r:r + 2], RS[:, r:r + 2])
                    dve.drain()
                    dve.tensor_scalar(RW[:, r + 1:r + 2], RW[:, r + 1:r + 2], LAM[:, 0:1], None, ALU.mult)
                    dve.tensor_scalar(PBD[:, r, 0:w], PBD[:, r, 0:w], RW[:, r:r + 1], None, ALU.mult)
                    dve.drain()
                    dve.scalar_tensor_tensor(out=PBD[:, r, 0:w], in0=PBD[:, r + 1, 0:w], scalar=RW[:, r + 1:r + 2],
                                             in1=PBD[:, r, 0:w], op0=ALU.mult, op1=ALU.add).then_inc(da.cb, 1)
                if t >= 2:
                    k = t - 2
                    dve.wait_ge(da.pv, da.at.pv + 4 * i + k + 3)
                    dve.tensor_copy(OD[:, k, ds(i * P, P)], PS[:, 6 + k % 2, 0:P]).then_inc(da.ov, 1)

    sl = sems("sl", "ss rt")
    TMPS = a_("TMPS", 16, [P, DM])

    def subln_act(act):
        act.wait_ge(sl.ss, 1)
        act.activation(TINY[:, 64:96], TINY[:, 0:32], ACT.Sqrt, bias=EPS[:, 1:2], scale=1.0 / P).then_inc(sl.rt, 1)

    def subln_dve(dve):
        def head(c):
            return per(OD[:, c, :], 8)
        head_ss_dve(dve, head, 8, TINY[:, 0:32], TMPS)
        dve.drain().then_inc(sl.ss, 1)
        dve.wait_ge(sl.rt, 1)
        dve.reciprocal(TINY[:, 0:32], TINY[:, 64:96])
        dve.drain()
        dve.tensor_scalar(TINY[:, 0:32], TINY[:, 0:32], 1.0 - LAMBDA_INIT, None, ALU.mult)
        dve.drain()
        for c in range(NC_):
            dve.tensor_tensor(head(c), head(c), TINY[:, c * 8:(c + 1) * 8].unsqueeze(2).to_broadcast([P, 8, P]),
                              ALU.mult)

    T3 = a_("T3", 16, [P, NC_, 6 * NSA_G * HD])
    QF = a_("QF", 40, [P, KT, SEQ])
    KF = [a_("KSF", 56, [P, NSA_G, SEQ]), a_("KWF", 64, [P, NSA_G, SEQ])]
    TABN = a_("TABN", 64, [P, NC_, 2, HD])
    RABN = [a_(f"RABN{k}", at, [P, NC_, 2, HD]) for k, at in enumerate((66, 56, 58))]
    TMPN = a_("TMPN", 60, [P, DM])
    ON = a_("ON", 0, [P, NC_, DM])
    nq, nkv = turn(left_s, left=4 + 8), turn(left_s, left=4 + 12)

    CW = [a_("CWK", 40, [P, 16, CMP_HIDDEN]), a_("CWV", 56, [P, 16, CMP_HIDDEN])]
    KC2 = a_("KC2", 72, [P, NSA_G, SEQ])
    RH = a_("RH", 80, [P, 16, P])
    HV = a_("HV", 40, [P, 2, NSA_G, 4, 32])
    VBD = a_("VBD", 84, [P, NSA_G, 4 * HD])
    CKT = a_("CKT", 72, [P, 4, 2, HD])
    cm = sems("cm", "w tr kc2 rh hid gel out ss rt kn kt pos")

    def cmp_dma(act):
        for n, (w1, w2_, pos) in enumerate((("cmp_k_w1_2", "cmp_k_w2_2", "cmp_pos_k_2"),
                                            ("cmp_v_w1_2", "cmp_v_w2_2", "cmp_pos_v_2"))):
            act.dma_start(CW[n][:, :, :], A[w1][0].rearrange("(k p) c -> p k c", p=P)).then_inc(cm.w, 16)
            act.dma_start(CW2[n][:, :, :], A[w2_][0].rearrange("(k p) c -> p k c", p=P)).then_inc(cm.w, 16)
            act.dma_start(CPROW[16 * n:16 * n + 16, :], A[pos][0].rearrange("(k l) d -> k (l d)", l=2)).then_inc(cm.w, 16)
        act.dma_start(TABK[:, :, :], A["rope_cmp"]).then_inc(cm.w, 16)

    def cmp_pe(pe):
        pe.wait_ge(cm.w, 16 * 7)
        pe.transpose(PS[:, 5, 0:32], CPROW[:, :], IDF[0:32, 0:32]).then_inc(cm.pos, 1)
        for n in range(2):
            if n:
                pe.wait_ge(cm.kc2, 1)
            for j in range(2):
                for c in range(NC_):
                    last = pe.transpose(PS[:, j, c * P:(c + 1) * P], T3[:, c, n * 256 + j * P:n * 256 + (j + 1) * P],
                                        IDF[:, :])
            last.then_inc(cm.tr, 1)
            pe.wait_ge(cm.rh, n + 1)
            pe.wait_ge(cm.w, 16 * 7)
            for m in range(2):
                for k in range(16):
                    last = pe.matmul(PS[:, 4, m * P:(m + 1) * P], CW[n][:, k, m * P:(m + 1) * P], RH[:, k, :],
                                     start=k == 0, stop=k == 15)
            last.then_inc(cm.hid, 1)
            pe.wait_ge(cm.gel, n + 1)
            if n == 0:
                for m in range(2):
                    last = pe.matmul(PS[:, 5, 0:HD], TINY[:, m * P:(m + 1) * P], CW2[0][:, m, :],
                                     start=m == 0, stop=m == 1)
                last.then_inc(cm.out, 1)
                pe.wait_ge(cm.kn, 1)
                pe.transpose(PS[:, 6, 0:P], CKT[:, 3, :, :].rearrange("p a d -> p (a d)"), IDF[:, :]).then_inc(cm.kt, 1)
            else:
                for g in range(NSA_G):
                    for m in range(2):
                        last = pe.matmul(PS[:, 7, g * HD:(g + 1) * HD], HV[:, m, g, :, :].rearrange("p a n -> p (a n)"),
                                         CW2[1][:, m, :], start=m == 0, stop=m == 1)
                last.then_inc(cm.out, 1)

    def cmp_act(act):
        cmp_dma(act)
        for n in range(2):
            act.wait_ge(cm.tr, n + 1)
            for g in range(NSA_G):
                half = slice((g % 2) * HD, (g % 2 + 1) * HD)
                act.activation(KC2[0:HD, g, :], PS[half, g // 2, :], ACT.Copy)
                act.activation(KC2[HD:P, g, 0:SEQ - 1], PS[half, g // 2, 1:SEQ], ACT.Copy)
            act.drain().then_inc(cm.kc2, 1)
            act.wait_ge(cm.hid, n + 1)
            hid = PS[:, 4, 0:2 * P]
            if n == 0:
                act.activation(TINY[:, 0:2 * P], hid, ACT.Gelu_apprx_tanh)
            else:
                for r in range(4):
                    act.activation(HV[:, :, :, r, :], hid.rearrange("p (m g n) -> p m g n", m=2, g=NSA_G),
                                   ACT.Gelu_apprx_tanh)
            act.drain().then_inc(cm.gel, 1)
            if n == 0:
                act.wait_ge(cm.ss, 1)
                act.activation(LAM[:, 5:6], LAM[:, 6:7], ACT.Sqrt, bias=EPS[:, 1:2], scale=1.0 / HD).then_inc(cm.rt, 1)
                act.wait_ge(cm.kt, 1)
                act.activation(KCF[:, :, :], PS[:, 6, 0:P].rearrange("p (g n) -> p g n", g=NSA_G), ACT.Copy)

    def cmp_dve(dve):
        dve.wait_ge(cm.pos, 1)
        dve.tensor_copy(CPOS[:, :, :], PS[:, 5, 0:32].rearrange("p (n k) -> p n k", n=2))
        for n in range(2):
            if n:
                dve.wait_ge(cm.hid, 1)
            dve.wait_ge(cm.kc2, n + 1)
            dve.memset(RH[:, :, :], 0.0)
            dve.wait_ge(cm.w, 16 * 7)
            dve.drain()
            for k in range(16):
                dst = RH[:, k, :].rearrange("p (g n) -> p g n", g=NSA_G)[:, :, 0:NCMP]
                src = KC2[:, :, 2 * k:2 * k + CMP_STRIDE * (NCMP - 1) + 1:CMP_STRIDE]
                dve.tensor_scalar(dst, src, CPOS[:, n, k:k + 1], None, ALU.add)
            dve.drain().then_inc(cm.rh, 1)
            dve.wait_ge(cm.out, n + 1)
            if n == 0:
                dve.tensor_copy(CKT[:, 0, 0, :], PS[:, 5, 0:HD])
                dve.drain()
                dve.tensor_tensor(CKT[:, 0, 1, :], CKT[:, 0, 0, :], CKT[:, 0, 0, :], ALU.mult)
                dve.drain()
                dve.tensor_reduce(LAM[:, 6:7], CKT[:, 0, 1, :], AX, ALU.add).then_inc(cm.ss, 1)
                dve.wait_ge(cm.rt, 1)
                dve.reciprocal(LAM[:, 7:8], LAM[:, 5:6])
                dve.drain()
                x, h = CKT[:, 0, 0, :], HD // 2
                dve.tensor_scalar(x, x, LAM[:, 7:8], None, ALU.mult)
                dve.drain()
                dve.tensor_tensor(x, x, BCP[:, B_GAIN["kc"]:B_GAIN["kc"] + HD], ALU.mult)
                dve.drain()
                dve.tensor_tensor(CKT[:, 1, 0, :], x, TABK[:, 0, :], ALU.mult)
                dve.tensor_tensor(CKT[:, 1, 1, 0:h], x[:, h:HD], TABK[:, 1, 0:h], ALU.mult)
                dve.tensor_tensor(CKT[:, 1, 1, h:HD], x[:, 0:h], TABK[:, 1, h:HD], ALU.mult)
                dve.drain()
                for a in range(2):
                    dve.tensor_tensor(CKT[:, 3, a, :], CKT[:, 1, 0, :], CKT[:, 1, 1, :], ALU.add)
                dve.drain().then_inc(cm.kn, 1)
                dve.wait_ge(cm.kt, 1)
            else:
                dve.memset(VBD[:, :, :], 0.0)
                dve.drain()
                for a in range(4):
                    rows_ = slice(32 * a, 32 * a + 32)
                    dve.tensor_copy(VBD[rows_, :, a * HD:(a + 1) * HD], per(PS[rows_, 7, 0:256], NSA_G))

    SC = a_("SC", 72, [P, NC_ * HPG, 32])
    CMASK = a_("CMASK", 74, [P, NC_, 32])
    PTC = a_("PTC", 76, [P, SEQ])
    ca = sems("ca", "gate sig mask sc m ex p tr pt o od")

    def cattn_pe(pe):
        small_gemm_pe(pe, 7, SW[1], 0, 48).then_inc(ca.gate, 1)
        for g in range(NSA_G):
            if g:
                pe.wait_ge(ca.m, g)
            for qb in range(NC_):
                for hg in range(HPG):
                    h = HPG * g + hg
                    half = slice((h % 2) * HD, (h % 2 + 1) * HD)
                    k = (qb * 2 + hg // 2) * 32
                    last = pe.matmul(PS[:, 4 * (hg % 2), k:k + 32], QF[half, h // 2, qb * P:(qb + 1) * P], KCF[half, g, :],
                                     start=True, stop=True)
            last.then_inc(ca.sc, 1)
            pe.wait_ge(ca.p, g + 1)
            if g:
                pe.wait_ge(ca.pt, g)
            for qb in range(NC_):
                last = pe.transpose(PS[:, 1, qb * P:(qb + 1) * P],
                                    SC[:, qb * HPG:(qb + 1) * HPG, :].rearrange("p a n -> p (a n)"), IDF[:, :])
            last.then_inc(ca.tr, 1)
            pe.wait_ge(ca.pt, g + 1)
            if g:
                pe.wait_ge(ca.od, g)
            for qb in range(NC_):
                last = pe.matmul(PS[:, 2 + qb // 2, (qb % 2) * 256:(qb % 2) * 256 + 256],
                                 PTC[:, qb * P:(qb + 1) * P], VBD[:, g, :], start=True, stop=True)
            last.then_inc(ca.o, 1)

    def cattn_act(act):
        act.wait_ge(ca.gate, 1)
        act.activation(GT[:, :, :], PS[:, 7, 0:192].rearrange("p (c k) -> p c k", c=NC_), ACT.Sigmoid)
        act.drain().then_inc(ca.sig, 1)
        for g in range(NSA_G):
            act.wait_ge(ca.m, g + 1)
            act.activation(SC[:, :, :], SC[:, :, :], ACT.Exp).then_inc(ca.ex, 1)
            act.wait_ge(ca.tr, g + 1)
            if g:
                act.wait_ge(ca.o, g)
            act.activation(PTC[:, :], PS[:, 1, :], ACT.Copy).then_inc(ca.pt, 1)

    def cattn_pool(pool):
        pool.memset(CMASK[:, :, :], 0.0)
        pool.drain().then_inc(ca.mask, 1)
        pool.wait_ge(ca.mask, 1)
        pool.affine_select(out=CMASK[:, :, :], in_=CMASK[:, :, :], compare_op=ALU.is_ge, fill=MASKED,
                           base=-(CMP_BLOCK - 1), pattern=[[P, NC_], [-CMP_STRIDE, 32]], channel_multiplier=1)
        pool.drain().then_inc(ca.mask, 1)

    def cattn_dve(dve):
        n = NC_ * HPG
        dve.wait_ge(ca.mask, 2)
        dve.wait_ge(ca.sig, 1)
        for g in range(NSA_G):
            dve.wait_ge(ca.sc, g + 1)
            if g:
                dve.wait_ge(ca.tr, g)
            for r in range(2):
                dve.tensor_tensor(SC[:, :, :].rearrange("p (a b two) k -> p a b two k", a=NC_, two=2)[:, :, :, r, :],
                                  PS[:, 4 * r, 0:256].rearrange("p (a b k) -> p a b k", a=NC_, b=2),
                                  CMASK[:, :, :].unsqueeze(2).to_broadcast([P, NC_, 2, 32]), ALU.add)
            dve.drain()
            dve.tensor_reduce(TINY[:, 0:n], SC[:, :, :], AX, ALU.max)
            dve.drain()
            dve.tensor_scalar(TINY[:, 0:n], TINY[:, 0:n], MASKED / 10, None, ALU.max)
            dve.drain()
            dve.tensor_tensor(SC[:, :, :], SC[:, :, :], TINY[:, 0:n].unsqueeze(2).to_broadcast([P, n, 32]),
                              ALU.subtract)
            dve.drain().then_inc(ca.m, 1)
            dve.wait_ge(ca.ex, g + 1)
            dve.tensor_reduce(TINY[:, 16:16 + n], SC[:, :, :], AX, ALU.add)
            dve.drain()
            dve.tensor_scalar(TINY[:, 16:16 + n], TINY[:, 16:16 + n], 1e-30, None, ALU.max)
            dve.drain()
            dve.reciprocal(TINY[:, 32:32 + n], TINY[:, 16:16 + n])
            dve.drain()
            dve.tensor_tensor(TINY[:, 48:48 + n].rearrange("p (a b) -> p a b", a=NC_),
                              TINY[:, 32:32 + n].rearrange("p (a b) -> p a b", a=NC_),
                              GT[:, :, 12 * g:12 * g + 10:3], ALU.mult)
            dve.drain()
            dve.tensor_tensor(SC[:, :, :], SC[:, :, :], TINY[:, 48:48 + n].unsqueeze(2).to_broadcast([P, n, 32]),
                              ALU.mult)
            dve.drain().then_inc(ca.p, 1)
            dve.wait_ge(ca.o, g + 1)
            for b in range(2):
                dve.tensor_copy(ON[:, 2 * b:2 * b + 2, g * 256:(g + 1) * 256],
                                PS[:, 2 + b, :].rearrange("p (a k) -> p a k", a=2))
            dve.drain().then_inc(ca.od, 1)

    QZN = a_("QZN", 72, [P, 2, SEQ])
    PBN = a_("PBN", 76, [P, 2, SEQ])
    PTN = a_("PTN", 80, [P, 2, SEQ])
    npe_body, nact_body = ring_attn_bodies(PBN, PTN)
    na = attn_turn(128)
    NSTEP = 16

    def nsa_loop(e, body):
        with e.Fori(0, NSA_G) as g:
            with e.Fori(0, 2) as j:
                body(g, 2 * g + j)

    def nsa_pe(pe):
        pe.drain().then_inc(na.tr, 2)
        pe.drain().then_inc(na.pv, 2)

        def body(g, i):
            pe.wait_ge(na.qz, na.at.qz + i + 1)
            npe_body(pe, na, i, NSTEP, lambda t: t % 4,
                     lambda t: scores_pe(pe, t % 2, QZN[:, t // 8, (t % 4) * P:(t % 4 + 1) * P],
                                         lambda n: flat(KF[t // 4 % 2][:, ds(g, 1), 0:n]), t % 4),
                     lambda k, b: T3[:, b, ds(768 + 512 * (k // 4 % 2) + HD * g, HD)], (na.ex, na.at.ex), HD)
        nsa_loop(pe, body)

    def nsa_act(act):
        act.drain().then_inc(na.ex, 2)
        act.drain().then_inc(na.pt, 2)

        def body(g, i):
            queries_into(act, QZN, QF, i, na)

            def exps(t):
                w = (t % 4 + 1) * P
                return act.activation(PBN[:, t % 2, 0:w], PS[:, t % 2, 0:w], ACT.Exp, bias=NM[:, t % 4:t % 4 + 1],
                                      accum_out=RS[:, t % 4:t % 4 + 1])
            nact_body(act, na, i, NSTEP, lambda t: t % 4, exps)
        nsa_loop(act, body)

    def nsa_dve(dve):
        dve.drain().then_inc(na.ov, 2)

        def body(g, i):
            for t in range(NSTEP + 2):
                if t < NSTEP:
                    w = (t % 4 + 1) * P
                    dve.wait_ge(na.sc, na.at.sc + NSTEP * i + t + 1)
                    dve.tensor_reduce(NM[:, t % 4:t % 4 + 1], PS[:, t % 2, 0:w], AX, ALU.max,
                                      negate=True).then_inc(na.mx, 1)
                if t >= 2:
                    k = t - 2
                    r = 8 + k % 4
                    hh, branch, qb = k // 8, k // 4 % 2, k % 4
                    dve.wait_ge(na.pv, na.at.pv + NSTEP * i + k + 3)
                    dve.reciprocal(RW[:, r:r + 1], RS[:, k % 4:k % 4 + 1])
                    dve.drain()
                    dve.tensor_tensor(RW[:, r:r + 1], RW[:, r:r + 1], GT[:, qb, ds(6 * i + 3 * hh + 1 + branch, 1)],
                                      ALU.mult)
                    dve.drain()
                    o = ON[:, qb, ds(i * P + hh * HD, HD)]
                    dve.scalar_tensor_tensor(out=o, in0=PS[:, 6 + k % 2, 0:HD], scalar=RW[:, r:r + 1], in1=o,
                                             op0=ALU.mult, op1=ALU.add)
                    dve.drain().then_inc(na.ov, 1)
        nsa_loop(dve, body)

    YNH = a_("YNH", 16, [P, KT, SEQ], F32R)
    YNL = a_("YNL", 32, [P, KT, SEQ], F32R)
    MXH = a_("MXH", 48, [P, KT, SEQ], F32R)
    MXL = a_("MXL", 64, [P, KT, SEQ], F32R)
    SG = a_("SG", 80, [P, 2, SEQ])
    MT = a_("MT", 84, [P, 2, SEQ])
    mg = sems("mg", "sig y hi free")

    def merge_pe(pe):
        def body(i):
            for u in range(4):
                pe.wait_ge(mg.free, i + 1)
                ah, al = ((YDH, YDL), (YNH, YNL), (XH, XL), (XH, XL))[u]
                unit_fm(pe, first["merge"], 4, i, u, PS[:, u, :], ah, al)
        loop(pe, "merge", body)

    def merge_act(act):
        def body(i):
            for u in range(4):
                ring_step(hi, act, "merge", i, u)
                if u >= 2:
                    act.wait_ge(mg.free, i + 1)
                    act.wait_ge(unit_done, first["merge"] + 4 * i + u + 1)
                    act.activation(SG[:, u - 2, :], PS[:, u, :], ACT.Sigmoid).then_inc(mg.sig, 1)
            act.wait_ge(mg.y, i + 1)
            act.activation(MXH[:, ds(i, 1), :], MT[:, 0:1, :], ACT.Copy).then_inc(mg.hi, 1)
        loop(act, "merge", body)

    def merge_dve(dve):
        dve.drain().then_inc(mg.free, 1)

        def body(i):
            for u in range(4):
                ring_step(lo, dve, "merge", i, u)
            dve.wait_ge(mg.sig, 2 * i + 2)
            dve.wait_ge(unit_done, first["merge"] + 4 * i + 4)
            for k in range(2):
                dve.tensor_tensor(MT[:, k, :], SG[:, k, :], PS[:, k, :], ALU.mult)
            dve.drain()
            dve.tensor_tensor(MT[:, 0, :], MT[:, 0, :], MT[:, 1, :], ALU.add).then_inc(mg.y, 1)
            dve.wait_ge(mg.hi, i + 1)
            dve.tensor_tensor(MXL[:, ds(i, 1), :], MT[:, 0:1, :], MXH[:, ds(i, 1), :], ALU.subtract)
            dve.drain().then_inc(mg.free, 1)
        loop(dve, "merge", body)

    MH = a_("MH", 0, [P, 16, SEQ], F32R)
    ML = a_("ML", 32, [P, 16, SEQ], F32R)
    RL = a_("RL", 64, [P, 4, SEQ])

    up_s = shared("up", "relu y hi")

    def mlp_up(name):
        s = turn(up_s, relu=2 + 16, y=2 + 16, hi=16)

        def f_pe(pe):
            def body(i):
                for u in range(2):
                    pe.wait_ge(s.relu, s.at.relu + 2 * i + u + 1)
                    unit_fm(pe, first[name], 2, i, u, PS[:, u, :], XH, XL)
            loop(pe, name, body)

        def f_act(act):
            act.drain().then_inc(s.relu, 2)

            def body(i):
                for u in range(2):
                    ring_step(hi, act, name, i, u)
                    act.wait_ge(unit_done, first[name] + 2 * i + u + 1)
                    act.wait_ge(s.y, s.at.y + 2 * i + u + 1)
                    act.activation(RL[:, u, :], PS[:, u, :], ACT.Relu).then_inc(s.relu, 1)
                    act.wait_ge(s.y, s.at.y + 2 * i + u + 3)
                    act.activation(MH[:, ds(2 * i + u, 1), :], RL[:, 2 + u:3 + u, :], ACT.Copy).then_inc(s.hi, 1)
            loop(act, name, body)

        def f_dve(dve):
            dve.drain().then_inc(s.y, 2)

            def body(i):
                for u in range(2):
                    ring_step(lo, dve, name, i, u)
                    dve.wait_ge(s.relu, s.at.relu + 2 * i + u + 3)
                    dve.tensor_tensor(RL[:, 2 + u, :], RL[:, u, :], RL[:, u, :], ALU.mult).then_inc(s.y, 1)
                    dve.wait_ge(s.hi, s.at.hi + 2 * i + u + 1)
                    dve.tensor_tensor(ML[:, ds(2 * i + u, 1), :], RL[:, 2 + u:3 + u, :], MH[:, ds(2 * i + u, 1), :],
                                      ALU.subtract)
                    dve.drain()
            loop(dve, name, body)
        return f_pe, f_act, f_dve, None

    def add_banks(dve):
        for m in range(KT):
            dve.tensor_tensor(X[:, m, :], X[:, m, :], PS[:, m, :], ALU.add)

    n0, n1, n2, n3 = (norm_turn() for n in range(4))
    f0, f1 = ffn_turn(), ffn_turn()
    fin = sems("fin", "tr out st")
    OT = a_("OT", 0, [P, NC_, DM])
    want = list(size)

    r0, r1 = (turn(norm_s, cent=KT, sq=KT, ssq=KT, std=1, tmp=KT, hi=KT) for n in range(2))

    def tm_stage(name, s, dst, table=None):
        def f_act(act):
            if table is not None:
                act.dma_start(table[:, :, :, :], A["rope_tok"]).then_inc(tabs, 16)
            tm_act(act, name, s, lambda i, c: dst[:, c, ds(512 * i, 512)])
        return (lambda e: tm_pe(e, name, s)), f_act, (lambda e: split_only(lo, e, name)), None

    def finish_pe(pe):
        for f in range(KT):
            if f >= 4:
                pe.wait_ge(fin.out, f - 3)
            for c in range(NC_):
                last = pe.transpose(PS[:, f % 4, c * P:(c + 1) * P], X[:, f, c * P:(c + 1) * P], IDF[:, :])
            last.then_inc(fin.tr, 1)

    def finish_dve(dve):
        for f in range(KT):
            dve.wait_ge(fin.tr, f + 1)
            dve.tensor_copy(OT[:, :, f * P:(f + 1) * P],
                            PS[:, f % 4, :].rearrange("p (c t) -> p c t", c=NC_)).then_inc(fin.out, 1)

    def stages(e, kind):
        fns = STAGES[kind]
        for k, fn in enumerate(fns):
            if fn is not None:
                fn(e)
            barrier(e, kind)

    plan = [
        (setup_pe, setup_act, setup_dve, setup_pool),
        (gate_pe, gate_act, gate_dve, None),
        (xbc_pe, xbc_act, xbc_dve, None),
        (ssd_pe, ssd_act, ssd_dve, None),
        (ssdh_pe, ssdh_act, ssdh_dve, None),
        (lambda e: tm_pe(e, "z", zs), lambda e: tm_act(e, "z", zs, lambda i, c: Z[:, c, ds(512 * i, 512)], ACT.Silu),
         lambda e: split_only(lo, e, "z"), None),
        (gnorm_pe, gnorm_act, gnorm_dve, None),
        (lambda e: kmajor_pe(e, "out0", YH, YL), lambda e: split_only(hi, e, "out0"), lambda e: split_only(lo, e, "out0"), None),
        (lambda e: ln_pe(e, n0), lambda e: ln_act(e, n0, C_LMG, C_LMB), lambda e: ln_dve(e, n0, C_LMG, C_LMB), None),
        (lambda e: ffn_up_pe(e, 0, f0), lambda e: ffn_up_act(e, 0, f0), lambda e: ffn_up_dve(e, 0, f0), None),
        (lambda e: kmajor_pe(e, "down0", FH, FL), lambda e: split_only(hi, e, "down0"), lambda e: split_only(lo, e, "down0"), None),
        (lambda e: ln_pe(e, n1), lambda e: ln_act(e, n1, C_LFG, C_LFB), lambda e: ln_dve(e, n1, C_LFG, C_LFB), None),
        (lambda e: fm_pe(e, "foxqk", fq), foxqk_act, lambda e: split_only(lo, e, "foxqk"), None),
        (lambda e: tm_pe(e, "foxv", fv), lambda e: tm_act(e, "foxv", fv, lambda i, c: VT[:, c, ds(512 * i, 512)]),
         lambda e: split_only(lo, e, "foxv"), zero_qz),
        (forget_pe, forget_act, forget_dve, None),
        (fox_pe, fox_act, fox_dve, None),
        split_fm(OB, OH, OL),
        (lambda e: kmajor_pe(e, "foxout", OH, OL), lambda e: split_only(hi, e, "foxout"),
         lambda e: split_only(lo, e, "foxout"), None),
        (lambda e: ln_pe(e, n2), lambda e: ln_act(e, n2, C_LMG + 8, C_LMB + 8),
         lambda e: ln_dve(e, n2, C_LMG + 8, C_LMB + 8), None),
        (lambda e: ffn_up_pe(e, 1, f1), lambda e: ffn_up_act(e, 1, f1), lambda e: ffn_up_dve(e, 1, f1), None),
        (lambda e: kmajor_pe(e, "down1", FH, FL), lambda e: split_only(hi, e, "down1"), lambda e: split_only(lo, e, "down1"), None),
        (lambda e: ln_pe(e, n3), lambda e: ln_act(e, n3, C_LFG + 8, C_LFB + 8),
         lambda e: ln_dve(e, n3, C_LFG + 8, C_LFB + 8), None),
        (lambda e: ssq_pe(e, r0), lambda e: rms_act(e, r0, C_MG2), lambda e: rms_dve(e, r0, C_MG2, False), None),
        tm_stage("dq", dq, TQ, TABD),
        tm_stage("dk", dk, TK),
        tm_stage("dv", dvs, DV),
        rope_stage([(lambda c: per(TQ[:, c, :], 16), lambda c: per(TQ[:, c, :], 16), 16, RABQ, B_GAIN["dq"]),
                          (lambda c: per(TK[:, c, :], 16), lambda c: per(TK[:, c, :], 16), 16, RABK, B_GAIN["dk"])],
                   TABD, TMPD, 16),
        to_fm([(lambda c, f=f: TQ[:, c, f * P:(f + 1) * P], DQF[:, f, :], SCALE) for f in range(KT)]
              + [(lambda c, f=f: TK[:, c, f * P:(f + 1) * P], DKF[:, f, :], 1.0) for f in range(KT)]),
        (None, lam_act, lam_dve, zero_halves(QZD)),
        (diff_pe, diff_act, diff_dve, None),
        (None, subln_act, subln_dve, None),
        split_fm(OD, YDH, YDL, gain=PCOL[:, C_SUB:C_SUB + 1]),
        tm_stage("nq", nq, TQ),
        tm_stage("nkv", nkv, T3),
        (cmp_pe, cmp_act, cmp_dve, None),
        rope_stage([(lambda c: per(TQ[:, c, :], 16), lambda c: per(TQ[:, c, :], 16), 16, RABN[0], B_GAIN["nq"]),
                          (lambda c: per(T3[:, c, 512:768], 4), lambda c: per(T3[:, c, 512:768], 4), 4, RABN[1],
                           B_GAIN["ks"]),
                          (lambda c: per(T3[:, c, 1024:1280], 4), lambda c: per(T3[:, c, 1024:1280], 4), 4, RABN[2],
                           B_GAIN["kw"])], TABN, TMPN, 32, load=True),
        to_fm([(lambda c, f=f: TQ[:, c, f * P:(f + 1) * P], QF[:, f, :], SCALE) for f in range(KT)]
              + [(lambda c, b=b, j=j: T3[:, c, 512 + 512 * b + j * P:512 + 512 * b + (j + 1) * P],
                  (KF[b][:, 2 * j, :], KF[b][:, 2 * j + 1, :]), 1.0) for b in range(2) for j in range(2)]),
        (cattn_pe, cattn_act, cattn_dve, cattn_pool),
        (None, None, None, zero_halves(QZN)),
        (nsa_pe, nsa_act, nsa_dve, None),
        split_fm(ON, YNH, YNL),
        (merge_pe, merge_act, merge_dve, None),
        (lambda e: kmajor_pe(e, "out2", MXH, MXL), lambda e: split_only(hi, e, "out2"),
         lambda e: split_only(lo, e, "out2"), None),
        (lambda e: ssq_pe(e, r1), lambda e: rms_act(e, r1, C_ML2), lambda e: rms_dve(e, r1, C_ML2, True), None),
        mlp_up("mupa"),
        (lambda e: kmajor_pe(e, "mdna", MH, ML), lambda e: split_only(hi, e, "mdna"),
         lambda e: split_only(lo, e, "mdna"), None),
        (None, None, add_banks, None),
        mlp_up("mupb"),
        (lambda e: kmajor_pe(e, "mdnb", MH, ML), lambda e: split_only(hi, e, "mdnb"),
         lambda e: split_only(lo, e, "mdnb"), None),
        (None, None, add_banks, None),
    ]
    plan.append((finish_pe, None, finish_dve, None))
    STAGES = {k: [p[j] for p in plan] for j, k in enumerate(("pe", "act", "dve", "pool"))}

    block = ctx.enter_context(nc.Block())

    @block.sync
    def _(sp):
        for name, U, bodies, src in STREAM:
            b = first[name]

            def body(i):
                for u in range(U):
                    slot = u % 2
                    s = src(i, u)
                    if b + u < 2 and isinstance(i, int) and i == 0:
                        pass
                    else:
                        sp.wait_ge(lo_ready, b + u - 1 + U * i)
                    dst = RAW[:, slot, :].rearrange("p (k c) -> p k c", k=s.shape[1])
                    sp.dma_start(dst, s).then_inc(raw_loaded[slot], 16)
            start = 0
            if b == 0:
                body(0)
                start = 1
            with sp.Fori(start, bodies) as i:
                body(i)
        sp.wait_ge(stage_end, 4 * len(plan))
        sp.dma_start(out[0].rearrange("(c p) f -> p c f", p=P), OT[:, :, :]).then_inc(fin.st, 16)
        sp.wait_ge(fin.st, 16)

    @block.gpsimd
    def _(pool):
        stages(pool, "pool")

    @block.scalar
    def _(act):
        setup_dma(act)
        stages(act, "act")

    @block.vector
    def _(dve):
        stages(dve, "dve")

    @block.tensor
    def _(pe):
        stages(pe, "pe")

    ctx.close()


def constants():
    half = HD // 2
    inv = np.float32(10000.0) ** (-np.arange(half, dtype=np.float32) / np.float32(half))

    def table(pos):
        ang = pos.astype(np.float32)[:, None] * inv[None, :]
        c, s = np.cos(ang), np.sin(ang)
        return np.stack([np.concatenate([c, c], 1), np.concatenate([-s, s], 1)], 1).astype(np.float32)

    tok = table(np.arange(SEQ)).reshape(NC_, P, 2, HD).transpose(1, 0, 2, 3)
    centres = np.zeros((32, 2, HD), np.float32)
    centres[:NCMP] = table(np.arange(NCMP) * CMP_STRIDE + (CMP_BLOCK - 1) / 2.0)
    return {"rope_tok": np.ascontiguousarray(tok), "rope_cmp": np.ascontiguousarray(np.tile(centres, (NSA_G, 1, 1)))}


def kernel(**inputs):
    from concourse import bacc
    from concourse.bass_utils import run_bass_kernel_spmd

    nc = bacc.Bacc("TRN2", target_bir_lowering=False, num_devices=1)
    arrays, aps = {}, {}
    for name, value in {**inputs, **constants()}.items():
        a = np.ascontiguousarray(value)
        arrays[f"in_{name}"] = a
        aps[name] = nc.dram_tensor(f"in_{name}", a.shape, mybir.dt.from_np(a.dtype), kind="ExternalInput").ap()
    out = nc.dram_tensor("out", (1, SEQ, DM), F32, kind="ExternalOutput").ap()
    build(nc, aps, out)
    r = run_bass_kernel_spmd(nc, [arrays], core_ids=[0])
    return r.results[0]["out"]
```

```python
import math
from collections import namedtuple
from contextlib import ExitStack

import numpy as np
import concourse.bass as bass
from concourse import mybir

F32, F32R, BF16 = mybir.dt.float32, mybir.dt.float32r, mybir.dt.bfloat16
ALU = mybir.AluOpType
ACT = mybir.ActivationFunctionType
AX = mybir.AxisListType.X

P = 128
SEQ, DM = 512, 1024
NC_ = SEQ // P
KT = DM // P
DEPTH = 2
ALPHA = (2 * DEPTH) ** 0.25
LN_EPS, RMS_EPS = 1e-5, 1e-6
HEADS, HD = 16, 64
SCALE = HD ** -0.5
STATE, GROUPS = 128, 2
DFF = 2816
FT = DFF // P
DFF2 = 4096
FT2 = DFF2 // P
CMP_BLOCK, CMP_STRIDE, CMP_HIDDEN = 32, 16, 256
NCMP = (SEQ - CMP_BLOCK) // CMP_STRIDE + 1
NSA_G = 4
HPG = HEADS // NSA_G
MASKED = -1e30
LAMBDA_INIT = 0.8 - 0.6 * math.exp(0.0)
ds = bass.ds


def build(nc, A, out):
    ctx = ExitStack()
    base = (nc.sbuf_base + 63) // 64 * 64
    cursor = [base]

    def place(name, shape, dt=F32, at=None):
        size = int(np.prod(shape[1:])) * (2 if dt == BF16 else 4)
        if at is None:
            at = cursor[0]
            cursor[0] += (size + 31) // 32 * 32
        return nc.alloc_sbuf_tensor_at(name, shape, dt, offset=at)

    def sem(name):
        return ctx.enter_context(nc.semaphore(name))

    def sems(prefix, names):
        return namedtuple(prefix, names)(*[sem(f"{prefix}_{n}") for n in names.split()])

    def shared(prefix, names):
        return (namedtuple(prefix, names + " at"), namedtuple(prefix + "_at", names),
                {n: sem(f"{prefix}_{n}") for n in names.split()}, {n: 0 for n in names.split()})

    def turn(sh_, **counts):
        view, view_at, the_sems, so_far = sh_
        s = view(**the_sems, at=view_at(**so_far))
        for name, n in counts.items():
            so_far[name] += n
        return s

    RAW = place("RAW", [P, 2, 1024])
    WH = place("WH", [P, 2, 1024], F32R)
    WL = place("WL", [P, 2, 1024], F32R)
    X = place("X", [P, KT, SEQ])
    XH = place("XH", [P, KT, SEQ], F32R)
    XL = place("XL", [P, KT, SEQ], F32R)
    IDF = place("IDF", [P, P])
    ONES = place("ONES", [P, P])
    IDB = place("IDB", [P, P], BF16)
    MROW = place("MROW", [P, P], BF16)
    MCOL = place("MCOL", [P, P], BF16)
    PCOL = place("PCOL", [P, 608])
    BCP = place("BCP", [P, 768])
    narrow1 = cursor[0]
    SW = [(place("SWH1", [P, KT, 32], F32R), place("SWL1", [P, KT, 32], F32R)),
          (place("SWH2", [P, KT, 48], F32R), place("SWL2", [P, KT, 48], F32R))]
    TINY = place("TINY", [P, 512])
    EPS = place("EPS", [P, 2])
    NM = place("NM", [P, 16])
    RS = place("RS", [P, 16])
    RW = place("RW", [P, 16])
    LAM = place("LAM", [P, 8])
    CW2 = [place("CW2K", [P, 2, HD], at=narrow1), place("CW2V", [P, 2, HD], at=narrow1 + 512)]
    CPOS = place("CPOS", [P, 2, 16], at=narrow1 + 1024)
    TABK = place("TABK", [P, 2, HD], at=narrow1 + 1152)
    GT = place("GT", [P, NC_, 48])
    kcf_at = cursor[0]
    KCF = place("KCF", [P, NSA_G, 32])
    CPROW = place("CPROW", [32, P], at=kcf_at)
    arena = cursor[0]

    def a_(name, kb, shape, dt=F32):
        size = int(np.prod(shape[1:])) * (2 if dt == BF16 else 4)
        assert arena + kb * 1024 + size <= nc.sbuf_usable_end, (name, (nc.sbuf_usable_end - arena) / 1024)
        return place(name, shape, dt, at=arena + int(kb * 1024))

    PS = ctx.enter_context(nc.psum_tensor("PS", [P, 8, 512], F32))

    C_SC, C_SSM, C_SSMB, C_NG, C_MG2, C_ML2, C_SUB = 0, 24, 72, 84, 92, 100, 108
    C_LMG, C_LMB, C_LFG, C_LFB = 128, 144, 160, 176
    C_FW, C_FB = 256, 520
    B_DTB, B_ALOG, B_D, B_BF = 0, 16, 32, 48
    B_GAIN = {"dq": 64, "dk": 128, "nq": 192, "kc": 256, "ks": 320, "kw": 384}
    B_LAM = 448

    raw_loaded = [sem("raw_loaded0"), sem("raw_loaded1")]
    hi_ready, lo_ready, unit_done = sem("hi_ready"), sem("lo_ready"), sem("unit_done")

    def hi(act, b, U, i, u):
        slot = u % 2
        act.wait_ge(raw_loaded[slot], 16 * ((b + u) // 2 + 2) + 8 * U * i)
        act.wait_ge(unit_done, b + u + 1 + U * i)
        act.activation(WH[:, slot, :], RAW[:, slot, :], ACT.Copy).then_inc(hi_ready, 1)

    def lo(dve, b, U, i, u):
        slot = u % 2
        dve.wait_ge(hi_ready, b + u + 3 + U * i)
        dve.tensor_tensor(WL[:, slot, :], RAW[:, slot, :], WH[:, slot, :], ALU.subtract).then_inc(lo_ready, 1)

    def mm3(pe, o, wh, wl, ah, al, first, last, rhs_is_weight=False):
        if rhs_is_weight:
            pe.matmul(o, ah, wh, start=first, stop=False)
            pe.matmul(o, al, wh, start=False, stop=False)
            return pe.matmul(o, ah, wl, start=False, stop=last)
        pe.matmul(o, wh, ah, start=first, stop=False)
        pe.matmul(o, wh, al, start=False, stop=False)
        return pe.matmul(o, wl, ah, start=False, stop=last)

    def unit_fm(pe, b, U, i, u, o, ah, al):
        slot = u % 2
        pe.wait_ge(lo_ready, b + u + 1 + U * i)
        for k in range(KT):
            last = mm3(pe, o, WH[:, slot, k * P:(k + 1) * P], WL[:, slot, k * P:(k + 1) * P],
                       ah[:, k, :], al[:, k, :], k == 0, k == KT - 1)
        last.then_inc(unit_done, 1)

    def unit_tm(pe, b, U, i, u, banks, k0, before=None):
        slot = u % 2
        pe.wait_ge(lo_ready, b + u + 1 + U * i)
        for k in range(2):
            w = slice(k * 512, (k + 1) * 512)
            for c in range(NC_):
                if k0 + k == 0 and before is not None:
                    before(c)
                last = mm3(pe, banks(c), WH[:, slot, w], WL[:, slot, w],
                           XH[:, k0 + k, c * P:(c + 1) * P], XL[:, k0 + k, c * P:(c + 1) * P],
                           k0 + k == 0, k0 + k == KT - 1, rhs_is_weight=True)
        last.then_inc(unit_done, 1)

    def flat(ap):
        return ap.rearrange("p a b -> p (a b)")

    def rows(w):
        return w.rearrange("(k p) c -> p k c", p=P)

    def fm_src(w, col):
        return lambda i, u: rows(w)[:, :, ds(col(i, u), P)]

    w0 = A["sc_ssm_w_in"][0]
    wf = A["fox_w_in"][0]
    w2 = A["w_in_2"][0]

    def kmajor_src(w, tile0=0):
        def src(i, u):
            return rows(w)[:, tile0:tile0 + w.shape[0] // P, :][:, ds(2 * i, 2), u * 512:(u + 1) * 512] if tile0 == 0 \
                else rows(w)[:, tile0:, :][:, ds(2 * i, 2), u * 512:(u + 1) * 512]
        return src

    def tm_src(w, col0):
        def src(i, u):
            return rows(w)[:, 2 * u:2 * u + 2, ds(col0 + 512 * i, 512)]
        return src

    def ffn_src(l):
        return fm_src(A["ffn_w_up"][l], lambda i, u: 256 * i + (u // 2) * P + (u % 2) * DFF)

    def merge_src(i, u):
        jj, u = u // 4, u % 4
        if u < 2:
            return rows(A[("w_proj_diff_2", "w_proj_nsa_2")[u]][0])[:, :, ds(2 * P * i + jj * P, P)]
        return rows(w2)[:, :, ds(5680 + (u - 2) * DM + jj * P + 2 * P * i, P)]

    STREAM = [
        ("gate", 6, 4, fm_src(w0, lambda i, u: (0, DM, 2 * DM)[u % 3] + 256 * i + (u // 3) * P)),
        ("xbc", 2, 6, fm_src(w0, lambda i, u: 4 * DM + 256 * i + u * P)),
        ("z", 4, 2, tm_src(w0, 3 * DM)),
        ("out0", 2, 8, kmajor_src(A["sc_ssm_w_out"][0])),
        ("up0", 4, FT // 2, ffn_src(0)),
        ("down0", 2, FT // 2, kmajor_src(A["ffn_w_down"][0])),
        ("foxqk", 2, 8, fm_src(wf, lambda i, u: 256 * i + u * P)),
        ("foxv", 4, 2, tm_src(wf, 2 * DM)),
        ("foxout", 2, 4, kmajor_src(A["fox_w_out"][0])),
        ("up1", 4, FT // 2, ffn_src(1)),
        ("down1", 2, FT // 2, kmajor_src(A["ffn_w_down"][1])),
        ("dq", 4, 2, tm_src(w2, 0)),
        ("dk", 4, 2, tm_src(w2, DM)),
        ("dv", 4, 2, tm_src(w2, 2 * DM)),
        ("nq", 4, 2, tm_src(w2, 3 * DM)),
        ("nkv", 4, 3, tm_src(w2, 4 * DM)),
        ("merge", 8, 4, merge_src),
        ("out2", 2, 4, kmajor_src(A["w_out_2"][0])),
        ("mupa", 2, FT2 // 4, fm_src(A["w_mlp_up_2"][0], lambda i, u: 256 * i + u * P)),
        ("mdna", 2, FT2 // 4, kmajor_src(A["w_mlp_down_2"][0])),
        ("mupb", 2, FT2 // 4, fm_src(A["w_mlp_up_2"][0], lambda i, u: DFF2 // 2 + 256 * i + u * P)),
        ("mdnb", 2, FT2 // 4, kmajor_src(A["w_mlp_down_2"][0], FT2 // 2)),
    ]
    first, total = {}, 0
    for name, U, bodies, _ in STREAM:
        first[name] = total
        total += U * bodies
    size = {name: (U, bodies) for name, U, bodies, _ in STREAM}
    final = STREAM[-1][0]

    def ring_step(fn, e, name, i, u):
        U, bodies = size[name]
        if name == final and isinstance(i, int) and U * i + u + 2 >= U * bodies:
            return
        fn(e, first[name], U, i, u)

    def loop(e, name, body, peel=0, peel_last=False):
        U, n = size[name]
        cut = n - 1 if (name == final or peel_last) else n
        for i in range(peel):
            body(i)
        if cut > peel:
            with e.Fori(peel, cut) as i:
                body(i)
        if cut < n and cut >= peel:
            body(n - 1)

    stage_end = sem("stage_end")
    passed = {}

    def barrier(e, key):
        passed[key] = passed.get(key, 0) + 1
        e.drain().then_inc(stage_end, 1)
        e.wait_ge(stage_end, 4 * passed[key])

    XT = a_("XT", 0, [P, NC_, DM])
    PROW = a_("PROW", 16, [P, 5, P])
    SWR = a_("SWR", 20, [P, KT, 80])
    su = sems("su", "x par bc small ident tr ev split zero")
    PARAM_ROWS = [
        (0, C_SC, A["sc_conv_w"].rearrange("a t (n p) -> (a t n) p", p=P), 24),
        (0, C_SSM, A["ssm_conv_w"].rearrange("a t (n p) -> (a t n) p", p=P), 48),
        (0, C_SSMB, A["ssm_conv_b"].rearrange("a (n p) -> (a n) p", p=P), 12),
        (0, C_NG, A["ssm_norm_g"].rearrange("a (n p) -> (a n) p", p=P), 8),
        (0, C_MG2, A["ln_mix_g_2"].rearrange("a (n p) -> (a n) p", p=P), 8),
        (0, C_ML2, A["ln_mlp_g_2"].rearrange("a (n p) -> (a n) p", p=P), 8),
        (0, C_SUB, A["diff_subln_g_2"], 1),
        (1, 0, A["ln_mix_g"].rearrange("a (n p) -> (a n) p", p=P), 16),
        (1, 16, A["ln_mix_b"].rearrange("a (n p) -> (a n) p", p=P), 16),
        (1, 32, A["ln_ffn_g"].rearrange("a (n p) -> (a n) p", p=P), 16),
        (1, 48, A["ln_ffn_b"].rearrange("a (n p) -> (a n) p", p=P), 16),
    ]
    fw = A["ffn_conv_w"].rearrange("a t (n p) -> (a t n) p", p=P)
    PARAM_ROWS += [(2, 0, fw[0:128, :], 128), (3, 0, fw[128:256, :], 128), (4, 0, fw[256:264, :], 8),
                   (4, 8, A["ffn_conv_b"].rearrange("a (n p) -> (a n) p", p=P), 88)]
    ROWS_OF = [109, 64, 128, 128, 96]
    COL_OF = [0, 128, 256, 384, 512]
    nk = A["nsa_k_norm_g_2"][0]
    BCAST = [(B_DTB, A["ssm_dt_bias"], 16), (B_ALOG, A["ssm_a_log"], 16), (B_D, A["ssm_d"], 16),
             (B_BF, A["fox_b_f"], 16), (B_GAIN["dq"], A["diff_q_norm_g_2"], HD),
             (B_GAIN["dk"], A["diff_k_norm_g_2"], HD), (B_GAIN["nq"], A["nsa_q_norm_g_2"], HD),
             (B_GAIN["kc"], nk[0:1, :], HD), (B_GAIN["ks"], nk[1:2, :], HD), (B_GAIN["kw"], nk[2:3, :], HD),
             (B_LAM, A["diff_lambda_q1_2"], HD), (B_LAM + 64, A["diff_lambda_k1_2"], HD),
             (B_LAM + 128, A["diff_lambda_q2_2"], HD), (B_LAM + 192, A["diff_lambda_k2_2"], HD)]

    def setup_dma(act):
        act.dma_start(XT[:, :, :], A["x"][0].rearrange("(c p) f -> p c f", p=P)).then_inc(su.x, 16)
        for g, r, src, n in PARAM_ROWS:
            act.dma_start(PROW[r:r + n, g, :], src).then_inc(su.par, 16)
        for c, src, n in BCAST:
            act.dma_start(BCP[:, c:c + n], src[0, :].partition_broadcast(P)).then_inc(su.bc, 16)
        act.dma_start(SWR[:, :, 0:16], rows(w0)[:, :, 5632:5648]).then_inc(su.small, 16)
        act.dma_start(SWR[:, :, 16:32], rows(wf)[:, :, 3072:3088]).then_inc(su.small, 16)
        act.dma_start(SWR[:, :, 32:80], rows(w2)[:, :, 5632:5680]).then_inc(su.small, 16)

    def setup_pool(pool):
        pool.memset(IDF[:, :], 0.0)
        pool.memset(ONES[:, :], 1.0)
        pool.memset(IDB[:, :], 0.0)
        pool.memset(MROW[:, :], 0.0)
        pool.memset(MCOL[:, :], 0.0)
        pool.memset(EPS[:, 0:1], LN_EPS)
        pool.memset(EPS[:, 1:2], RMS_EPS)
        pool.drain().then_inc(su.zero, 1)
        pool.wait_ge(su.zero, 1)
        for m in (IDF, IDB):
            pool.affine_select(out=m[:, :], in_=m[:, :], compare_op=ALU.not_equal, fill=1.0,
                               base=0, pattern=[[-1, P]], channel_multiplier=1)
        pool.affine_select(out=MROW[:, :], in_=MROW[:, :], compare_op=ALU.is_ge, fill=MASKED,
                           base=0, pattern=[[-1, P]], channel_multiplier=1)
        pool.affine_select(out=MCOL[:, :], in_=MCOL[:, :], compare_op=ALU.is_ge, fill=MASKED,
                           base=0, pattern=[[1, P]], channel_multiplier=-1)
        pool.drain().then_inc(su.ident, 1)

    def setup_pe(pe):
        pe.wait_ge(su.ident, 1)
        pe.wait_ge(su.par, 16 * len(PARAM_ROWS))
        for g in range(5):
            last = pe.transpose(PS[:, g // 4, (g % 4) * P:(g % 4) * P + ROWS_OF[g]], PROW[0:ROWS_OF[g], g, :],
                                IDF[0:ROWS_OF[g], 0:ROWS_OF[g]])
        last.then_inc(su.tr, 1)
        pe.wait_ge(su.x, 16)
        for f in range(KT):
            if f >= 4:
                pe.wait_ge(su.ev, f - 3)
            for c in range(NC_):
                last = pe.transpose(PS[:, 2 + f % 4, c * P:(c + 1) * P], XT[:, c, f * P:(f + 1) * P], IDF[:, :])
            last.then_inc(su.tr, 1)

    def setup_act(act):
        for u in range(2):
            act.wait_ge(raw_loaded[u], 16)
            act.activation(WH[:, u, :], RAW[:, u, :], ACT.Copy).then_inc(hi_ready, 1)
        act.wait_ge(su.small, 48)
        act.activation(SW[0][0][:, :, :], SWR[:, :, 0:32], ACT.Copy)
        act.activation(SW[1][0][:, :, :], SWR[:, :, 32:80], ACT.Copy)
        act.drain().then_inc(su.split, 1)
        for f in range(KT):
            act.wait_ge(su.ev, f + 1)
            act.activation(XH[:, f, :], X[:, f, :], ACT.Copy).then_inc(su.split, 1)

    def setup_dve(dve):
        for u in range(2):
            dve.wait_ge(hi_ready, u + 1)
            dve.tensor_tensor(WL[:, u, :], RAW[:, u, :], WH[:, u, :], ALU.subtract).then_inc(lo_ready, 1)
        dve.wait_ge(su.tr, 1)
        for g in range(5):
            dve.tensor_copy(PCOL[:, COL_OF[g]:COL_OF[g] + ROWS_OF[g]],
                            PS[:, g // 4, (g % 4) * P:(g % 4) * P + ROWS_OF[g]])
        dve.wait_ge(su.split, 1)
        dve.tensor_tensor(SW[0][1][:, :, :], SWR[:, :, 0:32], SW[0][0][:, :, :], ALU.subtract)
        dve.tensor_tensor(SW[1][1][:, :, :], SWR[:, :, 32:80], SW[1][0][:, :, :], ALU.subtract)
        for f in range(KT):
            dve.wait_ge(su.tr, f + 2)
            dve.tensor_copy(X[:, f, :], PS[:, 2 + f % 4, :]).then_inc(su.ev, 1)
        for f in range(KT):
            dve.wait_ge(su.split, f + 2)
            dve.tensor_tensor(XL[:, f, :], X[:, f, :], XH[:, f, :], ALU.subtract)
        dve.wait_ge(su.bc, 16 * len(BCAST))

    YH = a_("YH", 0, [P, 16, SEQ], F32R)
    YL = a_("YL", 32, [P, 16, SEQ], F32R)
    CSB = a_("CSB", 64, [P, 2, SEQ])
    CHP = a_("CHP", 68, [P, 2, SEQ + 8])
    CT = a_("CT", 73, [P, 2, SEQ])
    CY = a_("CY", 77, [P, 2, SEQ])
    ga = sems("ga", "copied y hi lo free")

    def gate_pe(pe):
        def body(i):
            for u in range(6):
                jj = u // 3
                if u % 3 == 0:
                    pe.wait_ge(ga.free, 2 * i + jj + 1)
                unit_fm(pe, first["gate"], 6, i, u, PS[:, 4 * jj + u % 3, :], XH, XL)
        loop(pe, "gate", body)

    def gate_act(act):
        def body(i):
            for u in range(6):
                ring_step(hi, act, "gate", i, u)
                jj = u // 3
                if u % 3 == 1:
                    act.wait_ge(ga.free, 2 * i + jj + 1)
                    act.activation(CSB[:, jj, :], PS[:, 4 * jj + 1, :], ACT.Copy).then_inc(ga.copied, 1)
                if u % 3 == 2:
                    act.wait_ge(ga.y, 2 * i + jj + 1)
                    act.activation(YH[:, ds(2 * i + jj, 1), :], CY[:, jj:jj + 1, :], ACT.Copy).then_inc(ga.hi, 1)
        loop(act, "gate", body)

    def gate_dve(dve):
        dve.memset(CHP[:, :, 0:2], 0.0)
        dve.drain().then_inc(ga.free, 2)

        def body(i):
            for u in range(6):
                ring_step(lo, dve, "gate", i, u)
                jj = u // 3
                if u % 3 != 2:
                    continue
                j = 2 * i + jj
                ch = CHP[:, jj, 2:2 + SEQ]
                dve.wait_ge(ga.copied, j + 1)
                dve.wait_ge(unit_done, first["gate"] + 6 * i + u + 1)
                dve.tensor_tensor(ch, CSB[:, jj, :], PS[:, 4 * jj + 2, :], ALU.mult)
                dve.drain()
                tap = [PCOL[:, ds(C_SC + 8 * t + j, 1)] for t in range(3)]
                dve.tensor_scalar(CT[:, jj, :], CHP[:, jj, 0:SEQ], tap[0], None, ALU.mult)
                dve.drain()
                for t in (1, 2):
                    dve.scalar_tensor_tensor(out=CT[:, jj, :], in0=CHP[:, jj, t:t + SEQ], scalar=tap[t],
                                             in1=CT[:, jj, :], op0=ALU.mult, op1=ALU.add)
                    dve.drain()
                dve.tensor_tensor(CY[:, jj, :], CT[:, jj, :], PS[:, 4 * jj, :], ALU.mult).then_inc(ga.y, 1)
                dve.wait_ge(ga.hi, j + 1)
                dve.tensor_tensor(YL[:, ds(j, 1), :], CY[:, jj:jj + 1, :], YH[:, ds(j, 1), :],
                                  ALU.subtract)
                dve.drain().then_inc(ga.free, 1)
        loop(dve, "gate", body)

    XSF = a_("XSF", 16, [P, 8, SEQ])
    BF = a_("BF", 80, [P, 2, SEQ])
    CF = a_("CF", 96, [P, 2, SEQ])
    XP = a_("XP", 64, [P, 2, SEQ + 8])
    XQ = a_("XQ", 69, [P, 2, SEQ])
    xb = sems("xb", "copied conv free")

    def xbc_dst(i, u):
        if isinstance(i, int):
            if i == 4:
                return BF[:, u:u + 1, :]
            if i == 5:
                return CF[:, u:u + 1, :]
        return XSF[:, ds(2 * i + u, 1), :]

    def xbc_loop(e, body):
        with e.Fori(0, 4) as i:
            body(i)
        body(4)
        body(5)

    def xbc_pe(pe):
        def body(i):
            for u in range(2):
                pe.wait_ge(xb.copied, 2 * i + u + 1)
                unit_fm(pe, first["xbc"], 2, i, u, PS[:, u, :], XH, XL)
        xbc_loop(pe, body)

    def xbc_act(act):
        act.drain().then_inc(xb.copied, 2)
        act.drain().then_inc(xb.free, 2)

        def body(i):
            for u in range(2):
                hi(act, first["xbc"], 2, i, u)
                act.wait_ge(xb.conv, 2 * i + u + 1)
                act.activation(XP[:, u, 3:3 + SEQ], PS[:, u, :], ACT.Copy).then_inc(xb.copied, 1)
                act.wait_ge(xb.conv, 2 * i + u + 3)
                act.activation(xbc_dst(i, u), XQ[:, u:u + 1, :], ACT.Silu).then_inc(xb.free, 1)
        xbc_loop(act, body)

    def xbc_dve(dve):
        dve.memset(XP[:, :, 0:3], 0.0)
        dve.drain().then_inc(xb.conv, 2)
        dve.drain()

        def body(i):
            for u in range(2):
                lo(dve, first["xbc"], 2, i, u)
                j = 2 * i + u
                dve.wait_ge(xb.copied, j + 3)
                dve.wait_ge(xb.free, j + 1)
                tap = [PCOL[:, ds(C_SSM + 12 * t + j, 1)] for t in range(4)]
                dve.tensor_scalar(XQ[:, u, :], XP[:, u, 0:SEQ], tap[0], PCOL[:, ds(C_SSMB + j, 1)],
                                  ALU.mult, ALU.add)
                dve.drain()
                for t in (1, 2, 3):
                    last = dve.scalar_tensor_tensor(out=XQ[:, u, :], in0=XP[:, u, t:t + SEQ], scalar=tap[t],
                                                    in1=XQ[:, u, :], op0=ALU.mult, op1=ALU.add)
                    if t < 3:
                        dve.drain()
                last.then_inc(xb.conv, 1)
        xbc_loop(dve, body)

    LT = a_("LT", 104, [P, 7, SEQ])

    norm_s = shared("norm", "res sum cent sq ssq std tmp hi")

    def norm_turn():
        return turn(norm_s, res=KT, sum=1, cent=KT, sq=KT, ssq=KT, std=1, tmp=KT, hi=KT)

    def ln_pe(pe, s):
        for m in range(KT):
            pe.wait_ge(s.res, s.at.res + m + 1)
            last = pe.matmul(PS[:, 0, :], ONES[:, :], X[:, m, :], start=m == 0, stop=m == KT - 1)
        last.then_inc(s.sum, 1)
        ssq_pe(pe, s)

    def ssq_pe(pe, s):
        for m in range(KT):
            pe.wait_ge(s.sq, s.at.sq + m + 1)
            pe.matmul(PS[:, 1, :], ONES[:, :], LT[:, m % 2, :], start=m == 0, stop=m == KT - 1).then_inc(s.ssq, 1)

    def square_act(act, s):
        for m in range(KT):
            act.wait_ge(s.cent, s.at.cent + m + 1)
            if m >= 2:
                act.wait_ge(s.ssq, s.at.ssq + m - 1)
            act.activation(LT[:, m % 2, :], X[:, m, :], ACT.Square).then_inc(s.sq, 1)

    def ln_act(act, s, g, b):
        square_act(act, s)
        act.wait_ge(s.ssq, s.at.ssq + KT)
        act.activation(LT[:, 3, :], PS[:, 1, :], ACT.Sqrt, bias=EPS[:, 0:1], scale=1.0 / DM).then_inc(s.std, 1)
        for m in range(KT):
            act.wait_ge(s.tmp, s.at.tmp + m + 1)
            act.activation(XH[:, m, :], LT[:, 5 + m % 2, :], ACT.Identity, bias=PCOL[:, b + m:b + m + 1],
                           scale=PCOL[:, g + m:g + m + 1]).then_inc(s.hi, 1)

    def ln_dve(dve, s, g, b):
        for m in range(KT):
            dve.scalar_tensor_tensor(out=X[:, m, :], in0=X[:, m, :], scalar=ALPHA, in1=PS[:, m, :],
                                     op0=ALU.mult, op1=ALU.add).then_inc(s.res, 1)
        dve.wait_ge(s.sum, s.at.sum + 1)
        dve.tensor_scalar(LT[:, 2, :], PS[:, 0, :], 1.0 / DM, None, ALU.mult)
        dve.drain()
        for m in range(KT):
            dve.tensor_tensor(X[:, m, :], X[:, m, :], LT[:, 2, :], ALU.subtract).then_inc(s.cent, 1)
        dve.wait_ge(s.std, s.at.std + 1)
        dve.reciprocal(LT[:, 4, :], LT[:, 3, :])
        dve.drain()
        for m in range(KT):
            if m >= 2:
                dve.wait_ge(s.hi, s.at.hi + m - 1)
            dve.tensor_tensor(LT[:, 5 + m % 2, :], X[:, m, :], LT[:, 4, :], ALU.mult).then_inc(s.tmp, 1)
            dve.drain()
            dve.tensor_scalar(X[:, m, :], LT[:, 5 + m % 2, :], PCOL[:, g + m:g + m + 1], PCOL[:, b + m:b + m + 1],
                              ALU.mult, ALU.add)
            dve.drain()
            dve.wait_ge(s.hi, s.at.hi + m + 1)
            dve.tensor_tensor(XL[:, m, :], X[:, m, :], XH[:, m, :], ALU.subtract)

    def rms_act(act, s, g):
        square_act(act, s)
        act.wait_ge(s.ssq, s.at.ssq + KT)
        act.activation(LT[:, 3, :], PS[:, 1, :], ACT.Sqrt, bias=EPS[:, 1:2], scale=1.0 / DM).then_inc(s.std, 1)
        for m in range(KT):
            act.wait_ge(s.tmp, s.at.tmp + m + 1)
            act.activation(XH[:, m, :], LT[:, 5 + m % 2, :], ACT.Copy,
                           scale=PCOL[:, g + m:g + m + 1]).then_inc(s.hi, 1)

    def rms_dve(dve, s, g, residual):
        for m in range(KT):
            if residual:
                dve.tensor_tensor(X[:, m, :], X[:, m, :], PS[:, m, :], ALU.add)
        dve.drain().then_inc(s.cent, KT)
        dve.wait_ge(s.std, s.at.std + 1)
        dve.reciprocal(LT[:, 4, :], LT[:, 3, :])
        dve.drain()
        for m in range(KT):
            if m >= 2:
                dve.wait_ge(s.hi, s.at.hi + m - 1)
            dve.tensor_tensor(LT[:, 5 + m % 2, :], X[:, m, :], LT[:, 4, :], ALU.mult).then_inc(s.tmp, 1)
            dve.drain()
            dve.wait_ge(s.hi, s.at.hi + m + 1)
            dve.scalar_tensor_tensor(out=XL[:, m, :], in0=LT[:, 5 + m % 2, :], scalar=PCOL[:, g + m:g + m + 1],
                                     in1=XH[:, m, :], op0=ALU.mult, op1=ALU.subtract)

    def kmajor_pe(pe, name, ah, al):
        U, n = size[name]

        def body(i):
            for u in range(2):
                slot = u % 2
                pe.wait_ge(lo_ready, first[name] + u + 1 + 2 * i)
                for k in range(2):
                    for m in range(4):
                        w = slice(k * 512 + m * P, k * 512 + (m + 1) * P)
                        a = (flat(ah[:, ds(2 * i + k, 1), :]), flat(al[:, ds(2 * i + k, 1), :]))
                        begin = isinstance(i, int) and i == 0 and k == 0
                        end = isinstance(i, int) and i == n - 1 and k == 1
                        last = mm3(pe, PS[:, 4 * u + m, :], WH[:, slot, w], WL[:, slot, w], *a, begin, end)
                last.then_inc(unit_done, 1)
        loop(pe, name, body, peel=1, peel_last=True)

    def split_only(fn, e, name):
        def body(i):
            for u in range(size[name][0]):
                ring_step(fn, e, name, i, u)
        loop(e, name, body)

    FH = a_("FH", 0, [P, FT, SEQ], F32R)
    FL = a_("FL", 44, [P, FT, SEQ], F32R)
    UP = a_("UP", 88, [P, 4, SEQ + 8])
    UT = a_("UT", 97, [P, 4, SEQ])
    FY = a_("FY", 105, [P, 2, SEQ])

    ffn_s = shared("ffn", "copied conv silu y hi")

    def ffn_turn():
        return turn(ffn_s, copied=4 + 2 * FT, conv=4 + 2 * FT, silu=2 + FT, y=FT, hi=2 + FT)

    def ffn_up_pe(pe, l, s):
        name = f"up{l}"

        def body(i):
            for u in range(4):
                pe.wait_ge(s.copied, s.at.copied + 4 * i + u + 1)
                unit_fm(pe, first[name], 4, i, u, PS[:, u, :], XH, XL)
        loop(pe, name, body)

    def ffn_up_act(act, l, s):
        name = f"up{l}"
        act.drain().then_inc(s.copied, 4)
        act.drain().then_inc(s.silu, 2)
        act.drain().then_inc(s.hi, 2)

        def body(i):
            for u in range(4):
                ring_step(hi, act, name, i, u)
                act.wait_ge(s.conv, s.at.conv + 4 * i + u + 1)
                act.activation(UP[:, u, 2:2 + SEQ], PS[:, u, :], ACT.Copy).then_inc(s.copied, 1)
                if u % 2:
                    jj = u // 2
                    act.wait_ge(s.conv, s.at.conv + 4 * i + u + 5)
                    act.activation(UT[:, u, :], UT[:, u, :], ACT.Silu).then_inc(s.silu, 1)
                    act.wait_ge(s.y, s.at.y + 2 * i + jj + 1)
                    act.activation(FH[:, ds(2 * i + jj, 1), :], FY[:, jj:jj + 1, :], ACT.Copy).then_inc(s.hi, 1)
        loop(act, name, body)

    def ffn_up_dve(dve, l, s):
        name = f"up{l}"
        dve.memset(UP[:, :, 0:2], 0.0)
        dve.drain().then_inc(s.conv, 4)

        def body(i):
            for u in range(4):
                ring_step(lo, dve, name, i, u)
                jj = u // 2
                j = 2 * i + jj
                col = C_FW + l * 132 + (u % 2) * FT + j
                dve.wait_ge(s.copied, s.at.copied + 4 * i + u + 5)
                tap = [PCOL[:, ds(col + 44 * t, 1)] for t in range(3)]
                bias = PCOL[:, ds(C_FB + l * 44 + (u % 2) * FT + j, 1)]
                dve.tensor_scalar(UT[:, u, :], UP[:, u, 0:SEQ], tap[0], bias, ALU.mult, ALU.add)
                dve.drain()
                dve.scalar_tensor_tensor(out=UT[:, u, :], in0=UP[:, u, 1:1 + SEQ], scalar=tap[1],
                                         in1=UT[:, u, :], op0=ALU.mult, op1=ALU.add)
                dve.drain()
                dve.scalar_tensor_tensor(out=UT[:, u, :], in0=UP[:, u, 2:2 + SEQ], scalar=tap[2],
                                         in1=UT[:, u, :], op0=ALU.mult, op1=ALU.add).then_inc(s.conv, 1)
                if u % 2:
                    dve.wait_ge(s.silu, s.at.silu + j + 3)
                    dve.tensor_tensor(FY[:, jj, :], UT[:, u - 1, :], UT[:, u, :], ALU.mult).then_inc(s.y, 1)
                    dve.wait_ge(s.hi, s.at.hi + j + 3)
                    dve.tensor_tensor(FL[:, ds(j, 1), :], FY[:, jj:jj + 1, :], FH[:, ds(j, 1), :], ALU.subtract)
                    dve.drain()
        loop(dve, name, body)


    XS = a_("XS", 64, [P, NC_, DM])
    YB = a_("YB", 80, [P, NC_, DM])
    BT = a_("BT", 100, [P, NC_, GROUPS * STATE])
    XDT = a_("XDT", 104, [P, NC_, DM])
    XDEC = a_("XDEC", 16, [P, NC_, DM])
    EM = a_("EM", 48, [P, 2, SEQ])
    CBT = a_("CBT", 52, [P, GROUPS, SEQ])
    HS = a_("HS", 56, [P, DM])
    ACST = a_("ACST", 60, [HEADS, SEQ])
    SELB = a_("SELB", 62, [HEADS, 2, P])
    Z = a_("Z", 16, [P, NC_, DM])
    t64 = [TINY[:, 64 * k:64 * (k + 1)] for k in range(8)]

    def heads4(ap):
        return ap.rearrange("p (c h) -> p c h", c=NC_)

    def small_gemm_pe(pe, bank, sw, c0, c1):
        n = c1 - c0
        for c in range(NC_):
            for k in range(KT):
                last = mm3(pe, PS[:, bank, c * n:(c + 1) * n], sw[0][:, k, c0:c1], sw[1][:, k, c0:c1],
                           XH[:, k, c * P:(c + 1) * P], XL[:, k, c * P:(c + 1) * P], k == 0, k == KT - 1,
                           rhs_is_weight=True)
        return last

    def softplus_dve_b(dve, v, e, w, r, q):
        dve.tensor_scalar(w, e, 1.0, None, ALU.add)
        dve.drain()
        dve.tensor_scalar(r, w, -1.0, None, ALU.add)
        dve.reciprocal(q, w)
        dve.drain()
        dve.tensor_tensor(r, e, r, ALU.subtract)
        dve.drain()
        dve.tensor_tensor(r, r, q, ALU.mult)
        dve.drain()
        dve.tensor_scalar(q, v, 0.0, None, ALU.max)
        dve.drain()
        dve.tensor_tensor(r, r, q, ALU.add)

    sd = sems("sd", "tr ev dt e w ln dta t1 scan t2 tot acs exps cb xdec st h yo ydone")
    V_, E_, W_, R_, Q_, LN_, DTA, DTV = t64
    DEC = a_("DEC", 63, [P, 4, 64])

    def ssd_pe(pe):
        small_gemm_pe(pe, 4, SW[0], 0, 16).then_inc(sd.dt, 1)
        pe.wait_ge(sd.dta, 1)
        for c in range(NC_):
            last = pe.transpose(PS[0:16, 5, c * P:(c + 1) * P], DTA[:, c * 16:(c + 1) * 16], IDF[:, :])
        last.then_inc(sd.t1, 1)
        pe.matmul(PS[:, 7, 0:64], ONES[:, :], DTA, start=True, stop=True).then_inc(sd.tot, 1)
        for j in range(10):
            if j >= 4:
                pe.wait_ge(sd.ev, j - 3)
            for c in range(NC_):
                src = XSF[:, j, c * P:(c + 1) * P] if j < 8 else BF[:, j - 8, c * P:(c + 1) * P]
                last = pe.transpose(PS[:, j % 4, c * P:(c + 1) * P], src, IDF[:, :])
            last.then_inc(sd.tr, 1)
        pe.wait_ge(sd.scan, 1)
        for c in range(NC_):
            last = pe.transpose(PS[:, 6, c * 16:(c + 1) * 16], ACST[0:16, c * P:(c + 1) * P], IDF[0:16, 0:16])
        last.then_inc(sd.t2, 1)
        pe.wait_ge(sd.ev, 10)
        for g in range(GROUPS):
            for c in range(NC_):
                last = pe.matmul(PS[:, g, c * P:(c + 1) * P], BF[:, g, c * P:(c + 1) * P],
                                 CF[:, g, c * P:(c + 1) * P], start=True, stop=True)
        last.then_inc(sd.cb, 1)
        pe.wait_ge(sd.xdec, 1)
        for c in range(NC_):
            if c < NC_ - 1:
                if c:
                    pe.wait_ge(sd.h, c)
                for g in range(GROUPS):
                    last = pe.matmul(PS[:, 2 + g, :], BT[:, c, g * STATE:(g + 1) * STATE],
                                     XDEC[:, c, g * 512:(g + 1) * 512], start=True, stop=True)
                last.then_inc(sd.st, 1)
            if c:
                pe.wait_ge(sd.h, c)
                if c > 1:
                    pe.wait_ge(sd.ydone, c)
                for g in range(GROUPS):
                    last = pe.matmul(PS[:, 4 + g, :], CF[:, g, c * P:(c + 1) * P],
                                     HS[:, g * 512:(g + 1) * 512], start=True, stop=True)
                last.then_inc(sd.yo, 1)

    def ssd_act(act):
        act.wait_ge(sd.e, 1)
        act.activation(E_, V_, ACT.Abs)
        act.drain()
        act.activation(E_, E_, ACT.Exp, scale=-1.0)
        act.activation(BCP[:, 752:768], BCP[:, B_ALOG:B_ALOG + 16], ACT.Exp)
        act.drain().then_inc(sd.w, 1)
        act.wait_ge(sd.ln, 1)
        act.activation(LN_, W_, ACT.Ln).then_inc(sd.ln, 1)
        act.wait_ge(sd.acs, 1)
        for k in range(3):
            last = act.activation(DEC[:, k, :], DEC[:, k, :], ACT.Exp)
        last.then_inc(sd.exps, 1)

    def ssd_dve(dve):
        dve.wait_ge(sd.dt, 1)
        dve.tensor_tensor(heads4(V_), heads4(PS[:, 4, 0:64]),
                          BCP[:, B_DTB:B_DTB + 16].unsqueeze(1).to_broadcast([P, NC_, 16]), ALU.add)
        dve.drain()
        dve.drain().then_inc(sd.e, 1)
        dve.wait_ge(sd.w, 1)
        dve.tensor_copy(BCP[:, B_ALOG:B_ALOG + 16], BCP[:, 752:768])
        softplus_dve_b(dve, V_, E_, W_, R_, Q_)
        dve.drain().then_inc(sd.ln, 1)
        dve.wait_ge(sd.ln, 2)
        dve.tensor_tensor(DTV, R_, LN_, ALU.add)
        dve.drain()
        dve.scalar_tensor_tensor(out=heads4(DTA), in0=heads4(DTV), scalar=-1.0,
                                 in1=BCP[:, B_ALOG:B_ALOG + 16].unsqueeze(1).to_broadcast([P, NC_, 16]),
                                 op0=ALU.mult, op1=ALU.mult)
        dve.drain().then_inc(sd.dta, 1)
        dve.wait_ge(sd.t1, 1)
        for c in range(NC_):
            dve.tensor_tensor_scan(ACST[0:16, c * P:(c + 1) * P], ONES[0:16, :], PS[0:16, 5, c * P:(c + 1) * P],
                                   0.0, ALU.mult, ALU.add)
        dve.drain().then_inc(sd.scan, 1)
        for j in range(10):
            dve.wait_ge(sd.tr, j + 1)
            dst = XS[:, :, j * P:(j + 1) * P] if j < 8 else BT[:, :, (j - 8) * P:(j - 7) * P]
            dve.tensor_copy(dst, PS[:, j % 4, :].rearrange("p (c t) -> p c t", c=NC_)).then_inc(sd.ev, 1)
        dve.wait_ge(sd.t2, 1)
        dve.wait_ge(sd.tot, 1)
        dve.tensor_copy(DEC[:, 2, :], PS[:, 6, 0:64])
        dve.tensor_copy(DEC[:, 1, :], PS[:, 7, 0:64])
        dve.drain()
        dve.tensor_scalar(DEC[:, 3, :], DEC[:, 2, :], -1.0, None, ALU.mult)
        dve.tensor_tensor(DEC[:, 0, :], DEC[:, 1, :], DEC[:, 2, :], ALU.subtract)
        dve.drain().then_inc(sd.acs, 1)

        def per_head(ap):
            return ap.unsqueeze(2).to_broadcast([P, HEADS, HD])

        def by_head(ap):
            return ap.rearrange("p (h d) -> p h d", h=HEADS)

        for c in range(NC_):
            dve.tensor_tensor(by_head(XDT[:, c, :]), by_head(XS[:, c, :]), per_head(DTV[:, c * 16:(c + 1) * 16]),
                              ALU.mult)
        dve.wait_ge(sd.exps, 1)
        dve.wait_ge(sd.cb, 1)
        for g in range(GROUPS):
            dve.tensor_copy(CBT[:, g, :], PS[:, g, :])
        dve.drain()
        for c in range(NC_):
            dve.tensor_tensor(by_head(XDEC[:, c, :]), by_head(XDT[:, c, :]),
                              per_head(DEC[:, 0, c * 16:(c + 1) * 16]), ALU.mult)
            dve.tensor_tensor(by_head(YB[:, c, :]), by_head(XS[:, c, :]), per_head(BCP[:, B_D:B_D + 16]), ALU.mult)
        dve.drain().then_inc(sd.xdec, 1)
        for c in range(NC_):
            if c:
                dve.wait_ge(sd.yo, c)
                for g in range(GROUPS):
                    half = XS[:, c, g * 512:(g + 1) * 512]
                    dve.tensor_tensor(half.rearrange("p (h d) -> p h d", h=8),
                                      PS[:, 4 + g, :].rearrange("p (h d) -> p h d", h=8),
                                      DEC[:, 2, c * 16 + 8 * g:c * 16 + 8 * g + 8].unsqueeze(2)
                                      .to_broadcast([P, 8, HD]), ALU.mult)
                dve.drain().then_inc(sd.ydone, 2 if c == 1 else 1)
                dve.tensor_tensor(YB[:, c, :], YB[:, c, :], XS[:, c, :], ALU.add)
            if c < NC_ - 1:
                dve.wait_ge(sd.st, c + 1)
                new = PS[:, 2:4, :].rearrange("p a b -> p (a b)")
                if c == 0:
                    dve.tensor_copy(HS[:, :], new)
                else:
                    dve.tensor_tensor(by_head(HS[:, :]), by_head(HS[:, :]),
                                      per_head(DEC[:, 1, c * 16:(c + 1) * 16]), ALU.mult)
                    dve.drain()
                    dve.tensor_tensor(HS[:, :], HS[:, :], new, ALU.add)
                dve.drain().then_inc(sd.h, 1)

    sh = sems("sh", "sel bc e m y yd")

    def ssdh_pe(pe):
        with pe.Fori(0, GROUPS) as g:
            for i in range(4):
                n = 8 * g + 2 * i
                for hh in range(2):
                    pe.wait_ge(sh.sel, n + hh + 1)
                    pe.wait_ge(sh.e, n + hh + 1)
                    pe.matmul(PS[:, hh, :], SELB[:, hh, :], ACST[:, :], start=True, stop=False)
                    for c in range(NC_):
                        last = pe.matmul(PS[:, hh, c * P:(c + 1) * P], IDB[:, :], MCOL[:, :], start=False,
                                         stop=c == NC_ - 1)
                    last.then_inc(sh.bc, 1)

                def free(c):
                    pe.wait_ge(zs.left, zs.at.left + 4 * g + c + 1)
                unit_tm(pe, first["z"], 4, g, i, lambda c: PS[:, 4 + c, :], 2 * i, free)
                for hh in range(2):
                    pe.wait_ge(sh.m, n + hh + 1)
                    pe.wait_ge(sh.yd, n + hh + 1)
                    for c in range(NC_):
                        last = pe.matmul(PS[:, 2 + hh, c * HD:(c + 1) * HD], EM[:, hh, c * P:(c + 1) * P],
                                         XDT[:, c, ds((n + hh) * HD, HD)], start=True, stop=True)
                    last.then_inc(sh.y, 1)

    def ssdh_act(act):
        act.drain().then_inc(sh.e, 2)
        act.drain().then_inc(zs.left, 4)
        with act.Fori(0, GROUPS) as g:
            for i in range(4):
                n = 8 * g + 2 * i
                for hh in range(2):
                    act.wait_ge(sh.bc, n + hh + 1)
                    act.wait_ge(sh.yd, n + hh + 1)
                    for c in range(NC_):
                        last = act.activation(EM[:, hh, c * P:(c + 1) * P], PS[:, hh, c * P:(c + 1) * P], ACT.Exp,
                                              bias=DEC[:, 3, ds(c * 16 + n + hh, 1)])
                    last.then_inc(sh.e, 1)
                hi(act, first["z"], 4, g, i)
            act.wait_ge(unit_done, first["z"] + 4 * g + 4)
            for c in range(NC_):
                act.activation(Z[:, c, ds(512 * g, 512)], PS[:, 4 + c, :], ACT.Silu).then_inc(zs.left, 1)

    def ssdh_dve(dve):
        dve.drain().then_inc(sh.yd, 2)
        with dve.Fori(0, GROUPS) as g:
            for i in range(4):
                n = 8 * g + 2 * i
                for hh in range(2):
                    dve.tensor_copy(SELB[:, hh, :],
                                    IDF[0:16, ds(n + hh, 1)].to_broadcast([HEADS, P])).then_inc(sh.sel, 1)
                for hh in range(2):
                    dve.wait_ge(sh.e, n + hh + 3)
                    dve.tensor_tensor(EM[:, hh:hh + 1, :], EM[:, hh:hh + 1, :], CBT[:, ds(g, 1), :],
                                      ALU.mult).then_inc(sh.m, 1)
                lo(dve, first["z"], 4, g, i)
                for hh in range(2):
                    dve.wait_ge(sh.y, n + hh + 1)
                    y = YB[:, :, ds((n + hh) * HD, HD)]
                    dve.tensor_tensor(y, y, PS[:, 2 + hh, 0:256].rearrange("p (c d) -> p c d", c=NC_),
                                      ALU.add)
                    dve.drain().then_inc(sh.yd, 1)

    def tm_pe(pe, name, s, groups_before=0):
        def body(i):
            def free(c):
                pe.wait_ge(s.left, s.at.left + 4 * (i + groups_before) + c + 1)
            for u in range(4):
                unit_tm(pe, first[name], 4, i, u, lambda c: PS[:, c, :], 2 * u, free)
        loop(pe, name, body)

    def tm_act(act, name, s, dst, func=ACT.Copy, credit=True):
        if credit:
            act.drain().then_inc(s.left, 4)

        def body(i):
            for u in range(4):
                ring_step(hi, act, name, i, u)
            act.wait_ge(unit_done, first[name] + 4 * i + 4)
            for c in range(NC_):
                act.activation(dst(i, c), PS[:, c, :], func).then_inc(s.left, 1)
        loop(act, name, body)

    left_s = shared("left", "left")
    zs = turn(left_s, left=4 + 8)
    gn = sems("gn", "u ss std n tr hi lo")

    def gnorm_pe(pe):
        for f in range(KT):
            pe.wait_ge(gn.n, f // 4 + 1)
            if f >= 4:
                pe.wait_ge(gn.lo, f - 3)
            for c in range(NC_):
                last = pe.transpose(PS[:, f % 4, c * P:(c + 1) * P], YB[:, c, f * P:(f + 1) * P], IDF[:, :])
            last.then_inc(gn.tr, 1)

    def gnorm_act(act):
        for g in range(GROUPS):
            for c in range(NC_):
                act.wait_ge(gn.u, g * NC_ + c + 1)
                act.activation(XS[:, c, g * 512:(g + 1) * 512], YB[:, c, g * 512:(g + 1) * 512], ACT.Square,
                               accum_out=TINY[:, g * NC_ + c:g * NC_ + c + 1])
        act.drain()
        act.activation(TINY[:, 8:16], TINY[:, 0:8], ACT.Sqrt, bias=EPS[:, 0:1], scale=1.0 / 512).then_inc(gn.std, 1)
        for f in range(KT):
            act.wait_ge(gn.tr, f + 1)
            act.activation(YH[:, 8 + f, :], PS[:, f % 4, :], ACT.Copy,
                           scale=PCOL[:, C_NG + f:C_NG + f + 1]).then_inc(gn.hi, 1)

    def gnorm_dve(dve):
        for g in range(GROUPS):
            for c in range(NC_):
                seg = YB[:, c, g * 512:(g + 1) * 512]
                dve.tensor_tensor(seg, seg, Z[:, c, g * 512:(g + 1) * 512], ALU.mult).then_inc(gn.u, 1)
        dve.wait_ge(gn.std, 1)
        dve.reciprocal(TINY[:, 16:24], TINY[:, 8:16])
        dve.drain()
        for g in range(GROUPS):
            for c in range(NC_):
                seg = YB[:, c, g * 512:(g + 1) * 512]
                dve.tensor_scalar(seg, seg, TINY[:, 16 + g * NC_ + c:17 + g * NC_ + c], None, ALU.mult)
            dve.drain().then_inc(gn.n, 1)
        for f in range(KT):
            dve.wait_ge(gn.hi, f + 1)
            dve.scalar_tensor_tensor(out=YL[:, 8 + f, :], in0=PS[:, f % 4, :], scalar=PCOL[:, C_NG + f:C_NG + f + 1],
                                     in1=YH[:, 8 + f, :], op0=ALU.mult, op1=ALU.subtract).then_inc(gn.lo, 1)

    def fm_pe(pe, name, s):
        def body(i):
            for u in range(2):
                pe.wait_ge(s.left, s.at.left + 2 * i + u + 1)
                unit_fm(pe, first[name], 2, i, u, PS[:, u, :], XH, XL)
        loop(pe, name, body)

    attn_s = shared("attn", "qz sc mx ex cb tr pt pv ov")
    NP = 4
    LAG = 3

    def attn_turn(loops, n, slots):
        m = loops * n
        return turn(attn_s, qz=loops, sc=m, mx=m, ex=m + slots, tr=m, pt=m, pv=m + 2, ov=m // NC_ + 2)

    def scores_pe(pe, bank, q, k, qb):
        n = (qb + 1) * P
        pe.matmul(PS[:, bank, 0:n], q, k(n), start=True, stop=False)
        return pe.matmul(PS[:, bank, qb * P:n], IDB[:, :], MROW[:, :], start=False, stop=True)

    def attn_pe(pe, s, loops, n, slots, scores, pblock, PTx, value, ready, width):
        pe.drain().then_inc(s.pv, 2)
        with pe.Fori(0, loops) as i:
            B = i * n
            pe.wait_ge(s.qz, s.at.qz + i + 1)
            for t in range(n + LAG + 1):
                if t < n:
                    if slots <= LAG:
                        pe.wait_ge(s.ex, s.at.ex + B + t + 1)
                    scores(i, t).then_inc(s.sc, 1)
                if LAG <= t < n + LAG:
                    k = t - LAG
                    pe.wait_ge(ready[0], ready[1] + B + k)
                    for b in range(k % 4 + 1):
                        last = pe.transpose(PS[:, 4 + k % 2, b * P:(b + 1) * P], pblock(k, b), IDF[:, :])
                    last.then_inc(s.tr, 1)
                if t > LAG:
                    k = t - LAG - 1
                    pe.wait_ge(s.pt, s.at.pt + B + k + 1)
                    if k % NC_ == 0:
                        pe.wait_ge(s.ov, s.at.ov + (n // NC_) * i + k // NC_ + 1)
                    o = slice((k % NC_) * width, (k % NC_ + 1) * width)
                    for b in range(k % 4 + 1):
                        last = pe.matmul(PS[:, 6 + k // NC_ % 2, o], PTx[:, k % 2, b * P:(b + 1) * P], value(i, k, b),
                                         start=b == 0, stop=b == k % 4)
                    last.then_inc(s.pv, 1)

    def attn_act(act, s, loops, n, slots, queries, exps, PTx):
        act.drain().then_inc(s.ex, slots)
        with act.Fori(0, loops) as i:
            B = i * n
            queries(i).then_inc(s.qz, 1)
            for t in range(n + LAG):
                if t >= LAG:
                    k = t - LAG
                    act.wait_ge(s.tr, s.at.tr + B + k + 1)
                    act.wait_ge(s.pv, s.at.pv + B + k + 1)
                    w = (k % 4 + 1) * P
                    act.activation(PTx[:, k % 2, 0:w], PS[:, 4 + k % 2, 0:w], ACT.Copy).then_inc(s.pt, 1)
                if t < n:
                    act.wait_ge(s.mx, s.at.mx + B + t + 1)
                    exps(t).then_inc(s.ex, 1)

    def attn_dve(dve, s, loops, n, maxima, output, combine=None):
        dve.drain().then_inc(s.ov, 2)
        with dve.Fori(0, loops) as i:
            B = i * n
            for t in range(n + LAG + 2):
                if t < n:
                    dve.wait_ge(s.sc, s.at.sc + B + t + 1)
                    maxima(t).then_inc(s.mx, 1)
                if combine is not None and 1 <= t <= n:
                    combine(B, t - 1).then_inc(s.cb, 1)
                k = t - LAG - 2
                if k >= 0 and k % NC_ == NC_ - 1:
                    dve.wait_ge(s.pv, s.at.pv + B + k + 3)
                    output(i, k // NC_).then_inc(s.ov, 1)

    def one_softmax(act, dve, PBx):
        def exps(t):
            w = (t % 4 + 1) * P
            return act.activation(PBx(t, 0, w), PS[:, t % 4, 0:w], ACT.Exp, bias=NM[:, t % 4:t % 4 + 1],
                                  accum_out=RS[:, t % 16:t % 16 + 1])

        def maxima(t):
            w = (t % 4 + 1) * P
            return dve.tensor_reduce(NM[:, t % 4:t % 4 + 1], PS[:, t % 4, 0:w], AX, ALU.max, negate=True)
        return exps, maxima

    KZ = a_("KZ", 0, [P, HEADS, SEQ])
    VT = a_("VT", 32, [P, NC_, DM])
    OB = a_("OB", 48, [P, NC_, DM])
    QT = a_("QT", 64, [P, KT, SEQ])
    QZ = a_("QZ", 80, [P, 4, SEQ])
    PB = a_("PB", 88, [P, NP, SEQ])
    PT = a_("PT", 96, [P, 2, SEQ])
    NCUM = a_("NCUM", 100, [HEADS, SEQ])
    ONE16 = a_("ONE16", 102, [HEADS, SEQ])
    fq = turn(left_s, left=2 + 16)
    fv = turn(left_s, left=4 + 8)
    fg = sems("fg", "f w ln sp t1 cum row")
    fa = attn_turn(4, 16, 4)

    def foxqk_act(act):
        act.drain().then_inc(fq.left, 2)

        def step(i, u):
            ring_step(hi, act, "foxqk", i, u)
            act.wait_ge(unit_done, first["foxqk"] + 2 * i + u + 1)
        with act.Fori(0, 4) as i:
            for u in range(2):
                step(i, u)
                act.activation(QT[:, ds(2 * i + u, 1), :], PS[:, u:u + 1, :], ACT.Copy,
                               scale=SCALE).then_inc(fq.left, 1)
        with act.Fori(4, 8) as i:
            for u in range(2):
                step(i, u)
                for hh in range(2):
                    last = act.activation(KZ[0:HD, ds(4 * i + (2 * u + hh - 16), 1), :],
                                          PS[hh * HD:(hh + 1) * HD, u:u + 1, :], ACT.Copy)
                last.then_inc(fq.left, 1)

    def foxqk_stage_pe(pe):
        small_gemm_pe(pe, 4, SW[0], 16, 32).then_inc(fg.f, 1)
        fm_pe(pe, "foxqk", fq)

    def foxqk_stage_act(act):
        act.wait_ge(fg.w, 1)
        act.activation(E_, V_, ACT.Abs)
        act.drain()
        act.activation(E_, E_, ACT.Exp, scale=-1.0).then_inc(fg.ln, 1)
        act.wait_ge(fg.w, 2)
        act.activation(LN_, W_, ACT.Ln).then_inc(fg.ln, 1)
        foxqk_act(act)

    def foxqk_stage_dve(dve):
        dve.wait_ge(fg.f, 1)
        dve.tensor_tensor(heads4(V_), heads4(PS[:, 4, 0:64]),
                          BCP[:, B_BF:B_BF + 16].unsqueeze(1).to_broadcast([P, NC_, 16]), ALU.add)
        dve.drain()
        dve.tensor_scalar(V_, V_, -1.0, None, ALU.mult)
        dve.drain().then_inc(fg.w, 1)
        dve.wait_ge(fg.ln, 1)
        softplus_dve_b(dve, V_, E_, W_, R_, Q_)
        dve.drain().then_inc(fg.w, 1)
        dve.wait_ge(fg.ln, 2)
        dve.tensor_tensor(DTA, R_, LN_, ALU.add).then_inc(fg.sp, 1)
        split_only(lo, dve, "foxqk")

    def foxv_stage_pe(pe):
        pe.wait_ge(fg.sp, 1)
        for c in range(NC_):
            last = pe.transpose(PS[0:16, 5, c * P:(c + 1) * P], DTA[:, c * 16:(c + 1) * 16], IDF[:, :])
        last.then_inc(fg.t1, 1)
        tm_pe(pe, "foxv", fv)

    def foxv_stage_act(act):
        act.wait_ge(fg.cum, 1)
        act.dma_start(KZ[HD:HD + 1, :, :], NCUM[:, :]).then_inc(fg.row, 16)
        tm_act(act, "foxv", fv, lambda i, c: VT[:, c, ds(512 * i, 512)])

    def foxv_stage_dve(dve):
        dve.memset(ONE16[:, :], 1.0)
        dve.drain()
        dve.wait_ge(fg.t1, 1)
        dve.tensor_tensor_scan(NCUM[:, :], ONE16[:, :], PS[0:16, 5, :], 0.0, ALU.mult, ALU.add)
        dve.drain().then_inc(fg.cum, 1)
        split_only(lo, dve, "foxv")

    def lower_rows(pool):
        pool.memset(QZ[HD:P, :, :], 1.0)
        pool.memset(KZ[HD:P, :, :], 0.0)

    def fox_pe(pe):
        pe.wait_ge(fg.row, 16)
        attn_pe(pe, fa, 4, 16, 4,
                lambda i, t: scores_pe(pe, t % 4, QZ[:, t // 4, (t % 4) * P:(t % 4 + 1) * P],
                                       lambda n: flat(KZ[:, ds(4 * i + t // 4, 1), 0:n]), t % 4),
                lambda k, b: PB[:, k % NP, b * P:(b + 1) * P], PT,
                lambda i, k, b: VT[:, b, ds(i * 256 + (k // 4) * HD, HD)], (fa.ex, fa.at.ex + 4 + 1), HD)

    def head_queries(act, QZx, src, i):
        for h in range(4):
            last = act.activation(QZx[0:HD, h:h + 1, :], src[(h % 2) * HD:(h % 2 + 1) * HD, ds(2 * i + h // 2, 1), :],
                                  ACT.Copy)
        return last

    def fox_act(act):
        exps, _ = one_softmax(act, None, lambda t, a, b: PB[:, t % NP, a:b])
        attn_act(act, fa, 4, 16, 4, lambda i: head_queries(act, QZ, QT, i), exps, PT)

    def fox_dve(dve):
        def output(i, h):
            rw = RW[:, 4 * (h % 2):4 * (h % 2) + 4]
            dve.reciprocal(rw, RS[:, 4 * (h % 4):4 * (h % 4) + 4])
            dve.drain()
            return dve.tensor_tensor(OB[:, :, ds(i * 256 + h * HD, HD)],
                                     PS[:, 6 + h % 2, 0:256].rearrange("p (c d) -> p c d", c=NC_),
                                     rw.unsqueeze(2).to_broadcast([P, NC_, HD]), ALU.mult)
        _, maxima = one_softmax(None, dve, None)
        attn_dve(dve, fa, 4, 16, maxima, output)

    split_s = shared("split", "tr hi lo")

    def split_fm(src, dh, dl, gain=None, const=1.0):
        s = turn(split_s, tr=KT, hi=KT, lo=KT)

        def f_pe(pe):
            for f in range(KT):
                if f >= 4:
                    pe.wait_ge(s.lo, s.at.lo + f - 3)
                for c in range(NC_):
                    last = pe.transpose(PS[:, f % 4, c * P:(c + 1) * P], src[:, c, f * P:(f + 1) * P], IDF[:, :])
                last.then_inc(s.tr, 1)

        def f_act(act):
            for f in range(KT):
                act.wait_ge(s.tr, s.at.tr + f + 1)
                act.activation(dh[:, f, :], PS[:, f % 4, :], ACT.Copy,
                               scale=const if gain is None else gain).then_inc(s.hi, 1)

        def f_dve(dve):
            for f in range(KT):
                dve.wait_ge(s.hi, s.at.hi + f + 1)
                dve.scalar_tensor_tensor(out=dl[:, f, :], in0=PS[:, f % 4, :],
                                         scalar=const if gain is None else gain,
                                         in1=dh[:, f, :], op0=ALU.mult, op1=ALU.subtract).then_inc(s.lo, 1)
        return f_pe, f_act, f_dve, None

    OH = a_("OH", 0, [P, KT, SEQ], F32R)
    OL = a_("OL", 16, [P, KT, SEQ], F32R)

    def rope_tables_pool(pool, RAB, TABC, gain, s):
        g = BCP[:, gain:gain + HD]
        h = HD // 2
        for c in range(NC_):
            pool.tensor_tensor(RAB[:, c, 0, :], TABC[:, c, 0, :], g, ALU.mult)
            pool.tensor_tensor(RAB[:, c, 1, 0:h], TABC[:, c, 1, 0:h], g[:, h:HD], ALU.mult)
            pool.tensor_tensor(RAB[:, c, 1, h:HD], TABC[:, c, 1, h:HD], g[:, 0:h], ALU.mult)
        pool.drain().then_inc(s, 1)

    def rope_chunk(dve, t, out_, nh, RAB, c, ss, TMP):
        h = HD // 2
        tmp = TMP[:, 0:nh * HD].rearrange("p (h d) -> p h d", h=nh)
        dve.tensor_tensor(t, t, ss.unsqueeze(2).to_broadcast([P, nh, HD]), ALU.mult)
        dve.drain()
        for a, b in ((0, h), (h, 0)):
            dve.tensor_tensor(tmp[:, :, a:a + h], t[:, :, b:b + h],
                              RAB[:, c, 1, a:a + h].unsqueeze(1).to_broadcast([P, nh, h]), ALU.mult)
        dve.drain()
        dve.tensor_tensor(t, t, RAB[:, c, 0, :].unsqueeze(1).to_broadcast([P, nh, HD]), ALU.mult)
        dve.drain()
        dve.tensor_tensor(out_, t, tmp, ALU.add)
        dve.drain()

    def head_ss_chunk(dve, t, ss, TMP):
        _, nh, w = t.shape
        tmp = TMP[:, 0:nh * w].rearrange("p (h d) -> p h d", h=nh)
        dve.tensor_tensor(tmp, t, t, ALU.mult)
        dve.drain()
        dve.tensor_reduce(ss, tmp, AX, ALU.add)
        dve.drain()

    def heads_of(T, c0=0, c1=DM):
        return lambda c: per(T[:, c, c0:c1], (c1 - c0) // HD)

    rope_s = shared("rope", "tab ss rt")
    tabs = sem("tabs")

    def load_table(act, TABC):
        act.dma_start(TABC[:, :, :, :], A["rope_tok"]).then_inc(tabs, 16)

    def rope_stage(items, TABC, TMP, tabs_at, load=False):
        s = turn(rope_s, tab=len(items), ss=1, rt=1)
        at = [0]
        for it in items:
            at.append(at[-1] + NC_ * it[1])

        def f_pool(pool):
            pool.wait_ge(tabs, tabs_at)
            for _, _, RAB, gain in items:
                rope_tables_pool(pool, RAB, TABC, B_GAIN[gain], s.tab)

        def f_act(act):
            if load:
                load_table(act, TABC)
            act.wait_ge(s.ss, s.at.ss + 1)
            act.activation(TINY[:, 256:256 + at[-1]], TINY[:, 0:at[-1]], ACT.Sqrt, bias=EPS[:, 1:2],
                           scale=1.0 / HD).then_inc(s.rt, 1)

        def f_dve(dve):
            for k, (T, nh, _, _) in enumerate(items):
                for c in range(NC_):
                    head_ss_chunk(dve, T(c), TINY[:, at[k] + c * nh:at[k] + (c + 1) * nh], TMP)
            dve.drain().then_inc(s.ss, 1)
            dve.wait_ge(s.rt, s.at.rt + 1)
            dve.reciprocal(TINY[:, 0:at[-1]], TINY[:, 256:256 + at[-1]])
            dve.wait_ge(s.tab, s.at.tab + len(items))
            dve.drain()
            for k, (T, nh, RAB, _) in enumerate(items):
                for c in range(NC_):
                    rope_chunk(dve, T(c), T(c), nh, RAB, c, TINY[:, at[k] + c * nh:at[k] + (c + 1) * nh], TMP)
        return None, f_act, f_dve, f_pool

    fm_s = shared("fm", "tr ev")

    def to_fm(items, act_too=None, dve_too=None, pool_too=None):
        s = turn(fm_s, tr=len(items), ev=len(items))

        def f_pe(pe):
            for k, (src, _, _) in enumerate(items):
                if k >= 4:
                    pe.wait_ge(s.ev, s.at.ev + k - 3)
                for c in range(NC_):
                    last = pe.transpose(PS[:, k % 4, c * P:(c + 1) * P], src(c), IDF[:, :])
                last.then_inc(s.tr, 1)

        def f_act(act):
            for k, (_, dst, scale) in enumerate(items):
                act.wait_ge(s.tr, s.at.tr + k + 1)
                if isinstance(dst, tuple):
                    for h, d in enumerate(dst):
                        last = act.activation(d[0:HD, :], PS[h * HD:(h + 1) * HD, k % 4, :], ACT.Copy)
                    last.then_inc(s.ev, 1)
                else:
                    act.activation(dst, PS[:, k % 4, :], ACT.Copy, scale=scale).then_inc(s.ev, 1)
            if act_too is not None:
                act_too(act)
        return f_pe, f_act, dve_too, pool_too

    def per(ap, n):
        return ap.rearrange("p (h d) -> p h d", h=n)

    TQ = a_("TQ", 0, [P, NC_, DM])
    TK = a_("TK", 16, [P, NC_, DM])
    DV = a_("DV", 32, [P, NC_, DM])
    DQF = a_("DQF", 48, [P, KT, SEQ])
    DKF = a_("DKF", 64, [P, KT, SEQ])
    OD = a_("OD", 0, [P, NC_, DM])
    TABD = a_("TABD", 80, [P, NC_, 2, HD])
    RABQ = a_("RABQ", 82, [P, NC_, 2, HD])
    RABK = a_("RABK", 84, [P, NC_, 2, HD])
    TMPD = a_("TMPD", 86, [P, DM])
    QZD = a_("QZD", 80, [P, 4, SEQ])
    PBD = a_("PBD", 88, [P, 2 * NP, SEQ])
    PTD = a_("PTD", 104, [P, 2, SEQ])
    YDH = a_("YDH", 88, [P, KT, SEQ], F32R)
    YDL = a_("YDL", 104, [P, KT, SEQ], F32R)
    dq, dk, dvs = (turn(left_s, left=4 + 8) for _ in range(3))
    dl = sems("dl", "a b")
    da = attn_turn(4, 8, 2)

    def lam_dve(dve):
        for k in range(2):
            dve.tensor_tensor(TINY[:, 64 * k:64 * k + 64], BCP[:, B_LAM + 128 * k:B_LAM + 128 * k + 64],
                              BCP[:, B_LAM + 128 * k + 64:B_LAM + 128 * k + 128], ALU.mult)
        dve.drain()
        dve.tensor_reduce(LAM[:, 1:3], TINY[:, 0:128].rearrange("p (k d) -> p k d", k=2), AX, ALU.add)
        dve.drain().then_inc(dl.a, 1)
        dve.wait_ge(dl.b, 1)
        dve.tensor_tensor(LAM[:, 0:1], LAM[:, 4:5], LAM[:, 3:4], ALU.subtract)
        dve.drain()
        dve.tensor_scalar(LAM[:, 0:1], LAM[:, 0:1], -LAMBDA_INIT, None, ALU.add)
        dve.drain()

    def lam_act(act):
        act.wait_ge(dl.a, 1)
        act.activation(LAM[:, 3:5], LAM[:, 1:3], ACT.Exp).then_inc(dl.b, 1)

    def zero_halves(pool):
        for r in range(4):
            half = slice(HD, P) if r % 2 == 0 else slice(0, HD)
            pool.memset(QZD[half, r, :], 0.0)

    def diff_queries(act, i):
        for r in range(4):
            half = slice((r % 2) * HD, (r % 2 + 1) * HD)
            last = act.activation(QZD[half, r:r + 1, :], DQF[half, ds(2 * i + r // 2, 1), :], ACT.Copy)
        return last

    def diff_pe(pe):
        def both(i, t):
            for hh in range(2):
                last = scores_pe(pe, 2 * (t % 2) + hh, QZD[:, 2 * (t // 4) + hh, (t % 4) * P:(t % 4 + 1) * P],
                                 lambda n: flat(DKF[:, ds(2 * i + t // 4, 1), 0:n]), t % 4)
            return last
        attn_pe(pe, da, 4, 8, 2, both, lambda k, b: PBD[:, 2 * (k % NP), b * P:(b + 1) * P], PTD,
                lambda i, k, b: DV[:, b, ds(i * 256 + (k // 4) * P, P)], (da.cb, da.at.cb + 1), P)

    def diff_act(act):
        def exps(t):
            w = (t % 4 + 1) * P
            for hh in range(2):
                r, q = 2 * (t % 2) + hh, 2 * (t % NP) + hh
                last = act.activation(PBD[:, q, 0:w], PS[:, r, 0:w], ACT.Exp, bias=NM[:, r:r + 1],
                                      accum_out=RS[:, q:q + 1])
            return last
        attn_act(act, da, 4, 8, 2, lambda i: diff_queries(act, i), exps, PTD)

    def diff_dve(dve):
        def maxima(t):
            for hh in range(2):
                r = 2 * (t % 2) + hh
                last = dve.tensor_reduce(NM[:, r:r + 1], PS[:, r, 0:(t % 4 + 1) * P], AX, ALU.max, negate=True)
            return last

        def combine(B, t):
            w, q = (t % 4 + 1) * P, 2 * (t % NP)
            dve.wait_ge(da.ex, da.at.ex + B + t + 3)
            dve.reciprocal(RW[:, q:q + 2], RS[:, q:q + 2])
            dve.drain()
            dve.tensor_scalar(RW[:, q + 1:q + 2], RW[:, q + 1:q + 2], LAM[:, 0:1], None, ALU.mult)
            dve.tensor_scalar(PBD[:, q, 0:w], PBD[:, q, 0:w], RW[:, q:q + 1], None, ALU.mult)
            dve.drain()
            return dve.scalar_tensor_tensor(out=PBD[:, q, 0:w], in0=PBD[:, q + 1, 0:w], scalar=RW[:, q + 1:q + 2],
                                            in1=PBD[:, q, 0:w], op0=ALU.mult, op1=ALU.add)

        def output(i, h):
            return dve.tensor_copy(OD[:, :, ds(i * 256 + h * P, P)],
                                   PS[:, 6 + h % 2, :].rearrange("p (c d) -> p c d", c=NC_))
        attn_dve(dve, da, 4, 8, maxima, output, combine)

    sl = sems("sl", "ss rt")
    TMPS = a_("TMPS", 16, [P, DM])

    def subln_act(act):
        act.wait_ge(sl.ss, 1)
        act.activation(TINY[:, 64:96], TINY[:, 0:32], ACT.Sqrt, bias=EPS[:, 1:2], scale=1.0 / P).then_inc(sl.rt, 1)

    def subln_dve(dve):
        def head(c):
            return per(OD[:, c, :], 8)
        for c in range(NC_):
            head_ss_chunk(dve, head(c), TINY[:, 8 * c:8 * c + 8], TMPS)
        dve.drain().then_inc(sl.ss, 1)
        dve.wait_ge(sl.rt, 1)
        dve.reciprocal(TINY[:, 0:32], TINY[:, 64:96])
        dve.drain()
        dve.tensor_scalar(TINY[:, 0:32], TINY[:, 0:32], 1.0 - LAMBDA_INIT, None, ALU.mult)
        dve.drain()
        for c in range(NC_):
            dve.tensor_tensor(head(c), head(c), TINY[:, c * 8:(c + 1) * 8].unsqueeze(2).to_broadcast([P, 8, P]),
                              ALU.mult)

    T3 = a_("T3", 16, [P, NC_, 6 * NSA_G * HD])
    QF = a_("QF", 40, [P, KT, SEQ])
    KF = [a_("KSF", 56, [P, NSA_G, SEQ]), a_("KWF", 64, [P, NSA_G, SEQ])]
    TABN, RABN, TMPN = a_("TABN", 72, [P, NC_, 2, HD]), a_("RABN", 74, [P, NC_, 2, HD]), a_("TMPN", 76, [P, DM])
    TABKN, TMPK = a_("TABKN", 64, [P, NC_, 2, HD]), a_("TMPK", 60, [P, DM])
    RABKS, RABKW = a_("RABKS", 56, [P, NC_, 2, HD]), a_("RABKW", 58, [P, NC_, 2, HD])
    ON = a_("ON", 0, [P, NC_, DM])
    nq, nkv = turn(left_s, left=4 + 8), turn(left_s, left=4 + 12)

    CW = [a_("CWK", 40, [P, 16, CMP_HIDDEN]), a_("CWV", 56, [P, 16, CMP_HIDDEN])]
    KC2 = a_("KC2", 72, [P, NSA_G, SEQ])
    RH = a_("RH", 80, [P, 16, P])
    HV = a_("HV", 40, [P, 2, NSA_G, 4, 32])
    VBD = a_("VBD", 84, [P, NSA_G, 4 * HD])
    CKT = a_("CKT", 72, [P, 4, 2, HD])
    cm = sems("cm", "w tr kc2 rh hid gel out ss rt kn kt pos")

    def cmp_dma(act):
        for n, (w1, w2_, pos) in enumerate((("cmp_k_w1_2", "cmp_k_w2_2", "cmp_pos_k_2"),
                                            ("cmp_v_w1_2", "cmp_v_w2_2", "cmp_pos_v_2"))):
            act.dma_start(CW[n][:, :, :], A[w1][0].rearrange("(k p) c -> p k c", p=P)).then_inc(cm.w, 16)
            act.dma_start(CW2[n][:, :, :], A[w2_][0].rearrange("(k p) c -> p k c", p=P)).then_inc(cm.w, 16)
            act.dma_start(CPROW[16 * n:16 * n + 16, :], A[pos][0].rearrange("(k l) d -> k (l d)", l=2)).then_inc(cm.w, 16)
        act.dma_start(TABK[:, :, :], A["rope_cmp"]).then_inc(cm.w, 16)

    def cmp_pe(pe):
        pe.wait_ge(cm.w, 16 * 7)
        pe.transpose(PS[:, 5, 0:32], CPROW[:, :], IDF[0:32, 0:32]).then_inc(cm.pos, 1)
        for n in range(2):
            if n:
                pe.wait_ge(cm.kc2, 1)
            for j in range(2):
                for c in range(NC_):
                    last = pe.transpose(PS[:, j, c * P:(c + 1) * P], T3[:, c, n * 256 + j * P:n * 256 + (j + 1) * P],
                                        IDF[:, :])
            last.then_inc(cm.tr, 1)
            pe.wait_ge(cm.rh, n + 1)
            pe.wait_ge(cm.w, 16 * 7)
            for m in range(2):
                for k in range(16):
                    last = pe.matmul(PS[:, 4, m * P:(m + 1) * P], CW[n][:, k, m * P:(m + 1) * P], RH[:, k, :],
                                     start=k == 0, stop=k == 15)
            last.then_inc(cm.hid, 1)
            pe.wait_ge(cm.gel, n + 1)
            if n == 0:
                for m in range(2):
                    last = pe.matmul(PS[:, 5, 0:HD], TINY[:, m * P:(m + 1) * P], CW2[0][:, m, :],
                                     start=m == 0, stop=m == 1)
                last.then_inc(cm.out, 1)
                pe.wait_ge(cm.kn, 1)
                pe.transpose(PS[:, 6, 0:P], CKT[:, 3, :, :].rearrange("p a d -> p (a d)"), IDF[:, :]).then_inc(cm.kt, 1)
            else:
                for g in range(NSA_G):
                    for m in range(2):
                        last = pe.matmul(PS[:, 7, g * HD:(g + 1) * HD], HV[:, m, g, :, :].rearrange("p a n -> p (a n)"),
                                         CW2[1][:, m, :], start=m == 0, stop=m == 1)
                last.then_inc(cm.out, 1)

    def cmp_act(act):
        for n in range(2):
            act.wait_ge(cm.tr, n + 1)
            for g in range(NSA_G):
                half = slice((g % 2) * HD, (g % 2 + 1) * HD)
                act.activation(KC2[0:HD, g, :], PS[half, g // 2, :], ACT.Copy)
                act.activation(KC2[HD:P, g, 0:SEQ - 1], PS[half, g // 2, 1:SEQ], ACT.Copy)
            act.drain().then_inc(cm.kc2, 1)
            act.wait_ge(cm.hid, n + 1)
            hid = PS[:, 4, 0:2 * P]
            if n == 0:
                act.activation(TINY[:, 0:2 * P], hid, ACT.Gelu_apprx_tanh)
            else:
                for r in range(4):
                    act.activation(HV[:, :, :, r, :], hid.rearrange("p (m g n) -> p m g n", m=2, g=NSA_G),
                                   ACT.Gelu_apprx_tanh)
            act.drain().then_inc(cm.gel, 1)
            if n == 0:
                act.wait_ge(cm.ss, 1)
                act.activation(LAM[:, 5:6], LAM[:, 6:7], ACT.Sqrt, bias=EPS[:, 1:2], scale=1.0 / HD).then_inc(cm.rt, 1)
                act.wait_ge(cm.kt, 1)
                act.activation(KCF[:, :, :], PS[:, 6, 0:P].rearrange("p (g n) -> p g n", g=NSA_G), ACT.Copy)

    def cmp_dve(dve):
        dve.wait_ge(cm.pos, 1)
        dve.tensor_copy(CPOS[:, :, :], PS[:, 5, 0:32].rearrange("p (n k) -> p n k", n=2))
        for n in range(2):
            if n:
                dve.wait_ge(cm.hid, 1)
            dve.wait_ge(cm.kc2, n + 1)
            dve.memset(RH[:, :, :], 0.0)
            dve.wait_ge(cm.w, 16 * 7)
            dve.drain()
            for k in range(16):
                dst = RH[:, k, :].rearrange("p (g n) -> p g n", g=NSA_G)[:, :, 0:NCMP]
                src = KC2[:, :, 2 * k:2 * k + CMP_STRIDE * (NCMP - 1) + 1:CMP_STRIDE]
                dve.tensor_scalar(dst, src, CPOS[:, n, k:k + 1], None, ALU.add)
            dve.drain().then_inc(cm.rh, 1)
            dve.wait_ge(cm.out, n + 1)
            if n == 0:
                dve.tensor_copy(CKT[:, 0, 0, :], PS[:, 5, 0:HD])
                dve.drain()
                dve.tensor_tensor(CKT[:, 0, 1, :], CKT[:, 0, 0, :], CKT[:, 0, 0, :], ALU.mult)
                dve.drain()
                dve.tensor_reduce(LAM[:, 6:7], CKT[:, 0, 1, :], AX, ALU.add).then_inc(cm.ss, 1)
                dve.wait_ge(cm.rt, 1)
                dve.reciprocal(LAM[:, 7:8], LAM[:, 5:6])
                dve.drain()
                x, h = CKT[:, 0, 0, :], HD // 2
                dve.tensor_scalar(x, x, LAM[:, 7:8], None, ALU.mult)
                dve.drain()
                dve.tensor_tensor(x, x, BCP[:, B_GAIN["kc"]:B_GAIN["kc"] + HD], ALU.mult)
                dve.drain()
                dve.tensor_tensor(CKT[:, 1, 0, :], x, TABK[:, 0, :], ALU.mult)
                dve.tensor_tensor(CKT[:, 1, 1, 0:h], x[:, h:HD], TABK[:, 1, 0:h], ALU.mult)
                dve.tensor_tensor(CKT[:, 1, 1, h:HD], x[:, 0:h], TABK[:, 1, h:HD], ALU.mult)
                dve.drain()
                for a in range(2):
                    dve.tensor_tensor(CKT[:, 3, a, :], CKT[:, 1, 0, :], CKT[:, 1, 1, :], ALU.add)
                dve.drain().then_inc(cm.kn, 1)
                dve.wait_ge(cm.kt, 1)
            else:
                dve.memset(VBD[:, :, :], 0.0)
                dve.drain()
                for a in range(4):
                    rows_ = slice(32 * a, 32 * a + 32)
                    dve.tensor_copy(VBD[rows_, :, a * HD:(a + 1) * HD], per(PS[rows_, 7, 0:256], NSA_G))

    SC = a_("SC", 72, [P, NC_ * HPG, 32])
    CMASK = T3[:, 0, 0:P].rearrange("p (c n) -> p c n", c=NC_)
    PTC = a_("PTC", 74, [P, SEQ])
    ca = sems("ca", "gate sig mask sc m ex p tr pt o od")

    def cattn_pe(pe):
        small_gemm_pe(pe, 7, SW[1], 0, 48).then_inc(ca.gate, 1)
        for g in range(NSA_G):
            if g:
                pe.wait_ge(ca.m, g)
            for qb in range(NC_):
                for hg in range(HPG):
                    h = HPG * g + hg
                    half = slice((h % 2) * HD, (h % 2 + 1) * HD)
                    k = (qb * 2 + hg // 2) * 32
                    last = pe.matmul(PS[:, 4 * (hg % 2), k:k + 32], QF[half, h // 2, qb * P:(qb + 1) * P], KCF[half, g, :],
                                     start=True, stop=True)
            last.then_inc(ca.sc, 1)
            pe.wait_ge(ca.p, g + 1)
            if g:
                pe.wait_ge(ca.pt, g)
            for qb in range(NC_):
                last = pe.transpose(PS[:, 1, qb * P:(qb + 1) * P],
                                    SC[:, qb * HPG:(qb + 1) * HPG, :].rearrange("p a n -> p (a n)"), IDF[:, :])
            last.then_inc(ca.tr, 1)
            pe.wait_ge(ca.pt, g + 1)
            if g:
                pe.wait_ge(ca.od, g)
            for qb in range(NC_):
                last = pe.matmul(PS[:, 2 + qb // 2, (qb % 2) * 256:(qb % 2) * 256 + 256],
                                 PTC[:, qb * P:(qb + 1) * P], VBD[:, g, :], start=True, stop=True)
            last.then_inc(ca.o, 1)

    def cattn_act(act):
        act.wait_ge(ca.gate, 1)
        act.activation(GT[:, :, :], PS[:, 7, 0:192].rearrange("p (c k) -> p c k", c=NC_), ACT.Sigmoid)
        act.drain().then_inc(ca.sig, 1)
        for g in range(NSA_G):
            act.wait_ge(ca.m, g + 1)
            act.activation(SC[:, :, :], SC[:, :, :], ACT.Exp).then_inc(ca.ex, 1)
            act.wait_ge(ca.tr, g + 1)
            if g:
                act.wait_ge(ca.o, g)
            act.activation(PTC[:, :], PS[:, 1, :], ACT.Copy).then_inc(ca.pt, 1)

    def cattn_pool(pool):
        pool.memset(CMASK[:, :, :], 0.0)
        pool.drain().then_inc(ca.mask, 1)
        pool.wait_ge(ca.mask, 1)
        pool.affine_select(out=CMASK[:, :, :], in_=CMASK[:, :, :], compare_op=ALU.is_ge, fill=MASKED,
                           base=-(CMP_BLOCK - 1), pattern=[[P, NC_], [-CMP_STRIDE, 32]], channel_multiplier=1)
        pool.drain().then_inc(ca.mask, 1)

    def cattn_dve(dve):
        n = NC_ * HPG
        dve.wait_ge(ca.mask, 2)
        dve.wait_ge(ca.sig, 1)
        for g in range(NSA_G):
            dve.wait_ge(ca.sc, g + 1)
            if g:
                dve.wait_ge(ca.tr, g)
            for r in range(2):
                dve.tensor_tensor(SC[:, :, :].rearrange("p (a b two) k -> p a b two k", a=NC_, two=2)[:, :, :, r, :],
                                  PS[:, 4 * r, 0:256].rearrange("p (a b k) -> p a b k", a=NC_, b=2),
                                  CMASK[:, :, :].unsqueeze(2).to_broadcast([P, NC_, 2, 32]), ALU.add)
            dve.drain()
            dve.tensor_reduce(TINY[:, 0:n], SC[:, :, :], AX, ALU.max)
            dve.drain()
            dve.tensor_scalar(TINY[:, 0:n], TINY[:, 0:n], MASKED / 10, None, ALU.max)
            dve.drain()
            dve.tensor_tensor(SC[:, :, :], SC[:, :, :], TINY[:, 0:n].unsqueeze(2).to_broadcast([P, n, 32]),
                              ALU.subtract)
            dve.drain().then_inc(ca.m, 1)
            dve.wait_ge(ca.ex, g + 1)
            dve.tensor_reduce(TINY[:, 16:16 + n], SC[:, :, :], AX, ALU.add)
            dve.drain()
            dve.tensor_scalar(TINY[:, 16:16 + n], TINY[:, 16:16 + n], 1e-30, None, ALU.max)
            dve.drain()
            dve.reciprocal(TINY[:, 32:32 + n], TINY[:, 16:16 + n])
            dve.drain()
            dve.tensor_tensor(TINY[:, 48:48 + n].rearrange("p (a b) -> p a b", a=NC_),
                              TINY[:, 32:32 + n].rearrange("p (a b) -> p a b", a=NC_),
                              GT[:, :, 12 * g:12 * g + 10:3], ALU.mult)
            dve.drain()
            dve.tensor_tensor(SC[:, :, :], SC[:, :, :], TINY[:, 48:48 + n].unsqueeze(2).to_broadcast([P, n, 32]),
                              ALU.mult)
            dve.drain().then_inc(ca.p, 1)
            dve.wait_ge(ca.o, g + 1)
            for b in range(2):
                dve.tensor_copy(ON[:, 2 * b:2 * b + 2, g * 256:(g + 1) * 256],
                                PS[:, 2 + b, :].rearrange("p (a k) -> p a k", a=2))
            dve.drain().then_inc(ca.od, 1)

    QZN = a_("QZN", 76, [P, HPG, SEQ])
    PTN = a_("PTN", 72, [P, 2, SEQ])
    OTMP = a_("OTMP", 84, [P, NC_, HD])
    NSTEP = HPG * 2 * NC_
    na = attn_turn(NSA_G, NSTEP, 4)

    def pn(t, a, b):
        return T3[:, t % NP, a:b]

    def zero_rows(pool):
        for T in (KF[0], KF[1], QZN):
            pool.memset(T[HD:P, :, :], 0.0)

    def nsa_pe(pe):
        attn_pe(pe, na, NSA_G, NSTEP, 4,
                lambda g, t: scores_pe(pe, t % 4, QZN[:, t // 8, (t % 4) * P:(t % 4 + 1) * P],
                                       lambda n: flat(KF[t // 4 % 2][:, ds(g, 1), 0:n]), t % 4),
                lambda k, b: pn(k, b * P, (b + 1) * P), PTN,
                lambda g, k, b: T3[:, b, ds(768 + 512 * (k // 4 % 2) + HD * g, HD)], (na.ex, na.at.ex + 4 + 1), HD)

    def nsa_act(act):
        exps, _ = one_softmax(act, None, pn)
        attn_act(act, na, NSA_G, NSTEP, 4, lambda g: head_queries(act, QZN, QF, g), exps, PTN)

    def nsa_dve(dve):
        def output(g, q):
            hh, branch = q // 2, q % 2
            inv, rw = (RW[:, 8 * (q % 2) + r:8 * (q % 2) + r + 4] for r in (0, 4))
            dve.reciprocal(inv, RS[:, 4 * (q % 4):4 * (q % 4) + 4])
            dve.drain()
            dve.tensor_tensor(rw.unsqueeze(2), inv.unsqueeze(2),
                              GT[:, :, ds(12 * g + 3 * hh + 1 + branch, 1)], ALU.mult)
            dve.drain()
            dve.tensor_tensor(OTMP[:, :, :], PS[:, 6 + q % 2, 0:256].rearrange("p (c d) -> p c d", c=NC_),
                              rw.unsqueeze(2).to_broadcast([P, NC_, HD]), ALU.mult)
            dve.drain()
            o = ON[:, :, ds(g * 256 + hh * HD, HD)]
            return dve.tensor_tensor(o, o, OTMP[:, :, :], ALU.add)
        _, maxima = one_softmax(None, dve, None)
        attn_dve(dve, na, NSA_G, NSTEP, maxima, output)

    YNH = a_("YNH", 16, [P, KT, SEQ], F32R)
    YNL = a_("YNL", 32, [P, KT, SEQ], F32R)
    MXH = a_("MXH", 48, [P, KT, SEQ], F32R)
    MXL = a_("MXL", 64, [P, KT, SEQ], F32R)
    SG = a_("SG", 0, [P, 4, SEQ])
    MT = a_("MT", 8, [P, 4, SEQ])
    mg = sems("mg", "sig y hi free")

    def merge_pe(pe):
        def body(i):
            for u in range(8):
                jj = u // 4
                if u % 4 == 0:
                    pe.wait_ge(mg.free, 2 * i + jj + 1)
                ah, al = ((YDH, YDL), (YNH, YNL), (XH, XL), (XH, XL))[u % 4]
                unit_fm(pe, first["merge"], 8, i, u, PS[:, u, :], ah, al)
        loop(pe, "merge", body)

    def merge_act(act):
        def body(i):
            for u in range(8):
                jj = u // 4
                ring_step(hi, act, "merge", i, u)
                if u % 4 >= 2:
                    act.wait_ge(mg.free, 2 * i + jj + 1)
                    act.wait_ge(unit_done, first["merge"] + 8 * i + u + 1)
                    act.activation(SG[:, 2 * jj + u % 4 - 2, :], PS[:, u, :], ACT.Sigmoid).then_inc(mg.sig, 1)
                if u % 4 == 3:
                    act.wait_ge(mg.y, 2 * i + jj + 1)
                    act.activation(MXH[:, ds(2 * i + jj, 1), :], MT[:, 2 * jj:2 * jj + 1, :],
                                   ACT.Copy).then_inc(mg.hi, 1)
        loop(act, "merge", body)

    def merge_dve(dve):
        dve.drain().then_inc(mg.free, 2)

        def body(i):
            for u in range(8):
                jj = u // 4
                ring_step(lo, dve, "merge", i, u)
                if u % 4 < 3:
                    continue
                dve.wait_ge(mg.sig, 2 * (2 * i + jj) + 2)
                dve.wait_ge(unit_done, first["merge"] + 8 * i + u + 1)
                for k in range(2):
                    dve.tensor_tensor(MT[:, 2 * jj + k, :], SG[:, 2 * jj + k, :], PS[:, 4 * jj + k, :], ALU.mult)
                dve.drain()
                dve.tensor_tensor(MT[:, 2 * jj, :], MT[:, 2 * jj, :], MT[:, 2 * jj + 1, :],
                                  ALU.add).then_inc(mg.y, 1)
                dve.wait_ge(mg.hi, 2 * i + jj + 1)
                dve.tensor_tensor(MXL[:, ds(2 * i + jj, 1), :], MT[:, 2 * jj:2 * jj + 1, :],
                                  MXH[:, ds(2 * i + jj, 1), :], ALU.subtract)
                dve.drain().then_inc(mg.free, 1)
        loop(dve, "merge", body)

    MH = a_("MH", 0, [P, 16, SEQ], F32R)
    ML = a_("ML", 32, [P, 16, SEQ], F32R)
    RL = a_("RL", 64, [P, 4, SEQ])

    up_s = shared("up", "relu y hi")

    def mlp_up(name, add=None):
        s = turn(up_s, relu=2 + 16, y=2 + 16, hi=16)

        def f_pe(pe):
            if add is not None:
                pe.wait_ge(add, 2)

            def body(i):
                for u in range(2):
                    pe.wait_ge(s.relu, s.at.relu + 2 * i + u + 1)
                    unit_fm(pe, first[name], 2, i, u, PS[:, u, :], XH, XL)
            loop(pe, name, body)

        def f_act(act):
            act.drain().then_inc(s.relu, 2)

            def body(i):
                for u in range(2):
                    ring_step(hi, act, name, i, u)
                    act.wait_ge(unit_done, first[name] + 2 * i + u + 1)
                    act.wait_ge(s.y, s.at.y + 2 * i + u + 1)
                    act.activation(RL[:, u, :], PS[:, u, :], ACT.Relu).then_inc(s.relu, 1)
                    act.wait_ge(s.y, s.at.y + 2 * i + u + 3)
                    act.activation(MH[:, ds(2 * i + u, 1), :], RL[:, 2 + u:3 + u, :], ACT.Copy).then_inc(s.hi, 1)
            loop(act, name, body)

        def f_dve(dve):
            dve.drain().then_inc(s.y, 2)
            if add is not None:
                add_banks(dve, add)

            def body(i):
                for u in range(2):
                    ring_step(lo, dve, name, i, u)
                    dve.wait_ge(s.relu, s.at.relu + 2 * i + u + 3)
                    dve.tensor_tensor(RL[:, 2 + u, :], RL[:, u, :], RL[:, u, :], ALU.mult).then_inc(s.y, 1)
                    dve.wait_ge(s.hi, s.at.hi + 2 * i + u + 1)
                    dve.tensor_tensor(ML[:, ds(2 * i + u, 1), :], RL[:, 2 + u:3 + u, :], MH[:, ds(2 * i + u, 1), :],
                                      ALU.subtract)
                    dve.drain()
            loop(dve, name, body)
        return f_pe, f_act, f_dve, None

    def add_banks(dve, done):
        for m in range(KT):
            dve.tensor_tensor(X[:, m, :], X[:, m, :], PS[:, m, :], ALU.add).then_inc(done, 1)

    n0, n1, n2, n3 = (norm_turn() for n in range(4))
    f0, f1 = ffn_turn(), ffn_turn()
    fin = sems("fin", "half add tr out st")
    OT = a_("OT", 0, [P, NC_, DM])
    want = list(size)

    r0, r1 = (turn(norm_s, cent=KT, sq=KT, ssq=KT, std=1, tmp=KT, hi=KT) for n in range(2))

    def tm_stage(name, s, dst, loads=None, rope=None, pool_fn=None):
        if rope is None:
            def f_act(act):
                if loads is not None:
                    loads(act)
                tm_act(act, name, s, lambda i, c: dst[:, c, ds(512 * i, 512)])
            return (lambda e: tm_pe(e, name, s)), f_act, (lambda e: split_only(lo, e, name)), pool_fn

        T, nh, RAB, gain, TABC, tabs_at, TMP = rope
        r = turn(rope_s, tab=1, ss=NC_, rt=NC_)
        U, bodies = size[name]

        def f_pool(pool):
            pool.wait_ge(tabs, tabs_at)
            rope_tables_pool(pool, RAB, TABC, B_GAIN[gain], r.tab)

        def f_act(act):
            if loads is not None:
                loads(act)
            act.drain().then_inc(s.left, 4)
            for p in range(U * bodies):
                i, u = divmod(p, U)
                ring_step(hi, act, name, i, u)
                c = p // 2
                if p % 2 == 0 and c < NC_:
                    act.wait_ge(r.ss, r.at.ss + c + 1)
                    act.activation(TINY[:, 256 + c * nh:256 + (c + 1) * nh], TINY[:, c * nh:(c + 1) * nh], ACT.Sqrt,
                                   bias=EPS[:, 1:2], scale=1.0 / HD).then_inc(r.rt, 1)
                if u == U - 1:
                    act.wait_ge(unit_done, first[name] + p + 1)
                    for k in range(NC_):
                        act.activation(dst[:, k, 512 * i:512 * i + 512], PS[:, k, :], ACT.Copy).then_inc(s.left, 1)

        def f_dve(dve):
            for p in range(U * bodies):
                ring_step(lo, dve, name, *divmod(p, U))
                c = p // 2
                if c >= NC_:
                    continue
                ss = TINY[:, c * nh:(c + 1) * nh]
                if p % 2 == 0:
                    head_ss_chunk(dve, T(c), ss, TMP)
                    dve.drain().then_inc(r.ss, 1)
                else:
                    if c == 0:
                        dve.wait_ge(r.tab, r.at.tab + 1)
                    dve.wait_ge(r.rt, r.at.rt + c + 1)
                    dve.reciprocal(ss, TINY[:, 256 + c * nh:256 + (c + 1) * nh])
                    dve.drain()
                    rope_chunk(dve, T(c), T(c), nh, RAB, c, ss, TMP)
        return (lambda e: tm_pe(e, name, s)), f_act, f_dve, f_pool

    def finish_pe(pe):
        for f in range(KT):
            pe.wait_ge(fin.add, f + 1)
            if f >= 4:
                pe.wait_ge(fin.out, f - 3)
            for c in range(NC_):
                last = pe.transpose(PS[:, f % 4, c * P:(c + 1) * P], X[:, f, c * P:(c + 1) * P], IDF[:, :])
            last.then_inc(fin.tr, 1)

    def finish_dve(dve):
        add_banks(dve, fin.add)
        for f in range(KT):
            dve.wait_ge(fin.tr, f + 1)
            dve.tensor_copy(OT[:, :, f * P:(f + 1) * P],
                            PS[:, f % 4, :].rearrange("p (c t) -> p c t", c=NC_)).then_inc(fin.out, 1)

    def stages(e, kind):
        fns = STAGES[kind]
        for k, fn in enumerate(fns):
            if fn is not None:
                fn(e)
            barrier(e, kind)

    plan = [
        (setup_pe, setup_act, setup_dve, setup_pool),
        (gate_pe, gate_act, gate_dve, None),
        (xbc_pe, xbc_act, xbc_dve, None),
        (ssd_pe, ssd_act, ssd_dve, None),
        (ssdh_pe, ssdh_act, ssdh_dve, None),
        (gnorm_pe, gnorm_act, gnorm_dve, None),
        (lambda e: kmajor_pe(e, "out0", YH, YL), lambda e: split_only(hi, e, "out0"), lambda e: split_only(lo, e, "out0"), None),
        (lambda e: ln_pe(e, n0), lambda e: ln_act(e, n0, C_LMG, C_LMB), lambda e: ln_dve(e, n0, C_LMG, C_LMB), None),
        (lambda e: ffn_up_pe(e, 0, f0), lambda e: ffn_up_act(e, 0, f0), lambda e: ffn_up_dve(e, 0, f0), None),
        (lambda e: kmajor_pe(e, "down0", FH, FL), lambda e: split_only(hi, e, "down0"), lambda e: split_only(lo, e, "down0"), None),
        (lambda e: ln_pe(e, n1), lambda e: ln_act(e, n1, C_LFG, C_LFB), lambda e: ln_dve(e, n1, C_LFG, C_LFB), None),
        (foxqk_stage_pe, foxqk_stage_act, foxqk_stage_dve, lower_rows),
        (foxv_stage_pe, foxv_stage_act, foxv_stage_dve, None),
        (fox_pe, fox_act, fox_dve, None),
        split_fm(OB, OH, OL),
        (lambda e: kmajor_pe(e, "foxout", OH, OL), lambda e: split_only(hi, e, "foxout"),
         lambda e: split_only(lo, e, "foxout"), None),
        (lambda e: ln_pe(e, n2), lambda e: ln_act(e, n2, C_LMG + 8, C_LMB + 8),
         lambda e: ln_dve(e, n2, C_LMG + 8, C_LMB + 8), None),
        (lambda e: ffn_up_pe(e, 1, f1), lambda e: ffn_up_act(e, 1, f1), lambda e: ffn_up_dve(e, 1, f1), None),
        (lambda e: kmajor_pe(e, "down1", FH, FL), lambda e: split_only(hi, e, "down1"), lambda e: split_only(lo, e, "down1"), None),
        (lambda e: ln_pe(e, n3), lambda e: ln_act(e, n3, C_LFG + 8, C_LFB + 8),
         lambda e: ln_dve(e, n3, C_LFG + 8, C_LFB + 8), None),
        (lambda e: ssq_pe(e, r0), lambda e: rms_act(e, r0, C_MG2), lambda e: rms_dve(e, r0, C_MG2, False), None),
        tm_stage("dq", dq, TQ, loads=lambda act: load_table(act, TABD)),
        tm_stage("dk", dk, TK, rope=(heads_of(TQ), 16, RABQ, "dq", TABD, 16, TMPD)),
        tm_stage("dv", dvs, DV, rope=(heads_of(TK), 16, RABK, "dk", TABD, 16, TMPD)),
        to_fm([(lambda c, f=f: TQ[:, c, f * P:(f + 1) * P], DQF[:, f, :], SCALE) for f in range(KT)]
              + [(lambda c, f=f: TK[:, c, f * P:(f + 1) * P], DKF[:, f, :], 1.0) for f in range(KT)],
              lam_act, lam_dve, zero_halves),
        (diff_pe, diff_act, diff_dve, None),
        (None, subln_act, subln_dve, None),
        split_fm(OD, YDH, YDL, gain=PCOL[:, C_SUB:C_SUB + 1]),
        tm_stage("nq", nq, TQ, loads=lambda act: (load_table(act, TABN), cmp_dma(act))),
        tm_stage("nkv", nkv, T3, rope=(heads_of(TQ), 16, RABN, "nq", TABN, 32, TMPN)),
        (cmp_pe, cmp_act, cmp_dve, None),
        rope_stage([(heads_of(T3, 512, 768), 4, RABKS, "ks"), (heads_of(T3, 1024, 1280), 4, RABKW, "kw")],
                   TABKN, TMPK, 48, load=True),
        to_fm([(lambda c, f=f: TQ[:, c, f * P:(f + 1) * P], QF[:, f, :], SCALE) for f in range(KT)]
              + [(lambda c, b=b, j=j: T3[:, c, 512 + 512 * b + j * P:512 + 512 * b + (j + 1) * P],
                  (KF[b][:, 2 * j, :], KF[b][:, 2 * j + 1, :]), 1.0) for b in range(2) for j in range(2)],
              pool_too=zero_rows),
        (cattn_pe, cattn_act, cattn_dve, cattn_pool),
        (nsa_pe, nsa_act, nsa_dve, None),
        split_fm(ON, YNH, YNL),
        (merge_pe, merge_act, merge_dve, None),
        (lambda e: kmajor_pe(e, "out2", MXH, MXL), lambda e: split_only(hi, e, "out2"),
         lambda e: split_only(lo, e, "out2"), None),
        (lambda e: ssq_pe(e, r1), lambda e: rms_act(e, r1, C_ML2), lambda e: rms_dve(e, r1, C_ML2, True), None),
        mlp_up("mupa"),
        (lambda e: kmajor_pe(e, "mdna", MH, ML), lambda e: split_only(hi, e, "mdna"),
         lambda e: split_only(lo, e, "mdna"), None),
        mlp_up("mupb", add=fin.half),
        (lambda e: kmajor_pe(e, "mdnb", MH, ML), lambda e: split_only(hi, e, "mdnb"),
         lambda e: split_only(lo, e, "mdnb"), None),
    ]
    plan.append((finish_pe, None, finish_dve, None))
    STAGES = {k: [p[j] for p in plan] for j, k in enumerate(("pe", "act", "dve", "pool"))}

    block = ctx.enter_context(nc.Block())

    @block.sync
    def _(sp):
        for name, U, bodies, src in STREAM:
            b = first[name]

            def body(i):
                for u in range(U):
                    slot = u % 2
                    s = src(i, u)
                    if b + u < 2 and isinstance(i, int) and i == 0:
                        pass
                    else:
                        sp.wait_ge(lo_ready, b + u - 1 + U * i)
                    dst = RAW[:, slot, :].rearrange("p (k c) -> p k c", k=s.shape[1])
                    sp.dma_start(dst, s).then_inc(raw_loaded[slot], 16)
            start = 0
            if b == 0:
                body(0)
                start = 1
            with sp.Fori(start, bodies) as i:
                body(i)
        sp.wait_ge(stage_end, 4 * len(plan))
        sp.dma_start(out[0].rearrange("(c p) f -> p c f", p=P), OT[:, :, :]).then_inc(fin.st, 16)
        sp.wait_ge(fin.st, 16)

    @block.gpsimd
    def _(pool):
        stages(pool, "pool")

    @block.scalar
    def _(act):
        setup_dma(act)
        stages(act, "act")

    @block.vector
    def _(dve):
        stages(dve, "dve")

    @block.tensor
    def _(pe):
        stages(pe, "pe")

    ctx.close()


def constants():
    half = HD // 2
    inv = np.float32(10000.0) ** (-np.arange(half, dtype=np.float32) / np.float32(half))

    def table(pos):
        ang = pos.astype(np.float32)[:, None] * inv[None, :]
        c, s = np.cos(ang), np.sin(ang)
        return np.stack([np.concatenate([c, c], 1), np.concatenate([-s, s], 1)], 1).astype(np.float32)

    tok = table(np.arange(SEQ)).reshape(NC_, P, 2, HD).transpose(1, 0, 2, 3)
    centres = np.zeros((32, 2, HD), np.float32)
    centres[:NCMP] = table(np.arange(NCMP) * CMP_STRIDE + (CMP_BLOCK - 1) / 2.0)
    return {"rope_tok": np.ascontiguousarray(tok), "rope_cmp": np.ascontiguousarray(np.tile(centres, (NSA_G, 1, 1)))}


def kernel(**inputs):
    from concourse import bacc
    from concourse.bass_utils import run_bass_kernel_spmd

    nc = bacc.Bacc("TRN2", target_bir_lowering=False, num_devices=1)
    arrays, aps = {}, {}
    for name, value in {**inputs, **constants()}.items():
        a = np.ascontiguousarray(value)
        arrays[f"in_{name}"] = a
        aps[name] = nc.dram_tensor(f"in_{name}", a.shape, mybir.dt.from_np(a.dtype), kind="ExternalInput").ap()
    out = nc.dram_tensor("out", (1, SEQ, DM), F32, kind="ExternalOutput").ap()
    build(nc, aps, out)
    r = run_bass_kernel_spmd(nc, [arrays], core_ids=[0])
    return r.results[0]["out"]
```

```python
import math
from collections import namedtuple
from contextlib import ExitStack

import numpy as np
import concourse.bass as bass
from concourse import mybir

F32, F32R, BF16 = mybir.dt.float32, mybir.dt.float32r, mybir.dt.bfloat16
ALU = mybir.AluOpType
ACT = mybir.ActivationFunctionType
AX = mybir.AxisListType.X

P = 128
SEQ, DM = 512, 1024
NC_ = SEQ // P
KT = DM // P
DEPTH = 2
ALPHA = (2 * DEPTH) ** 0.25
LN_EPS, RMS_EPS = 1e-5, 1e-6
HEADS, HD = 16, 64
SCALE = HD ** -0.5
STATE, GROUPS = 128, 2
DFF = 2816
FT = DFF // P
DFF2 = 4096
FT2 = DFF2 // P
CMP_BLOCK, CMP_STRIDE, CMP_HIDDEN = 32, 16, 256
NCMP = (SEQ - CMP_BLOCK) // CMP_STRIDE + 1
NSA_G = 4
HPG = HEADS // NSA_G
MASKED = -1e30
LAMBDA_INIT = 0.8 - 0.6 * math.exp(0.0)
ds = bass.ds


def build(nc, A, out):
    ctx = ExitStack()
    base = (nc.sbuf_base + 63) // 64 * 64
    cursor = [base]

    def place(name, shape, dt=F32, at=None):
        size = int(np.prod(shape[1:])) * (2 if dt == BF16 else 4)
        if at is None:
            at = cursor[0]
            cursor[0] += (size + 31) // 32 * 32
        return nc.alloc_sbuf_tensor_at(name, shape, dt, offset=at)

    def sem(name):
        return ctx.enter_context(nc.semaphore(name))

    def sems(prefix, names):
        return namedtuple(prefix, names)(*[sem(f"{prefix}_{n}") for n in names.split()])

    def shared(prefix, names):
        return (namedtuple(prefix, names + " at"), namedtuple(prefix + "_at", names),
                {n: sem(f"{prefix}_{n}") for n in names.split()}, {n: 0 for n in names.split()})

    def turn(sh_, **counts):
        view, view_at, the_sems, so_far = sh_
        s = view(**the_sems, at=view_at(**so_far))
        for name, n in counts.items():
            so_far[name] += n
        return s

    RAW = place("RAW", [P, 2, 1024])
    WH = place("WH", [P, 2, 1024], F32R)
    WL = place("WL", [P, 2, 1024], F32R)
    X = place("X", [P, KT, SEQ])
    XH = place("XH", [P, KT, SEQ], F32R)
    XL = place("XL", [P, KT, SEQ], F32R)
    IDF = place("IDF", [P, P])
    ONES = place("ONES", [P, P])
    IDB = place("IDB", [P, P], BF16)
    MROW = place("MROW", [P, P], BF16)
    MCOL = place("MCOL", [P, P], BF16)
    PCOL = place("PCOL", [P, 608])
    BCP = place("BCP", [P, 768])
    narrow1 = cursor[0]
    SW = [(place("SWH1", [P, KT, 32], F32R), place("SWL1", [P, KT, 32], F32R)),
          (place("SWH2", [P, KT, 48], F32R), place("SWL2", [P, KT, 48], F32R))]
    TINY = place("TINY", [P, 512])
    EPS = place("EPS", [P, 2])
    NM = place("NM", [P, 16])
    RS = place("RS", [P, 16])
    RW = place("RW", [P, 16])
    LAM = place("LAM", [P, 8])
    CW2 = [place("CW2K", [P, 2, HD], at=narrow1), place("CW2V", [P, 2, HD], at=narrow1 + 512)]
    CPOS = place("CPOS", [P, 2, 16], at=narrow1 + 1024)
    TABK = place("TABK", [P, 2, HD], at=narrow1 + 1152)
    GT = place("GT", [P, NC_, 48])
    kcf_at = cursor[0]
    KCF = place("KCF", [P, NSA_G, 32])
    CPROW = place("CPROW", [32, P], at=kcf_at)
    arena = cursor[0]

    def a_(name, kb, shape, dt=F32):
        size = int(np.prod(shape[1:])) * (2 if dt == BF16 else 4)
        assert arena + kb * 1024 + size <= nc.sbuf_usable_end, (name, (nc.sbuf_usable_end - arena) / 1024)
        return place(name, shape, dt, at=arena + int(kb * 1024))

    PS = ctx.enter_context(nc.psum_tensor("PS", [P, 8, 512], F32))

    C_SC, C_SSM, C_SSMB, C_NG, C_MG2, C_ML2, C_SUB = 0, 24, 72, 84, 92, 100, 108
    C_LMG, C_LMB, C_LFG, C_LFB = 128, 144, 160, 176
    C_FW, C_FB = 256, 520
    B_DTB, B_ALOG, B_D, B_BF = 0, 16, 32, 48
    B_GAIN = {"dq": 64, "dk": 128, "nq": 192, "kc": 256, "ks": 320, "kw": 384}
    B_LAM = 448

    raw_loaded = [sem("raw_loaded0"), sem("raw_loaded1")]
    hi_ready, lo_ready, unit_done = sem("hi_ready"), sem("lo_ready"), sem("unit_done")

    def hi(act, b, U, i, u):
        slot = u % 2
        act.wait_ge(raw_loaded[slot], 16 * ((b + u) // 2 + 2) + 8 * U * i)
        act.wait_ge(unit_done, b + u + 1 + U * i)
        act.activation(WH[:, slot, :], RAW[:, slot, :], ACT.Copy).then_inc(hi_ready, 1)

    def lo(dve, b, U, i, u):
        slot = u % 2
        dve.wait_ge(hi_ready, b + u + 3 + U * i)
        dve.tensor_tensor(WL[:, slot, :], RAW[:, slot, :], WH[:, slot, :], ALU.subtract).then_inc(lo_ready, 1)

    def mm3(pe, o, wh, wl, ah, al, first, last, rhs_is_weight=False):
        if rhs_is_weight:
            pe.matmul(o, ah, wh, start=first, stop=False)
            pe.matmul(o, al, wh, start=False, stop=False)
            return pe.matmul(o, ah, wl, start=False, stop=last)
        pe.matmul(o, wh, ah, start=first, stop=False)
        pe.matmul(o, wh, al, start=False, stop=False)
        return pe.matmul(o, wl, ah, start=False, stop=last)

    def at_start(i, u):
        return isinstance(i, int) and i == 0 and u == 0

    def unit_fm(pe, b, U, i, u, o, ah, al, tile_ready=None):
        slot = u % 2
        pe.wait_ge(lo_ready, b + u + 1 + U * i)
        for k in range(KT):
            if tile_ready is not None and at_start(i, u):
                tile_ready(k)
            last = mm3(pe, o, WH[:, slot, k * P:(k + 1) * P], WL[:, slot, k * P:(k + 1) * P],
                       ah[:, k, :], al[:, k, :], k == 0, k == KT - 1)
        last.then_inc(unit_done, 1)

    def unit_tm(pe, b, U, i, u, banks, k0, before=None, tile_ready=None):
        slot = u % 2
        pe.wait_ge(lo_ready, b + u + 1 + U * i)
        for k in range(2):
            w = slice(k * 512, (k + 1) * 512)
            if tile_ready is not None and at_start(i, 0):
                tile_ready(k0 + k)
            for c in range(NC_):
                if k0 + k == 0 and before is not None:
                    before(c)
                last = mm3(pe, banks(c), WH[:, slot, w], WL[:, slot, w],
                           XH[:, k0 + k, c * P:(c + 1) * P], XL[:, k0 + k, c * P:(c + 1) * P],
                           k0 + k == 0, k0 + k == KT - 1, rhs_is_weight=True)
        last.then_inc(unit_done, 1)

    def flat(ap):
        return ap.rearrange("p a b -> p (a b)")

    def rows(w):
        return w.rearrange("(k p) c -> p k c", p=P)

    def fm_src(w, col):
        return lambda i, u: rows(w)[:, :, ds(col(i, u), P)]

    w0 = A["sc_ssm_w_in"][0]
    wf = A["fox_w_in"][0]
    w2 = A["w_in_2"][0]

    def kmajor_src(w, tile0=0):
        def src(i, u):
            return rows(w)[:, tile0:, :][:, ds(2 * i, 2), u * 512:(u + 1) * 512]
        return src

    def tm_src(w, col0):
        def src(i, u):
            return rows(w)[:, 2 * u:2 * u + 2, ds(col0 + 512 * i, 512)]
        return src

    def ffn_src(l):
        return fm_src(A["ffn_w_up"][l], lambda i, u: 256 * i + (u // 2) * P + (u % 2) * DFF)

    def merge_src(i, u):
        jj, u = u // 4, u % 4
        if u < 2:
            return rows(A[("w_proj_diff_2", "w_proj_nsa_2")[u]][0])[:, :, ds(2 * P * i + jj * P, P)]
        return rows(w2)[:, :, ds(5680 + (u - 2) * DM + jj * P + 2 * P * i, P)]

    STREAM = [
        ("gate", 6, 4, fm_src(w0, lambda i, u: (0, DM, 2 * DM)[u % 3] + 256 * i + (u // 3) * P)),
        ("xbc", 4, 3, fm_src(w0, lambda i, u: 4 * DM + 512 * i + u * P)),
        ("z", 4, 2, tm_src(w0, 3 * DM)),
        ("out0", 2, 8, kmajor_src(A["sc_ssm_w_out"][0])),
        ("up0", 4, FT // 2, ffn_src(0)),
        ("down0", 2, FT // 2, kmajor_src(A["ffn_w_down"][0])),
        ("foxqk", 2, 8, fm_src(wf, lambda i, u: 256 * i + u * P)),
        ("foxv", 4, 2, tm_src(wf, 2 * DM)),
        ("foxout", 2, 4, kmajor_src(A["fox_w_out"][0])),
        ("up1", 4, FT // 2, ffn_src(1)),
        ("down1", 2, FT // 2, kmajor_src(A["ffn_w_down"][1])),
        ("dq", 4, 2, tm_src(w2, 0)),
        ("dk", 4, 2, tm_src(w2, DM)),
        ("dv", 4, 2, tm_src(w2, 2 * DM)),
        ("nq", 4, 2, tm_src(w2, 3 * DM)),
        ("nkv", 4, 3, tm_src(w2, 4 * DM)),
        ("merge", 8, 4, merge_src),
        ("out2", 2, 4, kmajor_src(A["w_out_2"][0])),
        ("mupa", 2, FT2 // 4, fm_src(A["w_mlp_up_2"][0], lambda i, u: 256 * i + u * P)),
        ("mdna", 2, FT2 // 4, kmajor_src(A["w_mlp_down_2"][0])),
        ("mupb", 2, FT2 // 4, fm_src(A["w_mlp_up_2"][0], lambda i, u: DFF2 // 2 + 256 * i + u * P)),
        ("mdnb", 2, FT2 // 4, kmajor_src(A["w_mlp_down_2"][0], FT2 // 2)),
    ]
    first, total = {}, 0
    for name, U, bodies, _ in STREAM:
        first[name] = total
        total += U * bodies
    size = {name: (U, bodies) for name, U, bodies, _ in STREAM}
    final = STREAM[-1][0]

    def ring_step(fn, e, name, i, u):
        U, bodies = size[name]
        if name == final and isinstance(i, int) and U * i + u + 2 >= U * bodies:
            return
        fn(e, first[name], U, i, u)

    def loop(e, name, body, peel=0, peel_last=False):
        U, n = size[name]
        cut = n - 1 if (name == final or peel_last) else n
        for i in range(peel):
            body(i)
        if cut > peel:
            with e.Fori(peel, cut) as i:
                body(i)
        if cut < n and cut >= peel:
            body(n - 1)

    stage_end = sem("stage_end")
    passed = {}

    def barrier(e, key, wait=True):
        passed[key] = passed.get(key, 0) + 1
        e.drain().then_inc(stage_end, 1)
        if not wait:
            return
        e.wait_ge(stage_end, 4 * passed[key])

    XT = a_("XT", 0, [P, NC_, DM])
    PROW = a_("PROW", 16, [P, 5, P])
    SWR = a_("SWR", 20, [P, KT, 80])
    su = sems("su", "x par bc small ident tr ev split zero")
    PARAM_ROWS = [
        (0, C_SC, A["sc_conv_w"].rearrange("a t (n p) -> (a t n) p", p=P), 24),
        (0, C_SSM, A["ssm_conv_w"].rearrange("a t (n p) -> (a t n) p", p=P), 48),
        (0, C_SSMB, A["ssm_conv_b"].rearrange("a (n p) -> (a n) p", p=P), 12),
        (0, C_NG, A["ssm_norm_g"].rearrange("a (n p) -> (a n) p", p=P), 8),
        (0, C_MG2, A["ln_mix_g_2"].rearrange("a (n p) -> (a n) p", p=P), 8),
        (0, C_ML2, A["ln_mlp_g_2"].rearrange("a (n p) -> (a n) p", p=P), 8),
        (0, C_SUB, A["diff_subln_g_2"], 1),
        (1, 0, A["ln_mix_g"].rearrange("a (n p) -> (a n) p", p=P), 16),
        (1, 16, A["ln_mix_b"].rearrange("a (n p) -> (a n) p", p=P), 16),
        (1, 32, A["ln_ffn_g"].rearrange("a (n p) -> (a n) p", p=P), 16),
        (1, 48, A["ln_ffn_b"].rearrange("a (n p) -> (a n) p", p=P), 16),
    ]
    fw = A["ffn_conv_w"].rearrange("a t (n p) -> (a t n) p", p=P)
    PARAM_ROWS += [(2, 0, fw[0:128, :], 128), (3, 0, fw[128:256, :], 128), (4, 0, fw[256:264, :], 8),
                   (4, 8, A["ffn_conv_b"].rearrange("a (n p) -> (a n) p", p=P), 88)]
    ROWS_OF = [109, 64, 128, 128, 96]
    COL_OF = [0, 128, 256, 384, 512]
    nk = A["nsa_k_norm_g_2"][0]
    BCAST = [(B_DTB, A["ssm_dt_bias"], 16), (B_ALOG, A["ssm_a_log"], 16), (B_D, A["ssm_d"], 16),
             (B_BF, A["fox_b_f"], 16), (B_GAIN["dq"], A["diff_q_norm_g_2"], HD),
             (B_GAIN["dk"], A["diff_k_norm_g_2"], HD), (B_GAIN["nq"], A["nsa_q_norm_g_2"], HD),
             (B_GAIN["kc"], nk[0:1, :], HD), (B_GAIN["ks"], nk[1:2, :], HD), (B_GAIN["kw"], nk[2:3, :], HD),
             (B_LAM, A["diff_lambda_q1_2"], HD), (B_LAM + 64, A["diff_lambda_k1_2"], HD),
             (B_LAM + 128, A["diff_lambda_q2_2"], HD), (B_LAM + 192, A["diff_lambda_k2_2"], HD)]

    def setup_dma(act):
        for h in range(2):
            act.dma_start(XT[:, 2 * h:2 * h + 2, :],
                          A["x"][0].rearrange("(c p) f -> p c f", p=P)[:, 2 * h:2 * h + 2, :]).then_inc(su.x, 16)
        for g, r, src, n in PARAM_ROWS:
            act.dma_start(PROW[r:r + n, g, :], src).then_inc(su.par, 16)
        act.dma_start(SWR[:, :, 0:16], rows(w0)[:, :, 5632:5648]).then_inc(su.small, 16)
        act.dma_start(SWR[:, :, 16:32], rows(wf)[:, :, 3072:3088]).then_inc(su.small, 16)
        act.dma_start(SWR[:, :, 32:80], rows(w2)[:, :, 5632:5680]).then_inc(su.small, 16)

    def setup_pool(pool):
        pool.memset(IDF[:, :], 0.0)
        pool.memset(ONES[:, :], 1.0)
        pool.memset(IDB[:, :], 0.0)
        pool.memset(MROW[:, :], 0.0)
        pool.memset(MCOL[:, :], 0.0)
        pool.memset(EPS[:, 0:1], LN_EPS)
        pool.memset(EPS[:, 1:2], RMS_EPS)
        pool.drain().then_inc(su.zero, 1)
        pool.wait_ge(su.zero, 1)
        for m in (IDF, IDB):
            pool.affine_select(out=m[:, :], in_=m[:, :], compare_op=ALU.not_equal, fill=1.0,
                               base=0, pattern=[[-1, P]], channel_multiplier=1)
        pool.affine_select(out=MROW[:, :], in_=MROW[:, :], compare_op=ALU.is_ge, fill=MASKED,
                           base=0, pattern=[[-1, P]], channel_multiplier=1)
        pool.affine_select(out=MCOL[:, :], in_=MCOL[:, :], compare_op=ALU.is_ge, fill=MASKED,
                           base=0, pattern=[[1, P]], channel_multiplier=-1)
        pool.drain().then_inc(su.ident, 1)

    def setup_pe(pe):
        pe.wait_ge(su.ident, 1)
        pe.wait_ge(su.x, 32)
        for f in range(KT):
            if f >= 4:
                pe.wait_ge(su.ev, f - 3)
            for c in range(NC_):
                last = pe.transpose(PS[:, 2 + f % 4, c * P:(c + 1) * P], XT[:, c, f * P:(f + 1) * P], IDF[:, :])
            last.then_inc(su.tr, 1)
        pe.wait_ge(su.par, 16 * len(PARAM_ROWS))
        for g in range(5):
            last = pe.transpose(PS[:, g // 4, (g % 4) * P:(g % 4) * P + ROWS_OF[g]], PROW[0:ROWS_OF[g], g, :],
                                IDF[0:ROWS_OF[g], 0:ROWS_OF[g]])
        last.then_inc(su.tr, 1)

    def setup_act(act):
        for u in range(2):
            act.wait_ge(raw_loaded[u], 16)
            act.activation(WH[:, u, :], RAW[:, u, :], ACT.Copy).then_inc(hi_ready, 1)
        for f in range(KT):
            act.wait_ge(su.ev, f + 1)
            act.activation(XH[:, f, :], X[:, f, :], ACT.Copy).then_inc(su.split, 1)
        act.wait_ge(su.small, 48)
        act.activation(SW[0][0][:, :, :], SWR[:, :, 0:32], ACT.Copy)
        act.activation(SW[1][0][:, :, :], SWR[:, :, 32:80], ACT.Copy)
        act.drain().then_inc(su.split, 1)
        for c, src, n in BCAST:
            act.dma_start(BCP[:, c:c + n], src[0, :].partition_broadcast(P)).then_inc(su.bc, 16)

    def setup_dve(dve):
        for u in range(2):
            dve.wait_ge(hi_ready, u + 1)
            dve.tensor_tensor(WL[:, u, :], RAW[:, u, :], WH[:, u, :], ALU.subtract).then_inc(lo_ready, 1)
        for f in range(KT):
            dve.wait_ge(su.tr, f + 1)
            dve.tensor_copy(X[:, f, :], PS[:, 2 + f % 4, :]).then_inc(su.ev, 1)
        for f in range(KT):
            dve.wait_ge(su.split, f + 1)
            dve.tensor_tensor(XL[:, f, :], X[:, f, :], XH[:, f, :], ALU.subtract)
        dve.wait_ge(su.tr, KT + 1)
        for g in range(5):
            dve.tensor_copy(PCOL[:, COL_OF[g]:COL_OF[g] + ROWS_OF[g]],
                            PS[:, g // 4, (g % 4) * P:(g % 4) * P + ROWS_OF[g]])
        dve.wait_ge(su.split, KT + 1)
        dve.tensor_tensor(SW[0][1][:, :, :], SWR[:, :, 0:32], SW[0][0][:, :, :], ALU.subtract)
        dve.tensor_tensor(SW[1][1][:, :, :], SWR[:, :, 32:80], SW[1][0][:, :, :], ALU.subtract)

    YH = a_("YH", 0, [P, 16, SEQ], F32R)
    YL = a_("YL", 32, [P, 16, SEQ], F32R)
    CSB = a_("CSB", 64, [P, 2, SEQ])
    CHP = a_("CHP", 68, [P, 2, SEQ + 8])
    CT = a_("CT", 73, [P, 2, SEQ])
    CY = a_("CY", 77, [P, 2, SEQ])
    ga = sems("ga", "copied y hi lo free")

    def gate_pe(pe):
        def body(i):
            for u in range(6):
                jj = u // 3
                if u % 3 == 0:
                    pe.wait_ge(ga.free, 2 * i + jj + 1)
                unit_fm(pe, first["gate"], 6, i, u, PS[:, 4 * jj + u % 3, :], XH, XL)
        loop(pe, "gate", body)

    def gate_act(act):
        def body(i):
            for u in range(6):
                ring_step(hi, act, "gate", i, u)
                jj = u // 3
                if u % 3 == 1:
                    act.wait_ge(ga.free, 2 * i + jj + 1)
                    act.activation(CSB[:, jj, :], PS[:, 4 * jj + 1, :], ACT.Copy).then_inc(ga.copied, 1)
                if u % 3 == 2:
                    act.wait_ge(ga.y, 2 * i + jj + 1)
                    act.activation(YH[:, ds(2 * i + jj, 1), :], CY[:, jj:jj + 1, :], ACT.Copy).then_inc(ga.hi, 1)
        loop(act, "gate", body)

    def gate_dve(dve):
        dve.memset(CHP[:, :, 0:2], 0.0)
        dve.drain().then_inc(ga.free, 2)

        def body(i):
            for u in range(6):
                ring_step(lo, dve, "gate", i, u)
                jj = u // 3
                if u % 3 != 2:
                    continue
                j = 2 * i + jj
                ch = CHP[:, jj, 2:2 + SEQ]
                dve.wait_ge(ga.copied, j + 1)
                dve.wait_ge(unit_done, first["gate"] + 6 * i + u + 1)
                dve.tensor_tensor(ch, CSB[:, jj, :], PS[:, 4 * jj + 2, :], ALU.mult)
                dve.drain()
                tap = [PCOL[:, ds(C_SC + 8 * t + j, 1)] for t in range(3)]
                dve.tensor_scalar(CT[:, jj, :], CHP[:, jj, 0:SEQ], tap[0], None, ALU.mult)
                dve.drain()
                for t in (1, 2):
                    dve.scalar_tensor_tensor(out=CT[:, jj, :], in0=CHP[:, jj, t:t + SEQ], scalar=tap[t],
                                             in1=CT[:, jj, :], op0=ALU.mult, op1=ALU.add)
                    dve.drain()
                dve.tensor_tensor(CY[:, jj, :], CT[:, jj, :], PS[:, 4 * jj, :], ALU.mult).then_inc(ga.y, 1)
                dve.wait_ge(ga.hi, j + 1)
                dve.tensor_tensor(YL[:, ds(j, 1), :], CY[:, jj:jj + 1, :], YH[:, ds(j, 1), :],
                                  ALU.subtract)
                dve.drain().then_inc(ga.free, 1)
        loop(dve, "gate", body)

    XSF = a_("XSF", 16, [P, 8, SEQ])
    BF = a_("BF", 80, [P, 2, SEQ])
    CF = a_("CF", 96, [P, 2, SEQ])
    XP = a_("XP", 64, [P, 4, SEQ + 8])
    XQ = a_("XQ", 48, [P, 4, SEQ])
    xb = sems("xb", "copied conv free")

    def xbc_dst(i, u):
        if isinstance(i, int):
            return (BF if u < 2 else CF)[:, u % 2:u % 2 + 1, :]
        return XSF[:, ds(4 * i + u, 1), :]

    def xbc_loop(e, body):
        with e.Fori(0, 2) as i:
            body(i)
        body(2)

    def xbc_pe(pe):
        def body(i):
            for u in range(4):
                if at_start(i, 0):
                    pe.wait_ge(ga.free, 2 + 7)
                else:
                    pe.wait_ge(xb.copied, 4 * i + u + 1)
                unit_fm(pe, first["xbc"], 4, i, u, PS[:, u, :], XH, XL)
        loop(pe, "xbc", body, peel=1)

    def xbc_act(act):
        act.drain().then_inc(xb.copied, 4)
        act.drain().then_inc(xb.free, 4)

        def body(i):
            for u in range(5):
                if u < 4:
                    hi(act, first["xbc"], 4, i, u)
                    act.wait_ge(xb.conv, 4 * i + u + 1)
                    act.activation(XP[:, u, 3:3 + SEQ], PS[:, u, :], ACT.Copy).then_inc(xb.copied, 1)
                if u >= 1:
                    act.wait_ge(xb.conv, 4 * i + u - 1 + 5)
                    act.activation(xbc_dst(i, u - 1), XQ[:, u - 1:u, :], ACT.Silu).then_inc(xb.free, 1)
        xbc_loop(act, body)

    def xbc_dve(dve):
        dve.memset(XP[:, :, 0:3], 0.0)
        dve.drain().then_inc(xb.conv, 4)

        def body(i):
            for u in range(4):
                lo(dve, first["xbc"], 4, i, u)
                j = 4 * i + u
                dve.wait_ge(xb.copied, j + 5)
                dve.wait_ge(xb.free, j + 1)
                tap = [PCOL[:, ds(C_SSM + 12 * t + j, 1)] for t in range(4)]
                dve.tensor_scalar(XQ[:, u, :], XP[:, u, 0:SEQ], tap[0], PCOL[:, ds(C_SSMB + j, 1)],
                                  ALU.mult, ALU.add)
                dve.drain()
                for t in (1, 2, 3):
                    last = dve.scalar_tensor_tensor(out=XQ[:, u, :], in0=XP[:, u, t:t + SEQ], scalar=tap[t],
                                                    in1=XQ[:, u, :], op0=ALU.mult, op1=ALU.add)
                    if t < 3:
                        dve.drain()
                last.then_inc(xb.conv, 1)
        xbc_loop(dve, body)

    LT = a_("LT", 104, [P, 7, SEQ])

    norm_s = shared("norm", "res sum cent sq ssq std tmp hi xl")

    def norm_turn(xl=KT):
        return turn(norm_s, res=KT, sum=1, cent=KT, sq=KT, ssq=KT, std=1, tmp=KT, hi=KT, xl=xl)

    def normed(pe, s):
        return lambda k: pe.wait_ge(s.xl, s.at.xl + k + 1)

    def ln_pe(pe, s):
        for m in range(KT):
            pe.wait_ge(s.res, s.at.res + m + 1)
            last = pe.matmul(PS[:, 0, :], ONES[:, :], X[:, m, :], start=m == 0, stop=m == KT - 1)
        last.then_inc(s.sum, 1)
        ssq_pe(pe, s)

    def ssq_pe(pe, s):
        pe.wait_ge(s.cent, s.at.cent + 2)
        for m in range(KT):
            pe.wait_ge(s.sq, s.at.sq + m + 1)
            pe.matmul(PS[:, 1, :], ONES[:, :], LT[:, m % 2, :], start=m == 0, stop=m == KT - 1).then_inc(s.ssq, 1)

    def square_act(act, s):
        for m in range(KT):
            act.wait_ge(s.cent, s.at.cent + m + 1)
            if m >= 2:
                act.wait_ge(s.ssq, s.at.ssq + m - 1)
            act.activation(LT[:, m % 2, :], X[:, m, :], ACT.Square).then_inc(s.sq, 1)

    def ln_act(act, s, g, b, split=True):
        square_act(act, s)
        act.wait_ge(s.ssq, s.at.ssq + KT)
        act.activation(LT[:, 3, :], PS[:, 1, :], ACT.Sqrt, bias=EPS[:, 0:1], scale=1.0 / DM).then_inc(s.std, 1)
        for m in range(KT):
            act.wait_ge(s.tmp, s.at.tmp + m + 1)
            for T in ((X, XH) if split else (X,)):
                last = act.activation(T[:, m, :], LT[:, 5 + m % 2, :], ACT.Identity, bias=PCOL[:, b + m:b + m + 1],
                                      scale=PCOL[:, g + m:g + m + 1])
            last.then_inc(s.hi, 1)

    def ln_dve(dve, s, g, b, split=True):
        for m in range(KT):
            dve.scalar_tensor_tensor(out=X[:, m, :], in0=X[:, m, :], scalar=ALPHA, in1=PS[:, m, :],
                                     op0=ALU.mult, op1=ALU.add).then_inc(s.res, 1)
        dve.wait_ge(s.sum, s.at.sum + 1)
        dve.tensor_scalar(LT[:, 2, :], PS[:, 0, :], 1.0 / DM, None, ALU.mult)
        dve.drain()
        for m in range(KT):
            dve.tensor_tensor(X[:, m, :], X[:, m, :], LT[:, 2, :], ALU.subtract).then_inc(s.cent, 1)
        dve.wait_ge(s.std, s.at.std + 1)
        dve.reciprocal(LT[:, 4, :], LT[:, 3, :])
        dve.drain()

        def scaled(m):
            dve.tensor_tensor(LT[:, 5 + m % 2, :], X[:, m, :], LT[:, 4, :], ALU.mult).then_inc(s.tmp, 1)

        scaled(0)
        scaled(1)
        for m in range(KT):
            if m + 2 < KT:
                dve.wait_ge(s.hi, s.at.hi + m + 1)
                scaled(m + 2)
            if not split:
                continue
            dve.wait_ge(s.hi, s.at.hi + m + 1)
            dve.tensor_tensor(XL[:, m, :], X[:, m, :], XH[:, m, :], ALU.subtract).then_inc(s.xl, 1)

    def rms_act(act, s, g):
        square_act(act, s)
        act.wait_ge(s.ssq, s.at.ssq + KT)
        act.activation(LT[:, 3, :], PS[:, 1, :], ACT.Sqrt, bias=EPS[:, 1:2], scale=1.0 / DM).then_inc(s.std, 1)
        for m in range(KT):
            act.wait_ge(s.tmp, s.at.tmp + m + 1)
            act.activation(XH[:, m, :], LT[:, (5, 6, 0, 1)[m % 4], :], ACT.Copy,
                           scale=PCOL[:, g + m:g + m + 1]).then_inc(s.hi, 1)

    def rms_dve(dve, s, g, residual):
        for m in range(KT):
            if residual:
                dve.tensor_tensor(X[:, m, :], X[:, m, :], PS[:, m, :], ALU.add).then_inc(s.cent, 1)
        if not residual:
            dve.drain().then_inc(s.cent, KT)
        dve.wait_ge(s.std, s.at.std + 1)
        dve.reciprocal(LT[:, 4, :], LT[:, 3, :])
        dve.drain()

        def scaled(m):
            dve.tensor_tensor(LT[:, (5, 6, 0, 1)[m % 4], :], X[:, m, :], LT[:, 4, :], ALU.mult).then_inc(s.tmp, 1)

        scaled(0)
        for m in range(KT):
            if m + 1 < KT:
                scaled(m + 1)
                dve.drain()
            dve.wait_ge(s.hi, s.at.hi + m + 1)
            dve.scalar_tensor_tensor(out=XL[:, m, :], in0=LT[:, (5, 6, 0, 1)[m % 4], :], scalar=PCOL[:, g + m:g + m + 1],
                                     in1=XH[:, m, :], op0=ALU.mult, op1=ALU.subtract).then_inc(s.xl, 1)

    def kmajor_pe(pe, name, ah, al, behind=None):
        U, n = size[name]
        if behind is not None:
            pe.wait_ge(*behind)

        def body(i):
            for u in range(2):
                slot = u % 2
                pe.wait_ge(lo_ready, first[name] + u + 1 + 2 * i)
                for k in range(2):
                    for m in range(4):
                        w = slice(k * 512 + m * P, k * 512 + (m + 1) * P)
                        a = (flat(ah[:, ds(2 * i + k, 1), :]), flat(al[:, ds(2 * i + k, 1), :]))
                        begin = isinstance(i, int) and i == 0 and k == 0
                        end = isinstance(i, int) and i == n - 1 and k == 1
                        last = mm3(pe, PS[:, 4 * u + m, :], WH[:, slot, w], WL[:, slot, w], *a, begin, end)
                last.then_inc(unit_done, 1)
            if behind is not None and at_start(i, 0):
                pe.wait_ge(stage_end, 4 * passed["pe"])
        loop(pe, name, body, peel=1, peel_last=True)

    def split_only(fn, e, name):
        def body(i):
            for u in range(size[name][0]):
                ring_step(fn, e, name, i, u)
        loop(e, name, body)

    FH = a_("FH", 0, [P, FT, SEQ], F32R)
    FL = a_("FL", 44, [P, FT, SEQ], F32R)
    UP = a_("UP", 88, [P, 4, SEQ + 8])
    UT = a_("UT", 97, [P, 4, SEQ])
    FY = a_("FY", 105, [P, 2, SEQ])

    ffn_s = shared("ffn", "copied conv silu y hi")

    def ffn_turn():
        return turn(ffn_s, copied=4 + 2 * FT, conv=4 + 2 * FT, silu=2 + FT, y=FT, hi=2 + FT)

    def ffn_up_pe(pe, l, s, tile_ready):
        name = f"up{l}"

        def body(i):
            for u in range(4):
                if not at_start(i, 0):
                    pe.wait_ge(s.copied, s.at.copied + 4 * i + u + 1)
                unit_fm(pe, first[name], 4, i, u, PS[:, u, :], XH, XL, tile_ready)
        loop(pe, name, body, peel=1)

    def ffn_up_act(act, l, s):
        name = f"up{l}"
        act.drain().then_inc(s.copied, 4)
        act.drain().then_inc(s.silu, 2)
        act.drain().then_inc(s.hi, 2)

        def body(i):
            for u in range(4):
                ring_step(hi, act, name, i, u)
                act.wait_ge(s.conv, s.at.conv + 4 * i + u + 1)
                act.activation(UP[:, u, 2:2 + SEQ], PS[:, u, :], ACT.Copy).then_inc(s.copied, 1)
                if u % 2:
                    jj = u // 2
                    act.wait_ge(s.conv, s.at.conv + 4 * i + u + 5)
                    act.activation(UT[:, u, :], UT[:, u, :], ACT.Silu).then_inc(s.silu, 1)
                    act.wait_ge(s.y, s.at.y + 2 * i + jj + 1)
                    act.activation(FH[:, ds(2 * i + jj, 1), :], FY[:, jj:jj + 1, :], ACT.Copy).then_inc(s.hi, 1)
        loop(act, name, body)

    def ffn_up_dve(dve, l, s):
        name = f"up{l}"
        dve.memset(UP[:, :, 0:2], 0.0)
        dve.drain().then_inc(s.conv, 4)

        def body(i):
            for u in range(4):
                ring_step(lo, dve, name, i, u)
                jj = u // 2
                j = 2 * i + jj
                col = C_FW + l * 132 + (u % 2) * FT + j
                dve.wait_ge(s.copied, s.at.copied + 4 * i + u + 5)
                tap = [PCOL[:, ds(col + 44 * t, 1)] for t in range(3)]
                bias = PCOL[:, ds(C_FB + l * 44 + (u % 2) * FT + j, 1)]
                dve.tensor_scalar(UT[:, u, :], UP[:, u, 0:SEQ], tap[0], bias, ALU.mult, ALU.add)
                dve.drain()
                dve.scalar_tensor_tensor(out=UT[:, u, :], in0=UP[:, u, 1:1 + SEQ], scalar=tap[1],
                                         in1=UT[:, u, :], op0=ALU.mult, op1=ALU.add)
                dve.drain()
                dve.scalar_tensor_tensor(out=UT[:, u, :], in0=UP[:, u, 2:2 + SEQ], scalar=tap[2],
                                         in1=UT[:, u, :], op0=ALU.mult, op1=ALU.add).then_inc(s.conv, 1)
                if u % 2:
                    dve.wait_ge(s.silu, s.at.silu + j + 3)
                    dve.tensor_tensor(FY[:, jj, :], UT[:, u - 1, :], UT[:, u, :], ALU.mult).then_inc(s.y, 1)
                    dve.wait_ge(s.hi, s.at.hi + j + 3)
                    dve.tensor_tensor(FL[:, ds(j, 1), :], FY[:, jj:jj + 1, :], FH[:, ds(j, 1), :], ALU.subtract)
                    dve.drain()
        loop(dve, name, body)


    XS = a_("XS", 64, [P, NC_, DM])
    YB = a_("YB", 80, [P, NC_, DM])
    BT = a_("BT", 100, [P, NC_, GROUPS * STATE])
    XDT = a_("XDT", 104, [P, NC_, DM])
    XDEC = a_("XDEC", 16, [P, NC_, DM])
    EM = a_("EM", 48, [P, 2, SEQ])
    CBT = a_("CBT", 52, [P, GROUPS, SEQ])
    HS = a_("HS", 56, [P, DM])
    ACST = a_("ACST", 60, [HEADS, SEQ])
    SELB = a_("SELB", 62, [HEADS, 2, P])
    Z = a_("Z", 16, [P, NC_, DM])
    t64 = [TINY[:, 64 * k:64 * (k + 1)] for k in range(8)]

    def heads4(ap):
        return ap.rearrange("p (c h) -> p c h", c=NC_)

    nar = shared("narrow", "fm copied")

    def narrow_pe(pe, s, bank, sw, c0, c1, buf):
        n = c1 - c0
        for k in range(KT):
            last = mm3(pe, PS[0:n, bank, :], sw[0][:, k, c0:c1], sw[1][:, k, c0:c1], XH[:, k, :], XL[:, k, :],
                       k == 0, k == KT - 1)
        last.then_inc(s.fm, 1)
        pe.wait_ge(s.copied, s.at.copied + 1)
        for c in range(NC_):
            last = pe.transpose(PS[:, bank + 1, c * n:(c + 1) * n], buf[0:n, c * P:(c + 1) * P], IDF[0:n, 0:n])
        return last

    def narrow_dve(dve, s, bank, n, buf):
        dve.wait_ge(s.fm, s.at.fm + 1)
        dve.tensor_copy(buf[0:n, :], PS[0:n, bank, :]).then_inc(s.copied, 1)

    nr = [turn(nar, fm=1, copied=1) for _ in range(3)]

    def softplus_dve_b(dve, v, e, w, r, q):
        dve.tensor_scalar(w, e, 1.0, None, ALU.add)
        dve.drain()
        dve.tensor_scalar(r, w, -1.0, None, ALU.add)
        dve.reciprocal(q, w)
        dve.drain()
        dve.tensor_tensor(r, e, r, ALU.subtract)
        dve.drain()
        dve.tensor_tensor(r, r, q, ALU.mult)
        dve.drain()
        dve.tensor_scalar(q, v, 0.0, None, ALU.max)
        dve.drain()
        dve.tensor_tensor(r, r, q, ALU.add)

    sd = sems("sd", "tr ev dt e w ln dta t1 scan t2 tot acs exps cb xdec st h yo ydone")
    V_, E_, W_, R_, Q_, LN_, DTA, DTV = t64
    DEC = a_("DEC", 63, [P, 4, 64])

    def ssd_pe(pe):
        narrow_pe(pe, nr[0], 4, SW[0], 0, 16, ACST).then_inc(sd.dt, 1)
        pe.wait_ge(sd.dta, 1)
        for c in range(NC_):
            last = pe.transpose(PS[0:16, 5, c * P:(c + 1) * P], DTA[:, c * 16:(c + 1) * 16], IDF[:, :])
        last.then_inc(sd.t1, 1)
        pe.matmul(PS[:, 7, 0:64], ONES[:, :], DTA, start=True, stop=True).then_inc(sd.tot, 1)
        for j in range(10):
            if j >= 4:
                pe.wait_ge(sd.ev, j - 3)
            for c in range(NC_):
                src = XSF[:, j, c * P:(c + 1) * P] if j < 8 else BF[:, j - 8, c * P:(c + 1) * P]
                last = pe.transpose(PS[:, j % 4, c * P:(c + 1) * P], src, IDF[:, :])
            last.then_inc(sd.tr, 1)
        pe.wait_ge(sd.scan, 1)
        for c in range(NC_):
            last = pe.transpose(PS[:, 6, c * 16:(c + 1) * 16], ACST[0:16, c * P:(c + 1) * P], IDF[0:16, 0:16])
        last.then_inc(sd.t2, 1)
        pe.wait_ge(sd.ev, 10)
        for g in range(GROUPS):
            for c in range(NC_):
                last = pe.matmul(PS[:, g, c * P:(c + 1) * P], BF[:, g, c * P:(c + 1) * P],
                                 CF[:, g, c * P:(c + 1) * P], start=True, stop=True)
        last.then_inc(sd.cb, 1)
        pe.wait_ge(sd.xdec, 1)
        for c in range(NC_):
            if c < NC_ - 1:
                if c:
                    pe.wait_ge(sd.h, c)
                for g in range(GROUPS):
                    last = pe.matmul(PS[:, 2 + g, :], BT[:, c, g * STATE:(g + 1) * STATE],
                                     XDEC[:, c, g * 512:(g + 1) * 512], start=True, stop=True)
                last.then_inc(sd.st, 1)
            if c:
                pe.wait_ge(sd.h, c)
                if c > 1:
                    pe.wait_ge(sd.ydone, c)
                for g in range(GROUPS):
                    last = pe.matmul(PS[:, 4 + g, :], CF[:, g, c * P:(c + 1) * P],
                                     HS[:, g * 512:(g + 1) * 512], start=True, stop=True)
                last.then_inc(sd.yo, 1)

    def ssd_act(act):
        act.wait_ge(sd.e, 1)
        act.activation(E_, V_, ACT.Abs)
        act.drain()
        act.activation(E_, E_, ACT.Exp, scale=-1.0)
        act.activation(BCP[:, 752:768], BCP[:, B_ALOG:B_ALOG + 16], ACT.Exp)
        act.drain().then_inc(sd.w, 1)
        act.wait_ge(sd.ln, 1)
        act.activation(LN_, W_, ACT.Ln).then_inc(sd.ln, 1)
        act.wait_ge(sd.acs, 1)
        for k in range(3):
            last = act.activation(DEC[:, k, :], DEC[:, k, :], ACT.Exp)
        last.then_inc(sd.exps, 1)

    def ssd_dve(dve):
        dve.wait_ge(su.bc, 16 * len(BCAST))
        narrow_dve(dve, nr[0], 4, 16, ACST)
        dve.wait_ge(sd.dt, 1)
        dve.tensor_tensor(heads4(V_), heads4(PS[:, 5, 0:64]),
                          BCP[:, B_DTB:B_DTB + 16].unsqueeze(1).to_broadcast([P, NC_, 16]), ALU.add)
        dve.drain()
        dve.drain().then_inc(sd.e, 1)
        dve.wait_ge(sd.w, 1)
        dve.tensor_copy(BCP[:, B_ALOG:B_ALOG + 16], BCP[:, 752:768])
        softplus_dve_b(dve, V_, E_, W_, R_, Q_)
        dve.drain().then_inc(sd.ln, 1)
        dve.wait_ge(sd.ln, 2)
        dve.tensor_tensor(DTV, R_, LN_, ALU.add)
        dve.drain()
        dve.scalar_tensor_tensor(out=heads4(DTA), in0=heads4(DTV), scalar=-1.0,
                                 in1=BCP[:, B_ALOG:B_ALOG + 16].unsqueeze(1).to_broadcast([P, NC_, 16]),
                                 op0=ALU.mult, op1=ALU.mult)
        dve.drain().then_inc(sd.dta, 1)
        dve.wait_ge(sd.t1, 1)
        for c in range(NC_):
            dve.tensor_tensor_scan(ACST[0:16, c * P:(c + 1) * P], ONES[0:16, :], PS[0:16, 5, c * P:(c + 1) * P],
                                   0.0, ALU.mult, ALU.add)
        dve.drain().then_inc(sd.scan, 1)
        for j in range(10):
            dve.wait_ge(sd.tr, j + 1)
            dst = XS[:, :, j * P:(j + 1) * P] if j < 8 else BT[:, :, (j - 8) * P:(j - 7) * P]
            dve.tensor_copy(dst, PS[:, j % 4, :].rearrange("p (c t) -> p c t", c=NC_)).then_inc(sd.ev, 1)
        dve.wait_ge(sd.t2, 1)
        dve.wait_ge(sd.tot, 1)
        dve.tensor_copy(DEC[:, 2, :], PS[:, 6, 0:64])
        dve.tensor_copy(DEC[:, 1, :], PS[:, 7, 0:64])
        dve.drain()
        dve.tensor_scalar(DEC[:, 3, :], DEC[:, 2, :], -1.0, None, ALU.mult)
        dve.tensor_tensor(DEC[:, 0, :], DEC[:, 1, :], DEC[:, 2, :], ALU.subtract)
        dve.drain().then_inc(sd.acs, 1)

        def per_head(ap):
            return ap.unsqueeze(2).to_broadcast([P, HEADS, HD])

        def by_head(ap):
            return ap.rearrange("p (h d) -> p h d", h=HEADS)

        for c in range(NC_):
            dve.tensor_tensor(by_head(XDT[:, c, :]), by_head(XS[:, c, :]), per_head(DTV[:, c * 16:(c + 1) * 16]),
                              ALU.mult)
        dve.wait_ge(sd.exps, 1)
        dve.wait_ge(sd.cb, 1)
        for g in range(GROUPS):
            dve.tensor_copy(CBT[:, g, :], PS[:, g, :])
        dve.drain()
        for c in range(NC_):
            dve.tensor_tensor(by_head(XDEC[:, c, :]), by_head(XDT[:, c, :]),
                              per_head(DEC[:, 0, c * 16:(c + 1) * 16]), ALU.mult)
            dve.tensor_tensor(by_head(YB[:, c, :]), by_head(XS[:, c, :]), per_head(BCP[:, B_D:B_D + 16]), ALU.mult)
        dve.drain().then_inc(sd.xdec, 1)
        for c in range(NC_):
            if c:
                dve.wait_ge(sd.yo, c)
                for g in range(GROUPS):
                    half = XS[:, c, g * 512:(g + 1) * 512]
                    dve.tensor_tensor(half.rearrange("p (h d) -> p h d", h=8),
                                      PS[:, 4 + g, :].rearrange("p (h d) -> p h d", h=8),
                                      DEC[:, 2, c * 16 + 8 * g:c * 16 + 8 * g + 8].unsqueeze(2)
                                      .to_broadcast([P, 8, HD]), ALU.mult)
                dve.drain().then_inc(sd.ydone, 2 if c == 1 else 1)
                dve.tensor_tensor(YB[:, c, :], YB[:, c, :], XS[:, c, :], ALU.add)
            if c < NC_ - 1:
                dve.wait_ge(sd.st, c + 1)
                new = PS[:, 2:4, :].rearrange("p a b -> p (a b)")
                if c == 0:
                    dve.tensor_copy(HS[:, :], new)
                else:
                    dve.tensor_tensor(by_head(HS[:, :]), by_head(HS[:, :]),
                                      per_head(DEC[:, 1, c * 16:(c + 1) * 16]), ALU.mult)
                    dve.drain()
                    dve.tensor_tensor(HS[:, :], HS[:, :], new, ALU.add)
                dve.drain().then_inc(sd.h, 1)

    sh = sems("sh", "sel bc e m y yd")

    def ssdh_pe(pe):
        with pe.Fori(0, GROUPS) as g:
            for i in range(4):
                n = 8 * g + 2 * i
                for hh in range(2):
                    pe.wait_ge(sh.sel, n + hh + 1)
                    pe.wait_ge(sh.e, n + hh + 1)
                    pe.matmul(PS[:, hh, :], SELB[:, hh, :], ACST[:, :], start=True, stop=False)
                    for c in range(NC_):
                        last = pe.matmul(PS[:, hh, c * P:(c + 1) * P], IDB[:, :], MCOL[:, :], start=False,
                                         stop=c == NC_ - 1)
                    last.then_inc(sh.bc, 1)

                def free(c):
                    pe.wait_ge(zs.left, zs.at.left + 4 * g + c + 1)
                unit_tm(pe, first["z"], 4, g, i, lambda c: PS[:, 4 + c, :], 2 * i, free)
                for hh in range(2):
                    pe.wait_ge(sh.m, n + hh + 1)
                    pe.wait_ge(sh.yd, n + hh + 1)
                    for c in range(NC_):
                        last = pe.matmul(PS[:, 2 + hh, c * HD:(c + 1) * HD], EM[:, hh, c * P:(c + 1) * P],
                                         XDT[:, c, ds((n + hh) * HD, HD)], start=True, stop=True)
                    last.then_inc(sh.y, 1)

    def ssdh_act(act):
        act.drain().then_inc(sh.e, 2)
        act.drain().then_inc(zs.left, 4)
        with act.Fori(0, GROUPS) as g:
            for i in range(4):
                n = 8 * g + 2 * i
                for hh in range(2):
                    act.wait_ge(sh.bc, n + hh + 1)
                    act.wait_ge(sh.yd, n + hh + 1)
                    for c in range(NC_):
                        last = act.activation(EM[:, hh, c * P:(c + 1) * P], PS[:, hh, c * P:(c + 1) * P], ACT.Exp,
                                              bias=DEC[:, 3, ds(c * 16 + n + hh, 1)])
                    last.then_inc(sh.e, 1)
                hi(act, first["z"], 4, g, i)
            act.wait_ge(unit_done, first["z"] + 4 * g + 4)
            for c in range(NC_):
                act.activation(Z[:, c, ds(512 * g, 512)], PS[:, 4 + c, :], ACT.Silu).then_inc(zs.left, 1)

    def ssdh_dve(dve):
        dve.drain().then_inc(sh.yd, 2)
        with dve.Fori(0, GROUPS) as g:
            for i in range(4):
                n = 8 * g + 2 * i
                for hh in range(2):
                    dve.tensor_copy(SELB[:, hh, :],
                                    IDF[0:16, ds(n + hh, 1)].to_broadcast([HEADS, P])).then_inc(sh.sel, 1)
                for hh in range(2):
                    dve.wait_ge(sh.e, n + hh + 3)
                    dve.tensor_tensor(EM[:, hh:hh + 1, :], EM[:, hh:hh + 1, :], CBT[:, ds(g, 1), :],
                                      ALU.mult).then_inc(sh.m, 1)
                lo(dve, first["z"], 4, g, i)
                for hh in range(2):
                    dve.wait_ge(sh.y, n + hh + 1)
                    y = YB[:, :, ds((n + hh) * HD, HD)]
                    dve.tensor_tensor(y, y, PS[:, 2 + hh, 0:256].rearrange("p (c d) -> p c d", c=NC_),
                                      ALU.add)
                    dve.drain().then_inc(sh.yd, 1)

    def tm_pe(pe, name, s, behind=None, tile_ready=None):
        for q in range(size[name][1]):
            def free(c):
                if q >= 2 or behind == "tm":
                    pe.wait_ge(s.left, s.at.left + 4 * (q - 2) + c + 1)
                elif q == 0 and behind == "fm":
                    pe.wait_ge(s.left, s.at.left)
            for u in range(4):
                unit_tm(pe, first[name] + 4 * q, 4, 0, u, lambda c: PS[:, 4 * (q % 2) + c, :], 2 * u, free,
                        tile_ready if q == 0 else None)

    def tm_copies(act, name, s, dst, q):
        act.wait_ge(unit_done, first[name] + 4 * q + 4)
        for c in range(NC_):
            act.activation(dst[:, c, 512 * q:512 * q + 512], PS[:, 4 * (q % 2) + c, :], ACT.Copy).then_inc(s.left, 1)

    def tm_act(act, name, s, dst, beside=None):
        for q in range(size[name][1]):
            for u in range(4):
                ring_step(hi, act, name, q, u)
                if beside is not None:
                    beside(act, 4 * q + u)
            tm_copies(act, name, s, dst, q)

    left_s = shared("left", "left")
    zs = turn(left_s, left=4 + 8)
    gn = sems("gn", "u ss std n tr hi lo")

    def gnorm_pe(pe):
        for f in range(KT):
            pe.wait_ge(gn.n, f // 4 + 1)
            if f >= 4:
                pe.wait_ge(gn.lo, f - 3)
            for c in range(NC_):
                last = pe.transpose(PS[:, f % 4, c * P:(c + 1) * P], YB[:, c, f * P:(f + 1) * P], IDF[:, :])
            last.then_inc(gn.tr, 1)

    def gnorm_act(act):
        for g in range(GROUPS):
            for c in range(NC_):
                act.wait_ge(gn.u, g * NC_ + c + 1)
                act.activation(XS[:, c, g * 512:(g + 1) * 512], YB[:, c, g * 512:(g + 1) * 512], ACT.Square,
                               accum_out=TINY[:, g * NC_ + c:g * NC_ + c + 1])
        act.drain()
        act.activation(TINY[:, 8:16], TINY[:, 0:8], ACT.Sqrt, bias=EPS[:, 0:1], scale=1.0 / 512).then_inc(gn.std, 1)
        for f in range(KT):
            act.wait_ge(gn.tr, f + 1)
            act.activation(YH[:, 8 + f, :], PS[:, f % 4, :], ACT.Copy,
                           scale=PCOL[:, C_NG + f:C_NG + f + 1]).then_inc(gn.hi, 1)

    def gnorm_dve(dve):
        for g in range(GROUPS):
            for c in range(NC_):
                seg = YB[:, c, g * 512:(g + 1) * 512]
                dve.tensor_tensor(seg, seg, Z[:, c, g * 512:(g + 1) * 512], ALU.mult).then_inc(gn.u, 1)
        dve.wait_ge(gn.std, 1)
        dve.reciprocal(TINY[:, 16:24], TINY[:, 8:16])
        dve.drain()
        for g in range(GROUPS):
            for c in range(NC_):
                seg = YB[:, c, g * 512:(g + 1) * 512]
                dve.tensor_scalar(seg, seg, TINY[:, 16 + g * NC_ + c:17 + g * NC_ + c], None, ALU.mult)
            dve.drain().then_inc(gn.n, 1)
        for f in range(KT):
            dve.wait_ge(gn.hi, f + 1)
            dve.scalar_tensor_tensor(out=YL[:, 8 + f, :], in0=PS[:, f % 4, :], scalar=PCOL[:, C_NG + f:C_NG + f + 1],
                                     in1=YH[:, 8 + f, :], op0=ALU.mult, op1=ALU.subtract).then_inc(gn.lo, 1)

    def foxqk_pe(pe):
        name, s = "foxqk", fq

        def body(i):
            for u in range(2):
                if not at_start(i, 0):
                    pe.wait_ge(s.left, s.at.left + 2 * i + u + 1)
                unit_fm(pe, first[name], 2, i, u, PS[:, u, :], XH, XL, normed(pe, n1))
            if at_start(i, 0):
                narrow_pe(pe, nr[1], 4, SW[0], 16, 32, NCUM).then_inc(fg.f, 1)
        loop(pe, name, body, peel=1)

    attn_s = shared("attn", "qz sc mx ex cb tr pt pv ov")
    NP = 4
    LAG = 3

    def attn_turn(loops, n, slots):
        m = loops * n
        return turn(attn_s, qz=loops, sc=m, mx=m, ex=m + slots, tr=m, pt=m, pv=m + 2, ov=m // NC_ + 2)

    def scores_pe(pe, bank, q, k, qb):
        n = (qb + 1) * P
        pe.matmul(PS[:, bank, 0:n], q, k(n), start=True, stop=False)
        return pe.matmul(PS[:, bank, qb * P:n], IDB[:, :], MROW[:, :], start=False, stop=True)

    def attn_pe(pe, s, loops, n, slots, scores, pblock, PTx, value, ready, width):
        pe.drain().then_inc(s.pv, 2)
        with pe.Fori(0, loops) as i:
            B = i * n
            pe.wait_ge(s.qz, s.at.qz + i + 1)
            for t in range(n + LAG + 1):
                if t < n:
                    if slots <= LAG:
                        pe.wait_ge(s.ex, s.at.ex + B + t + 1)
                    scores(i, t).then_inc(s.sc, 1)
                if LAG <= t < n + LAG:
                    k = t - LAG
                    pe.wait_ge(ready[0], ready[1] + B + k)
                    for b in range(k % 4 + 1):
                        last = pe.transpose(PS[:, 4 + k % 2, b * P:(b + 1) * P], pblock(k, b), IDF[:, :])
                    last.then_inc(s.tr, 1)
                if t > LAG:
                    k = t - LAG - 1
                    pe.wait_ge(s.pt, s.at.pt + B + k + 1)
                    if k % NC_ == 0:
                        pe.wait_ge(s.ov, s.at.ov + (n // NC_) * i + k // NC_ + 1)
                    o = slice((k % NC_) * width, (k % NC_ + 1) * width)
                    for b in range(k % 4 + 1):
                        last = pe.matmul(PS[:, 6 + k // NC_ % 2, o], PTx[:, k % 2, b * P:(b + 1) * P], value(i, k, b),
                                         start=b == 0, stop=b == k % 4)
                    last.then_inc(s.pv, 1)

    def attn_act(act, s, loops, n, slots, queries, exps, PTx):
        act.drain().then_inc(s.ex, slots)
        with act.Fori(0, loops) as i:
            B = i * n
            queries(i).then_inc(s.qz, 1)
            for t in range(n + LAG):
                if t >= LAG:
                    k = t - LAG
                    act.wait_ge(s.tr, s.at.tr + B + k + 1)
                    act.wait_ge(s.pv, s.at.pv + B + k + 1)
                    w = (k % 4 + 1) * P
                    act.activation(PTx[:, k % 2, 0:w], PS[:, 4 + k % 2, 0:w], ACT.Copy).then_inc(s.pt, 1)
                if t < n:
                    act.wait_ge(s.mx, s.at.mx + B + t + 1)
                    exps(t).then_inc(s.ex, 1)

    def attn_dve(dve, s, loops, n, maxima, output, combine=None):
        dve.drain().then_inc(s.ov, 2)
        with dve.Fori(0, loops) as i:
            B = i * n
            for t in range(n + LAG + 2):
                if t < n:
                    dve.wait_ge(s.sc, s.at.sc + B + t + 1)
                    maxima(t).then_inc(s.mx, 1)
                if combine is not None and 1 <= t <= n:
                    combine(B, t - 1).then_inc(s.cb, 1)
                k = t - LAG - 2
                if k >= 0 and k % NC_ == NC_ - 1:
                    dve.wait_ge(s.pv, s.at.pv + B + k + 3)
                    output(i, k // NC_).then_inc(s.ov, 1)

    def one_softmax(act, dve, PBx):
        def exps(t):
            w = (t % 4 + 1) * P
            return act.activation(PBx(t, 0, w), PS[:, t % 4, 0:w], ACT.Exp, bias=NM[:, t % 4:t % 4 + 1],
                                  accum_out=RS[:, t % 16:t % 16 + 1])

        def maxima(t):
            w = (t % 4 + 1) * P
            return dve.tensor_reduce(NM[:, t % 4:t % 4 + 1], PS[:, t % 4, 0:w], AX, ALU.max, negate=True)
        return exps, maxima

    KZ = a_("KZ", 0, [P, HEADS, SEQ])
    VT = a_("VT", 32, [P, NC_, DM])
    OB = a_("OB", 48, [P, NC_, DM])
    QT = a_("QT", 64, [P, KT, SEQ])
    QZ = a_("QZ", 80, [P, 4, SEQ])
    PB = a_("PB", 88, [P, NP, SEQ])
    PT = a_("PT", 96, [P, 2, SEQ])
    NCUM = a_("NCUM", 100, [HEADS, SEQ])
    ONE16 = a_("ONE16", 102, [HEADS, SEQ])
    fq = turn(left_s, left=2 + 16)
    fv = turn(left_s, left=8)
    fg = sems("fg", "f w ln sp t1 cum row")
    fa = attn_turn(4, 16, 4)

    def foxqk_act(act):
        def step(i, u):
            ring_step(hi, act, "foxqk", i, u)
            act.wait_ge(unit_done, first["foxqk"] + 2 * i + u + 1)
        with act.Fori(0, 4) as i:
            for u in range(2):
                step(i, u)
                act.activation(QT[:, ds(2 * i + u, 1), :], PS[:, u:u + 1, :], ACT.Copy,
                               scale=SCALE).then_inc(fq.left, 1)
        with act.Fori(4, 8) as i:
            for u in range(2):
                step(i, u)
                for hh in range(2):
                    last = act.activation(KZ[0:HD, ds(4 * i + (2 * u + hh - 16), 1), :],
                                          PS[hh * HD:(hh + 1) * HD, u:u + 1, :], ACT.Copy)
                last.then_inc(fq.left, 1)

    def foxqk_stage_act(act):
        act.drain().then_inc(fq.left, 2)
        act.wait_ge(fg.w, 1)
        act.activation(E_, V_, ACT.Abs)
        act.drain()
        act.activation(E_, E_, ACT.Exp, scale=-1.0).then_inc(fg.ln, 1)
        act.wait_ge(fg.w, 2)
        act.activation(LN_, W_, ACT.Ln).then_inc(fg.ln, 1)
        foxqk_act(act)

    def foxqk_stage_dve(dve):
        narrow_dve(dve, nr[1], 4, 16, NCUM)
        dve.wait_ge(fg.f, 1)
        dve.tensor_tensor(heads4(V_), heads4(PS[:, 5, 0:64]),
                          BCP[:, B_BF:B_BF + 16].unsqueeze(1).to_broadcast([P, NC_, 16]), ALU.add)
        dve.drain()
        dve.tensor_scalar(V_, V_, -1.0, None, ALU.mult)
        dve.drain().then_inc(fg.w, 1)
        dve.wait_ge(fg.ln, 1)
        softplus_dve_b(dve, V_, E_, W_, R_, Q_)
        dve.drain().then_inc(fg.w, 1)
        dve.wait_ge(fg.ln, 2)
        dve.tensor_tensor(DTA, R_, LN_, ALU.add).then_inc(fg.sp, 1)
        split_only(lo, dve, "foxqk")

    def foxv_stage_pe(pe):
        pe.wait_ge(fg.sp, 1)
        for c in range(NC_):
            last = pe.transpose(PS[0:16, 5, c * P:(c + 1) * P], DTA[:, c * 16:(c + 1) * 16], IDF[:, :])
        last.then_inc(fg.t1, 1)
        tm_pe(pe, "foxv", fv, "fm")

    def foxv_stage_act(act):
        act.wait_ge(fg.cum, 1)
        act.dma_start(KZ[HD:HD + 1, :, :], NCUM[:, :]).then_inc(fg.row, 16)
        tm_act(act, "foxv", fv, VT)

    def foxv_stage_dve(dve):
        dve.memset(ONE16[:, :], 1.0)
        dve.drain()
        dve.wait_ge(fg.t1, 1)
        dve.tensor_tensor_scan(NCUM[:, :], ONE16[:, :], PS[0:16, 5, :], 0.0, ALU.mult, ALU.add)
        dve.drain().then_inc(fg.cum, 1)
        split_only(lo, dve, "foxv")

    def lower_rows(pool):
        pool.memset(QZ[HD:P, :, :], 1.0)
        pool.memset(KZ[HD:P, :, :], 0.0)

    def fox_pe(pe):
        pe.wait_ge(fg.row, 16)
        attn_pe(pe, fa, 4, 16, 4,
                lambda i, t: scores_pe(pe, t % 4, QZ[:, t // 4, (t % 4) * P:(t % 4 + 1) * P],
                                       lambda n: flat(KZ[:, ds(4 * i + t // 4, 1), 0:n]), t % 4),
                lambda k, b: PB[:, k % NP, b * P:(b + 1) * P], PT,
                lambda i, k, b: VT[:, b, ds(i * 256 + (k // 4) * HD, HD)], (fa.ex, fa.at.ex + 4 + 1), HD)

    def head_queries(act, QZx, src, i):
        for h in range(4):
            last = act.activation(QZx[0:HD, h:h + 1, :], src[(h % 2) * HD:(h % 2 + 1) * HD, ds(2 * i + h // 2, 1), :],
                                  ACT.Copy)
        return last

    def fox_act(act):
        exps, _ = one_softmax(act, None, lambda t, a, b: PB[:, t % NP, a:b])
        attn_act(act, fa, 4, 16, 4, lambda i: head_queries(act, QZ, QT, i), exps, PT)

    def fox_dve(dve):
        def output(i, h):
            rw = RW[:, 4 * (h % 2):4 * (h % 2) + 4]
            dve.reciprocal(rw, RS[:, 4 * (h % 4):4 * (h % 4) + 4])
            dve.drain()
            return dve.tensor_tensor(OB[:, :, ds(i * 256 + h * HD, HD)],
                                     PS[:, 6 + h % 2, 0:256].rearrange("p (c d) -> p c d", c=NC_),
                                     rw.unsqueeze(2).to_broadcast([P, NC_, HD]), ALU.mult)
        _, maxima = one_softmax(None, dve, None)
        attn_dve(dve, fa, 4, 16, maxima, output)

    split_s = shared("split", "tr hi lo")

    def split_fm(src, dh, dl, gain=None, const=1.0):
        s = turn(split_s, tr=KT, hi=KT, lo=KT)

        def f_pe(pe):
            for f in range(KT):
                if f >= 4:
                    pe.wait_ge(s.lo, s.at.lo + f - 3)
                for c in range(NC_):
                    last = pe.transpose(PS[:, f % 4, c * P:(c + 1) * P], src[:, c, f * P:(f + 1) * P], IDF[:, :])
                last.then_inc(s.tr, 1)

        def f_act(act):
            for f in range(KT):
                act.wait_ge(s.tr, s.at.tr + f + 1)
                act.activation(dh[:, f, :], PS[:, f % 4, :], ACT.Copy,
                               scale=const if gain is None else gain).then_inc(s.hi, 1)

        def f_dve(dve):
            for f in range(KT):
                dve.wait_ge(s.hi, s.at.hi + f + 1)
                dve.scalar_tensor_tensor(out=dl[:, f, :], in0=PS[:, f % 4, :],
                                         scalar=const if gain is None else gain,
                                         in1=dh[:, f, :], op0=ALU.mult, op1=ALU.subtract).then_inc(s.lo, 1)
        return f_pe, f_act, f_dve, None

    OH = a_("OH", 0, [P, KT, SEQ], F32R)
    OL = a_("OL", 16, [P, KT, SEQ], F32R)

    def rope_tables_pool(pool, RAB, TABC, gain, s):
        g = BCP[:, gain:gain + HD]
        h = HD // 2
        for c in range(NC_):
            pool.tensor_tensor(RAB[:, c, 0, :], TABC[:, c, 0, :], g, ALU.mult)
            pool.tensor_tensor(RAB[:, c, 1, 0:h], TABC[:, c, 1, 0:h], g[:, h:HD], ALU.mult)
            pool.tensor_tensor(RAB[:, c, 1, h:HD], TABC[:, c, 1, h:HD], g[:, 0:h], ALU.mult)
        pool.drain().then_inc(s, 1)

    def rope_chunk(dve, t, out_, nh, RAB, c, ss, TMP):
        h = HD // 2
        tmp = TMP[:, 0:nh * HD].rearrange("p (h d) -> p h d", h=nh)
        dve.tensor_tensor(t, t, ss.unsqueeze(2).to_broadcast([P, nh, HD]), ALU.mult)
        dve.drain()
        for a, b in ((0, h), (h, 0)):
            dve.tensor_tensor(tmp[:, :, a:a + h], t[:, :, b:b + h],
                              RAB[:, c, 1, a:a + h].unsqueeze(1).to_broadcast([P, nh, h]), ALU.mult)
        dve.drain()
        dve.tensor_tensor(t, t, RAB[:, c, 0, :].unsqueeze(1).to_broadcast([P, nh, HD]), ALU.mult)
        dve.drain()
        dve.tensor_tensor(out_, t, tmp, ALU.add)
        dve.drain()

    def head_ss_chunk(dve, t, ss, TMP):
        _, nh, w = t.shape
        tmp = TMP[:, 0:nh * w].rearrange("p (h d) -> p h d", h=nh)
        dve.tensor_tensor(tmp, t, t, ALU.mult)
        dve.drain()
        dve.tensor_reduce(ss, tmp, AX, ALU.add)
        dve.drain()

    def heads_of(T, c0=0, c1=DM):
        return lambda c: per(T[:, c, c0:c1], (c1 - c0) // HD)

    rope_s = shared("rope", "tab ss rt")
    tabs = sem("tabs")

    def load_table(act, TABC):
        act.dma_start(TABC[:, :, :, :], A["rope_tok"]).then_inc(tabs, 16)

    def rope_stage(items, TABC, TMP, tabs_at, load=False):
        s = turn(rope_s, tab=len(items), ss=1, rt=1)
        at = [0]
        for it in items:
            at.append(at[-1] + NC_ * it[1])

        def f_pool(pool):
            pool.wait_ge(tabs, tabs_at)
            for _, _, RAB, gain in items:
                rope_tables_pool(pool, RAB, TABC, B_GAIN[gain], s.tab)

        def f_act(act):
            if load:
                load_table(act, TABC)
            act.wait_ge(s.ss, s.at.ss + 1)
            act.activation(TINY[:, 256:256 + at[-1]], TINY[:, 0:at[-1]], ACT.Sqrt, bias=EPS[:, 1:2],
                           scale=1.0 / HD).then_inc(s.rt, 1)

        def f_dve(dve):
            for k, (T, nh, _, _) in enumerate(items):
                for c in range(NC_):
                    head_ss_chunk(dve, T(c), TINY[:, at[k] + c * nh:at[k] + (c + 1) * nh], TMP)
            dve.drain().then_inc(s.ss, 1)
            dve.wait_ge(s.rt, s.at.rt + 1)
            dve.reciprocal(TINY[:, 0:at[-1]], TINY[:, 256:256 + at[-1]])
            dve.wait_ge(s.tab, s.at.tab + len(items))
            dve.drain()
            for k, (T, nh, RAB, _) in enumerate(items):
                for c in range(NC_):
                    rope_chunk(dve, T(c), T(c), nh, RAB, c, TINY[:, at[k] + c * nh:at[k] + (c + 1) * nh], TMP)
        return None, f_act, f_dve, f_pool

    fm_s = shared("fm", "tr ev")

    def to_fm(items, act_too=None, dve_too=None, pool_too=None):
        s = turn(fm_s, tr=len(items), ev=len(items))

        def f_pe(pe):
            for k, (src, _, _) in enumerate(items):
                if k >= 4:
                    pe.wait_ge(s.ev, s.at.ev + k - 3)
                for c in range(NC_):
                    last = pe.transpose(PS[:, k % 4, c * P:(c + 1) * P], src(c), IDF[:, :])
                last.then_inc(s.tr, 1)

        def f_act(act):
            for k, (_, dst, scale) in enumerate(items):
                act.wait_ge(s.tr, s.at.tr + k + 1)
                if isinstance(dst, tuple):
                    for h, d in enumerate(dst):
                        last = act.activation(d[0:HD, :], PS[h * HD:(h + 1) * HD, k % 4, :], ACT.Copy)
                    last.then_inc(s.ev, 1)
                else:
                    act.activation(dst, PS[:, k % 4, :], ACT.Copy, scale=scale).then_inc(s.ev, 1)
            if act_too is not None:
                act_too(act)
        return f_pe, f_act, dve_too, pool_too

    def per(ap, n):
        return ap.rearrange("p (h d) -> p h d", h=n)

    TQ = a_("TQ", 0, [P, NC_, DM])
    TK = a_("TK", 16, [P, NC_, DM])
    DV = a_("DV", 32, [P, NC_, DM])
    DQF = a_("DQF", 48, [P, KT, SEQ])
    DKF = a_("DKF", 64, [P, KT, SEQ])
    OD = a_("OD", 16, [P, NC_, DM])
    TABD = a_("TABD", 80, [P, NC_, 2, HD])
    RABQ = a_("RABQ", 82, [P, NC_, 2, HD])
    RABK = a_("RABK", 84, [P, NC_, 2, HD])
    TMPD = a_("TMPD", 86, [P, DM])
    QZD = a_("QZD", 80, [P, 4, SEQ])
    PBD = a_("PBD", 88, [P, 2 * NP, SEQ])
    PTD = a_("PTD", 104, [P, 2, SEQ])
    YDH = a_("YDH", 88, [P, KT, SEQ], F32R)
    YDL = a_("YDL", 104, [P, KT, SEQ], F32R)
    dq, dk, dvs = (turn(left_s, left=8) for _ in range(3))
    dl = sems("dl", "a b")
    da = attn_turn(4, 8, 2)

    def lam_dve(dve):
        for k in range(2):
            dve.tensor_tensor(TINY[:, 64 * k:64 * k + 64], BCP[:, B_LAM + 128 * k:B_LAM + 128 * k + 64],
                              BCP[:, B_LAM + 128 * k + 64:B_LAM + 128 * k + 128], ALU.mult)
        dve.drain()
        dve.tensor_reduce(LAM[:, 1:3], TINY[:, 0:128].rearrange("p (k d) -> p k d", k=2), AX, ALU.add)
        dve.drain().then_inc(dl.a, 1)
        dve.wait_ge(dl.b, 1)
        dve.tensor_tensor(LAM[:, 0:1], LAM[:, 4:5], LAM[:, 3:4], ALU.subtract)
        dve.drain()
        dve.tensor_scalar(LAM[:, 0:1], LAM[:, 0:1], -LAMBDA_INIT, None, ALU.add)
        dve.drain()

    def lam_act(act):
        act.wait_ge(dl.a, 1)
        act.activation(LAM[:, 3:5], LAM[:, 1:3], ACT.Exp).then_inc(dl.b, 1)

    def zero_halves(pool):
        for r in range(4):
            half = slice(HD, P) if r % 2 == 0 else slice(0, HD)
            pool.memset(QZD[half, r, :], 0.0)

    def diff_queries(act, i):
        for r in range(4):
            half = slice((r % 2) * HD, (r % 2 + 1) * HD)
            last = act.activation(QZD[half, r:r + 1, :], DQF[half, ds(2 * i + r // 2, 1), :], ACT.Copy)
        return last

    def diff_pe(pe):
        def both(i, t):
            for hh in range(2):
                last = scores_pe(pe, 2 * (t % 2) + hh, QZD[:, 2 * (t // 4) + hh, (t % 4) * P:(t % 4 + 1) * P],
                                 lambda n: flat(DKF[:, ds(2 * i + t // 4, 1), 0:n]), t % 4)
            return last
        attn_pe(pe, da, 4, 8, 2, both, lambda k, b: PBD[:, 2 * (k % NP), b * P:(b + 1) * P], PTD,
                lambda i, k, b: DV[:, b, ds(i * 256 + (k // 4) * P, P)], (da.cb, da.at.cb + 1), P)

    def diff_act(act):
        def exps(t):
            w = (t % 4 + 1) * P
            for hh in range(2):
                r, q = 2 * (t % 2) + hh, 2 * (t % NP) + hh
                last = act.activation(PBD[:, q, 0:w], PS[:, r, 0:w], ACT.Exp, bias=NM[:, r:r + 1],
                                      accum_out=RS[:, q:q + 1])
            return last
        attn_act(act, da, 4, 8, 2, lambda i: diff_queries(act, i), exps, PTD)

    def diff_dve(dve):
        def maxima(t):
            for hh in range(2):
                r = 2 * (t % 2) + hh
                last = dve.tensor_reduce(NM[:, r:r + 1], PS[:, r, 0:(t % 4 + 1) * P], AX, ALU.max, negate=True)
            return last

        def combine(B, t):
            w, q = (t % 4 + 1) * P, 2 * (t % NP)
            dve.wait_ge(da.ex, da.at.ex + B + t + 3)
            dve.reciprocal(RW[:, q:q + 2], RS[:, q:q + 2])
            dve.drain()
            dve.tensor_scalar(RW[:, q + 1:q + 2], RW[:, q + 1:q + 2], LAM[:, 0:1], None, ALU.mult)
            dve.tensor_scalar(PBD[:, q, 0:w], PBD[:, q, 0:w], RW[:, q:q + 1], None, ALU.mult)
            dve.drain()
            return dve.scalar_tensor_tensor(out=PBD[:, q, 0:w], in0=PBD[:, q + 1, 0:w], scalar=RW[:, q + 1:q + 2],
                                            in1=PBD[:, q, 0:w], op0=ALU.mult, op1=ALU.add)

        def output(i, h):
            return dve.tensor_copy(OD[:, :, ds(i * 256 + h * P, P)],
                                   PS[:, 6 + h % 2, :].rearrange("p (c d) -> p c d", c=NC_))
        attn_dve(dve, da, 4, 8, maxima, output, combine)

    sl = sems("sl", "ss rt")
    TMPS = a_("TMPS", 32, [P, DM])

    def subln_act(act, step):
        if step == NC_:
            act.wait_ge(sl.ss, 1)
            act.activation(TINY[:, 64:96], TINY[:, 0:32], ACT.Sqrt, bias=EPS[:, 1:2], scale=1.0 / P).then_inc(sl.rt, 1)

    def subln_dve(dve, step):
        def head(c):
            return per(OD[:, c, :], 8)
        if step < NC_:
            head_ss_chunk(dve, head(step), TINY[:, 8 * step:8 * step + 8], TMPS)
            if step == NC_ - 1:
                dve.drain().then_inc(sl.ss, 1)
            return
        if step == NC_:
            dve.wait_ge(sl.rt, 1)
            dve.reciprocal(TINY[:, 0:32], TINY[:, 64:96])
            dve.drain()
            dve.tensor_scalar(TINY[:, 0:32], TINY[:, 0:32], 1.0 - LAMBDA_INIT, None, ALU.mult)
            dve.drain()
        c = step - NC_
        dve.tensor_tensor(head(c), head(c), TINY[:, c * 8:(c + 1) * 8].unsqueeze(2).to_broadcast([P, 8, P]),
                          ALU.mult)

    T3 = a_("T3", 16, [P, NC_, 6 * NSA_G * HD])
    QF = a_("QF", 40, [P, KT, SEQ])
    KF = [a_("KSF", 56, [P, NSA_G, SEQ]), a_("KWF", 64, [P, NSA_G, SEQ])]
    TABN, RABN, TMPN = a_("TABN", 72, [P, NC_, 2, HD]), a_("RABN", 74, [P, NC_, 2, HD]), a_("TMPN", 76, [P, DM])
    TABKN, TMPK = a_("TABKN", 64, [P, NC_, 2, HD]), a_("TMPK", 60, [P, DM])
    RABKS, RABKW = a_("RABKS", 56, [P, NC_, 2, HD]), a_("RABKW", 58, [P, NC_, 2, HD])
    ON = a_("ON", 0, [P, NC_, DM])
    nq, nkv = turn(left_s, left=8), turn(left_s, left=12)

    CW = [a_("CWK", 40, [P, 16, CMP_HIDDEN]), a_("CWV", 56, [P, 16, CMP_HIDDEN])]
    KC2 = a_("KC2", 72, [P, NSA_G, SEQ])
    RH = a_("RH", 80, [P, 16, P])
    HV = a_("HV", 40, [P, 2, NSA_G, 4, 32])
    VBD = a_("VBD", 84, [P, NSA_G, 4 * HD])
    CKT = a_("CKT", 72, [P, 4, 2, HD])
    cm = sems("cm", "w tr kc2 rh hid gel out ss rt kn kt pos")

    def cmp_dma(act):
        for n, (w1, w2_, pos) in enumerate((("cmp_k_w1_2", "cmp_k_w2_2", "cmp_pos_k_2"),
                                            ("cmp_v_w1_2", "cmp_v_w2_2", "cmp_pos_v_2"))):
            act.dma_start(CW[n][:, :, :], A[w1][0].rearrange("(k p) c -> p k c", p=P)).then_inc(cm.w, 16)
            act.dma_start(CW2[n][:, :, :], A[w2_][0].rearrange("(k p) c -> p k c", p=P)).then_inc(cm.w, 16)
            act.dma_start(CPROW[16 * n:16 * n + 16, :], A[pos][0].rearrange("(k l) d -> k (l d)", l=2)).then_inc(cm.w, 16)
        act.dma_start(TABK[:, :, :], A["rope_cmp"]).then_inc(cm.w, 16)

    HID = (PS[:, 4, 0:2 * P], PS[:, 1, 0:2 * P])

    def cmp_pe(pe):
        pe.wait_ge(cm.w, 16 * 7)
        pe.transpose(PS[:, 5, 0:32], CPROW[:, :], IDF[0:32, 0:32]).then_inc(cm.pos, 1)
        for n in range(2):
            for j in range(2):
                for c in range(NC_):
                    last = pe.transpose(PS[:, 2 * n + j, c * P:(c + 1) * P],
                                        T3[:, c, n * 256 + j * P:n * 256 + (j + 1) * P], IDF[:, :])
            last.then_inc(cm.tr, 1)
        for n in range(2):
            pe.wait_ge(cm.rh, n + 1)
            for m in range(2):
                for k in range(16):
                    last = pe.matmul(HID[n][:, m * P:(m + 1) * P], CW[n][:, k, m * P:(m + 1) * P], RH[:, k, :],
                                     start=k == 0, stop=k == 15)
            last.then_inc(cm.hid, 1)
            if n == 0:
                pe.wait_ge(cm.gel, 1)
                for m in range(2):
                    last = pe.matmul(PS[:, 5, 0:HD], TINY[:, m * P:(m + 1) * P], CW2[0][:, m, :],
                                     start=m == 0, stop=m == 1)
                last.then_inc(cm.out, 1)
        pe.wait_ge(cm.kn, 1)
        pe.transpose(PS[:, 6, 0:P], CKT[:, 3, :, :].rearrange("p a d -> p (a d)"), IDF[:, :]).then_inc(cm.kt, 1)
        pe.wait_ge(cm.gel, 2)
        for g in range(NSA_G):
            for m in range(2):
                last = pe.matmul(PS[:, 7, g * HD:(g + 1) * HD], HV[:, m, g, :, :].rearrange("p a n -> p (a n)"),
                                 CW2[1][:, m, :], start=m == 0, stop=m == 1)
        last.then_inc(cm.out, 1)

    def cmp_act(act):
        for n in range(2):
            act.wait_ge(cm.tr, n + 1)
            if n:
                act.wait_ge(cm.rh, 1)
            for g in range(NSA_G):
                half, bank = slice((g % 2) * HD, (g % 2 + 1) * HD), 2 * n + g // 2
                act.activation(KC2[0:HD, g, :], PS[half, bank, :], ACT.Copy)
                act.activation(KC2[HD:P, g, 0:SEQ - 1], PS[half, bank, 1:SEQ], ACT.Copy)
            act.drain().then_inc(cm.kc2, 1)
        act.wait_ge(cm.hid, 1)
        act.activation(TINY[:, 0:2 * P], HID[0], ACT.Gelu_apprx_tanh).then_inc(cm.gel, 1)
        act.wait_ge(cm.ss, 1)
        act.activation(LAM[:, 5:6], LAM[:, 6:7], ACT.Sqrt, bias=EPS[:, 1:2], scale=1.0 / HD).then_inc(cm.rt, 1)
        act.wait_ge(cm.kt, 1)
        act.activation(KCF[:, :, :], PS[:, 6, 0:P].rearrange("p (g n) -> p g n", g=NSA_G), ACT.Copy)
        act.wait_ge(cm.hid, 2)
        for r in range(4):
            act.activation(HV[:, :, :, r, :], HID[1].rearrange("p (m g n) -> p m g n", m=2, g=NSA_G),
                           ACT.Gelu_apprx_tanh)
        act.drain().then_inc(cm.gel, 1)

    def cmp_dve(dve):
        dve.wait_ge(cm.pos, 1)
        dve.tensor_copy(CPOS[:, :, :], PS[:, 5, 0:32].rearrange("p (n k) -> p n k", n=2))
        dve.memset(RH[:, :, :], 0.0)
        dve.drain()
        for n in range(2):
            if n:
                dve.wait_ge(cm.hid, 1)
            dve.wait_ge(cm.kc2, n + 1)
            for k in range(16):
                dst = RH[:, k, :].rearrange("p (g n) -> p g n", g=NSA_G)[:, :, 0:NCMP]
                src = KC2[:, :, 2 * k:2 * k + CMP_STRIDE * (NCMP - 1) + 1:CMP_STRIDE]
                dve.tensor_scalar(dst, src, CPOS[:, n, k:k + 1], None, ALU.add)
            dve.drain().then_inc(cm.rh, 1)
        dve.wait_ge(cm.out, 1)
        dve.tensor_copy(CKT[:, 0, 0, :], PS[:, 5, 0:HD])
        dve.drain()
        dve.tensor_tensor(CKT[:, 0, 1, :], CKT[:, 0, 0, :], CKT[:, 0, 0, :], ALU.mult)
        dve.drain()
        dve.tensor_reduce(LAM[:, 6:7], CKT[:, 0, 1, :], AX, ALU.add).then_inc(cm.ss, 1)
        dve.wait_ge(cm.rt, 1)
        dve.reciprocal(LAM[:, 7:8], LAM[:, 5:6])
        dve.drain()
        x, h = CKT[:, 0, 0, :], HD // 2
        dve.tensor_scalar(x, x, LAM[:, 7:8], None, ALU.mult)
        dve.drain()
        dve.tensor_tensor(x, x, BCP[:, B_GAIN["kc"]:B_GAIN["kc"] + HD], ALU.mult)
        dve.drain()
        dve.tensor_tensor(CKT[:, 1, 0, :], x, TABK[:, 0, :], ALU.mult)
        dve.tensor_tensor(CKT[:, 1, 1, 0:h], x[:, h:HD], TABK[:, 1, 0:h], ALU.mult)
        dve.tensor_tensor(CKT[:, 1, 1, h:HD], x[:, 0:h], TABK[:, 1, h:HD], ALU.mult)
        dve.drain()
        for a in range(2):
            dve.tensor_tensor(CKT[:, 3, a, :], CKT[:, 1, 0, :], CKT[:, 1, 1, :], ALU.add)
        dve.drain().then_inc(cm.kn, 1)
        dve.wait_ge(cm.hid, 2)
        dve.memset(VBD[:, :, :], 0.0)
        dve.drain()
        dve.wait_ge(cm.out, 2)
        for a in range(4):
            rows_ = slice(32 * a, 32 * a + 32)
            dve.tensor_copy(VBD[rows_, :, a * HD:(a + 1) * HD], per(PS[rows_, 7, 0:256], NSA_G))

    NCH = NSA_G * NC_ * HPG
    SC = [T3[:, g, 0:512].rearrange("p (n k) -> p n k", k=32) for g in range(NSA_G)]
    CMASK = T3[:, 0, 512:512 + P].rearrange("p (c n) -> p c n", c=NC_)
    PTC = a_("PTC", 72, [P, 2, SEQ])
    GFM = PTC[:, 0, :]
    ca = sems("ca", "gate sig mask sc m ex p tr pt o od")

    def cattn_pe(pe):
        narrow_pe(pe, nr[2], 6, SW[1], 0, 48, GFM).then_inc(ca.gate, 1)
        pe.wait_ge(ca.sig, 1)
        for g in range(NSA_G):
            for r in range(2):
                half = slice(r * HD, (r + 1) * HD)
                for k in range(2 * NC_):
                    qb, j = divmod(k, 2)
                    last = pe.matmul(PS[:, g + 4 * r, k * 32:(k + 1) * 32],
                                     QF[half, 2 * g + j, qb * P:(qb + 1) * P], KCF[half, g, :], start=True, stop=True)
            last.then_inc(ca.sc, 1)
        for g in range(NSA_G + 1):
            if g < NSA_G:
                pe.wait_ge(ca.p, g + 1)
                if g >= 2:
                    pe.wait_ge(ca.pt, g - 1)
                for qb in range(NC_):
                    last = pe.transpose(PS[:, g % 2, qb * P:(qb + 1) * P], T3[:, g, qb * P:(qb + 1) * P], IDF[:, :])
                last.then_inc(ca.tr, 1)
            if g:
                q = g - 1
                pe.wait_ge(ca.pt, q + 1)
                if q >= 2:
                    pe.wait_ge(ca.od, q - 1)
                for qb in range(NC_):
                    last = pe.matmul(PS[:, 2 + 2 * (q % 2) + qb // 2, (qb % 2) * 256:(qb % 2) * 256 + 256],
                                     PTC[:, q % 2, qb * P:(qb + 1) * P], VBD[:, q, :], start=True, stop=True)
                last.then_inc(ca.o, 1)

    def cattn_act(act):
        act.wait_ge(ca.gate, 1)
        act.activation(GT[:, :, :], PS[:, 7, 0:192].rearrange("p (c k) -> p c k", c=NC_), ACT.Sigmoid)
        act.drain().then_inc(ca.sig, 1)
        for g in range(NSA_G):
            act.wait_ge(ca.m, g + 1)
            act.activation(SC[g], SC[g], ACT.Exp).then_inc(ca.ex, 1)
        for g in range(NSA_G):
            act.wait_ge(ca.tr, g + 1)
            if g >= 2:
                act.wait_ge(ca.o, g - 1)
            act.activation(PTC[:, g % 2, :], PS[:, g % 2, :], ACT.Copy).then_inc(ca.pt, 1)

    def cattn_pool(pool):
        pool.memset(CMASK[:, :, :], 0.0)
        pool.drain().then_inc(ca.mask, 1)
        pool.wait_ge(ca.mask, 1)
        pool.affine_select(out=CMASK[:, :, :], in_=CMASK[:, :, :], compare_op=ALU.is_ge, fill=MASKED,
                           base=-(CMP_BLOCK - 1), pattern=[[P, NC_], [-CMP_STRIDE, 32]], channel_multiplier=1)
        pool.drain().then_inc(ca.mask, 1)

    def cattn_dve(dve):
        n = NC_ * HPG
        narrow_dve(dve, nr[2], 6, 48, GFM)
        dve.wait_ge(ca.mask, 2)
        dve.wait_ge(ca.sig, 1)

        def over(ap, k):
            return ap.unsqueeze(2).to_broadcast([P, k, 32])

        for g in range(NSA_G):
            sc, mx = SC[g], TINY[:, n * g:n * (g + 1)]
            dve.wait_ge(ca.sc, g + 1)
            for r in range(2):
                dve.tensor_tensor(sc.rearrange("p (a b two) k -> p a b two k", a=NC_, two=2)[:, :, :, r, :],
                                  PS[:, g + 4 * r, 0:256].rearrange("p (a b k) -> p a b k", a=NC_, b=2),
                                  CMASK[:, :, :].unsqueeze(2).to_broadcast([P, NC_, 2, 32]), ALU.add)
            dve.drain()
            dve.tensor_reduce(mx, sc, AX, ALU.max)
            dve.drain()
            dve.tensor_scalar(mx, mx, MASKED / 10, None, ALU.max)
            dve.drain()
            dve.tensor_tensor(sc, sc, over(mx, n), ALU.subtract)
            dve.drain().then_inc(ca.m, 1)
        dve.wait_ge(ca.ex, NSA_G)
        total, inv, scale = (TINY[:, k * NCH:(k + 1) * NCH] for k in (1, 2, 3))
        for g in range(NSA_G):
            dve.tensor_reduce(total[:, n * g:n * (g + 1)], SC[g], AX, ALU.add)
        dve.drain()
        dve.tensor_scalar(total, total, 1e-30, None, ALU.max)
        dve.drain()
        dve.reciprocal(inv, total)
        dve.drain()
        for g in range(NSA_G):
            dve.tensor_tensor(scale[:, n * g:n * (g + 1)].rearrange("p (a b) -> p a b", a=NC_),
                              inv[:, n * g:n * (g + 1)].rearrange("p (a b) -> p a b", a=NC_),
                              GT[:, :, 12 * g:12 * g + 10:3], ALU.mult)
        dve.drain()
        for g in range(NSA_G):
            dve.tensor_tensor(SC[g], SC[g], over(scale[:, n * g:n * (g + 1)], n), ALU.mult)
            dve.drain().then_inc(ca.p, 1)
        for g in range(NSA_G):
            dve.wait_ge(ca.o, g + 1)
            for b in range(2):
                dve.tensor_copy(ON[:, 2 * b:2 * b + 2, g * 256:(g + 1) * 256],
                                PS[:, 2 + 2 * (g % 2) + b, :].rearrange("p (a k) -> p a k", a=2))
            dve.drain().then_inc(ca.od, 1)

    QZN = a_("QZN", 76, [P, HPG, SEQ])
    PTN = a_("PTN", 72, [P, 2, SEQ])
    OTMP = a_("OTMP", 84, [P, NC_, HD])
    NSTEP = HPG * 2 * NC_
    na = attn_turn(NSA_G, NSTEP, 4)

    def pn(t, a, b):
        return T3[:, t % NP, a:b]

    def zero_rows(pool):
        for T in (KF[0], KF[1], QZN):
            pool.memset(T[HD:P, :, :], 0.0)

    def nsa_pe(pe):
        attn_pe(pe, na, NSA_G, NSTEP, 4,
                lambda g, t: scores_pe(pe, t % 4, QZN[:, t // 8, (t % 4) * P:(t % 4 + 1) * P],
                                       lambda n: flat(KF[t // 4 % 2][:, ds(g, 1), 0:n]), t % 4),
                lambda k, b: pn(k, b * P, (b + 1) * P), PTN,
                lambda g, k, b: T3[:, b, ds(768 + 512 * (k // 4 % 2) + HD * g, HD)], (na.ex, na.at.ex + 4 + 1), HD)

    def nsa_act(act):
        exps, _ = one_softmax(act, None, pn)
        attn_act(act, na, NSA_G, NSTEP, 4, lambda g: head_queries(act, QZN, QF, g), exps, PTN)

    def nsa_dve(dve):
        def output(g, q):
            hh, branch = q // 2, q % 2
            inv, rw = (RW[:, 8 * (q % 2) + r:8 * (q % 2) + r + 4] for r in (0, 4))
            dve.reciprocal(inv, RS[:, 4 * (q % 4):4 * (q % 4) + 4])
            dve.drain()
            dve.tensor_tensor(rw.unsqueeze(2), inv.unsqueeze(2),
                              GT[:, :, ds(12 * g + 3 * hh + 1 + branch, 1)], ALU.mult)
            dve.drain()
            dve.tensor_tensor(OTMP[:, :, :], PS[:, 6 + q % 2, 0:256].rearrange("p (c d) -> p c d", c=NC_),
                              rw.unsqueeze(2).to_broadcast([P, NC_, HD]), ALU.mult)
            dve.drain()
            o = ON[:, :, ds(g * 256 + hh * HD, HD)]
            return dve.tensor_tensor(o, o, OTMP[:, :, :], ALU.add)
        _, maxima = one_softmax(None, dve, None)
        attn_dve(dve, na, NSA_G, NSTEP, maxima, output)

    YNH = a_("YNH", 16, [P, KT, SEQ], F32R)
    YNL = a_("YNL", 32, [P, KT, SEQ], F32R)
    MXH = a_("MXH", 48, [P, KT, SEQ], F32R)
    MXL = a_("MXL", 64, [P, KT, SEQ], F32R)
    SG = a_("SG", 0, [P, 4, SEQ])
    MT = a_("MT", 8, [P, 4, SEQ])
    mg = sems("mg", "sig y hi free")

    def merge_pe(pe):
        def body(i):
            for u in range(8):
                jj = u // 4
                if u % 4 == 0:
                    pe.wait_ge(mg.free, 2 * i + jj + 1)
                ah, al = ((YDH, YDL), (YNH, YNL), (XH, XL), (XH, XL))[u % 4]
                unit_fm(pe, first["merge"], 8, i, u, PS[:, u, :], ah, al)
        loop(pe, "merge", body)

    def merge_act(act):
        def body(i):
            for u in range(8):
                jj = u // 4
                ring_step(hi, act, "merge", i, u)
                if u % 4 >= 2:
                    act.wait_ge(mg.free, 2 * i + jj + 1)
                    act.wait_ge(unit_done, first["merge"] + 8 * i + u + 1)
                    act.activation(SG[:, 2 * jj + u % 4 - 2, :], PS[:, u, :], ACT.Sigmoid).then_inc(mg.sig, 1)
                if u % 4 == 3:
                    act.wait_ge(mg.y, 2 * i + jj + 1)
                    act.activation(MXH[:, ds(2 * i + jj, 1), :], MT[:, 2 * jj:2 * jj + 1, :],
                                   ACT.Copy).then_inc(mg.hi, 1)
        loop(act, "merge", body)

    def merge_dve(dve):
        dve.drain().then_inc(mg.free, 2)

        def body(i):
            for u in range(8):
                jj = u // 4
                ring_step(lo, dve, "merge", i, u)
                if u % 4 < 3:
                    continue
                dve.wait_ge(mg.sig, 2 * (2 * i + jj) + 2)
                dve.wait_ge(unit_done, first["merge"] + 8 * i + u + 1)
                for k in range(2):
                    dve.tensor_tensor(MT[:, 2 * jj + k, :], SG[:, 2 * jj + k, :], PS[:, 4 * jj + k, :], ALU.mult)
                dve.drain()
                dve.tensor_tensor(MT[:, 2 * jj, :], MT[:, 2 * jj, :], MT[:, 2 * jj + 1, :],
                                  ALU.add).then_inc(mg.y, 1)
                dve.wait_ge(mg.hi, 2 * i + jj + 1)
                dve.tensor_tensor(MXL[:, ds(2 * i + jj, 1), :], MT[:, 2 * jj:2 * jj + 1, :],
                                  MXH[:, ds(2 * i + jj, 1), :], ALU.subtract)
                dve.drain().then_inc(mg.free, 1)
        loop(dve, "merge", body)

    MH = a_("MH", 0, [P, 16, SEQ], F32R)
    ML = a_("ML", 32, [P, 16, SEQ], F32R)
    RL = a_("RL", 64, [P, 4, SEQ])

    up_s = shared("up", "relu y hi")

    def mlp_up(name, s, add=None, after=None):
        def f_pe(pe):
            if add is not None:
                pe.wait_ge(add, 2)

            def body(i):
                for u in range(2):
                    if after is None or not at_start(i, 0):
                        pe.wait_ge(s.relu, s.at.relu + 2 * i + u + 1)
                    unit_fm(pe, first[name], 2, i, u, PS[:, u, :], XH, XL,
                            None if after is None else normed(pe, after))
            loop(pe, name, body, peel=0 if after is None else 1)

        def f_act(act):
            act.drain().then_inc(s.relu, 2)

            def body(i):
                for u in range(2):
                    ring_step(hi, act, name, i, u)
                    act.wait_ge(unit_done, first[name] + 2 * i + u + 1)
                    act.wait_ge(s.y, s.at.y + 2 * i + u + 1)
                    act.activation(RL[:, u, :], PS[:, u, :], ACT.Relu).then_inc(s.relu, 1)
                    act.wait_ge(s.y, s.at.y + 2 * i + u + 3)
                    act.activation(MH[:, ds(2 * i + u, 1), :], RL[:, 2 + u:3 + u, :], ACT.Copy).then_inc(s.hi, 1)
            loop(act, name, body)

        def f_dve(dve):
            dve.drain().then_inc(s.y, 2)
            if add is not None:
                add_banks(dve, add)

            def body(i):
                for u in range(2):
                    ring_step(lo, dve, name, i, u)
                    dve.wait_ge(s.relu, s.at.relu + 2 * i + u + 3)
                    dve.tensor_tensor(RL[:, 2 + u, :], RL[:, u, :], RL[:, u, :], ALU.mult).then_inc(s.y, 1)
                    dve.wait_ge(s.hi, s.at.hi + 2 * i + u + 1)
                    dve.tensor_tensor(ML[:, ds(2 * i + u, 1), :], RL[:, 2 + u:3 + u, :], MH[:, ds(2 * i + u, 1), :],
                                      ALU.subtract)
                    dve.drain()
            loop(dve, name, body)
        return f_pe, f_act, f_dve, None

    def add_banks(dve, done):
        for m in range(KT):
            dve.tensor_tensor(X[:, m, :], X[:, m, :], PS[:, m, :], ALU.add).then_inc(done, 1)

    n0, n1, n2, n3 = (norm_turn(xl=n) for n in (KT, KT, KT, 0))
    f0, f1 = ffn_turn(), ffn_turn()
    ua, ub = (turn(up_s, relu=2 + 16, y=2 + 16, hi=16) for _ in range(2))
    fin = sems("fin", "half add tr out st")
    OT = a_("OT", 0, [P, NC_, DM])

    r0, r1 = (turn(norm_s, cent=KT, sq=KT, ssq=KT, std=1, tmp=KT, hi=KT, xl=KT) for n in range(2))

    def tm_stage(name, s, dst, loads=None, rope=None, after=None, behind=None, beside=None):
        if rope is None:
            def f_act(act):
                if loads is not None:
                    loads(act)
                tm_act(act, name, s, dst, beside and beside[0])

            def f_dve(dve):
                if beside is None:
                    return split_only(lo, dve, name)
                for p in range(size[name][0] * size[name][1]):
                    ring_step(lo, dve, name, *divmod(p, 4))
                    beside[1](dve, p)
            return ((lambda e: tm_pe(e, name, s, behind, None if after is None else normed(e, after))), f_act,
                    f_dve, None)

        T, nh, RAB, gain, TABC, tabs_at, TMP = rope
        r = turn(rope_s, tab=1, ss=NC_, rt=NC_)
        U, bodies = size[name]

        def f_pool(pool):
            pool.wait_ge(tabs, tabs_at)
            rope_tables_pool(pool, RAB, TABC, B_GAIN[gain], r.tab)

        def f_act(act):
            if loads is not None:
                loads(act)
            for p in range(U * bodies):
                i, u = divmod(p, U)
                ring_step(hi, act, name, i, u)
                c = p // 2
                if p % 2 == 0 and c < NC_:
                    act.wait_ge(r.ss, r.at.ss + c + 1)
                    act.activation(TINY[:, 256 + c * nh:256 + (c + 1) * nh], TINY[:, c * nh:(c + 1) * nh], ACT.Sqrt,
                                   bias=EPS[:, 1:2], scale=1.0 / HD).then_inc(r.rt, 1)
                if u == U - 1:
                    tm_copies(act, name, s, dst, i)

        def f_dve(dve):
            for p in range(U * bodies):
                ring_step(lo, dve, name, *divmod(p, U))
                c = p // 2
                if c >= NC_:
                    continue
                ss = TINY[:, c * nh:(c + 1) * nh]
                if p % 2 == 0:
                    head_ss_chunk(dve, T(c), ss, TMP)
                    dve.drain().then_inc(r.ss, 1)
                else:
                    if c == 0:
                        dve.wait_ge(r.tab, r.at.tab + 1)
                    dve.wait_ge(r.rt, r.at.rt + c + 1)
                    dve.reciprocal(ss, TINY[:, 256 + c * nh:256 + (c + 1) * nh])
                    dve.drain()
                    rope_chunk(dve, T(c), T(c), nh, RAB, c, ss, TMP)
        return (lambda e: tm_pe(e, name, s, behind)), f_act, f_dve, f_pool

    def finish_pe(pe):
        for f in range(KT):
            pe.wait_ge(fin.add, f + 1)
            if f >= 4:
                pe.wait_ge(fin.out, f - 3)
            for c in range(NC_):
                last = pe.transpose(PS[:, f % 4, c * P:(c + 1) * P], X[:, f, c * P:(c + 1) * P], IDF[:, :])
            last.then_inc(fin.tr, 1)

    def finish_dve(dve):
        add_banks(dve, fin.add)
        for f in range(KT):
            dve.wait_ge(fin.tr, f + 1)
            dve.tensor_copy(OT[:, :, f * P:(f + 1) * P],
                            PS[:, f % 4, :].rearrange("p (c t) -> p c t", c=NC_)).then_inc(fin.out, 1)

    def stages(e, kind):
        fns = STAGES[kind]
        for k, fn in enumerate(fns):
            if fn is not None:
                fn(e)
            barrier(e, kind, wait=not (kind == "pe" and plan[k][-1] == AHEAD))

    AHEAD = "ahead"
    plan = [
        (setup_pe, setup_act, setup_dve, setup_pool),
        (gate_pe, gate_act, gate_dve, None, AHEAD),
        (xbc_pe, xbc_act, xbc_dve, None),
        (ssd_pe, ssd_act, ssd_dve, None),
        (ssdh_pe, ssdh_act, ssdh_dve, None),
        (gnorm_pe, gnorm_act, gnorm_dve, None),
        (lambda e: kmajor_pe(e, "out0", YH, YL), lambda e: split_only(hi, e, "out0"),
         lambda e: split_only(lo, e, "out0"), None),
        (lambda e: ln_pe(e, n0), lambda e: ln_act(e, n0, C_LMG, C_LMB),
         lambda e: ln_dve(e, n0, C_LMG, C_LMB), None, AHEAD),
        (lambda e: ffn_up_pe(e, 0, f0, normed(e, n0)),
         lambda e: ffn_up_act(e, 0, f0), lambda e: ffn_up_dve(e, 0, f0), None, AHEAD),
        (lambda e: kmajor_pe(e, "down0", FH, FL, (f0.copied, f0.at.copied + 4 + 2 * FT)),
         lambda e: split_only(hi, e, "down0"), lambda e: split_only(lo, e, "down0"), None),
        (lambda e: ln_pe(e, n1), lambda e: ln_act(e, n1, C_LFG, C_LFB),
         lambda e: ln_dve(e, n1, C_LFG, C_LFB), None, AHEAD),
        (foxqk_pe, foxqk_stage_act, foxqk_stage_dve, lower_rows, AHEAD),
        (foxv_stage_pe, foxv_stage_act, foxv_stage_dve, None),
        (fox_pe, fox_act, fox_dve, None),
        split_fm(OB, OH, OL),
        (lambda e: kmajor_pe(e, "foxout", OH, OL), lambda e: split_only(hi, e, "foxout"),
         lambda e: split_only(lo, e, "foxout"), None),
        (lambda e: ln_pe(e, n2), lambda e: ln_act(e, n2, C_LMG + 8, C_LMB + 8),
         lambda e: ln_dve(e, n2, C_LMG + 8, C_LMB + 8), None, AHEAD),
        (lambda e: ffn_up_pe(e, 1, f1, normed(e, n2)),
         lambda e: ffn_up_act(e, 1, f1), lambda e: ffn_up_dve(e, 1, f1), None, AHEAD),
        (lambda e: kmajor_pe(e, "down1", FH, FL, (f1.copied, f1.at.copied + 4 + 2 * FT)),
         lambda e: split_only(hi, e, "down1"), lambda e: split_only(lo, e, "down1"), None),
        (lambda e: ln_pe(e, n3), lambda e: ln_act(e, n3, C_LFG + 8, C_LFB + 8, split=False),
         lambda e: ln_dve(e, n3, C_LFG + 8, C_LFB + 8, split=False), None),
        (lambda e: ssq_pe(e, r0), lambda e: rms_act(e, r0, C_MG2), lambda e: rms_dve(e, r0, C_MG2, False), None, AHEAD),
        tm_stage("dq", dq, TQ, after=r0, loads=lambda act: load_table(act, TABD)) + (AHEAD,),
        tm_stage("dk", dk, TK, rope=(heads_of(TQ), 16, RABQ, "dq", TABD, 16, TMPD), behind="tm") + (AHEAD,),
        tm_stage("dv", dvs, DV, rope=(heads_of(TK), 16, RABK, "dk", TABD, 16, TMPD), behind="tm"),
        to_fm([(lambda c, f=f: TQ[:, c, f * P:(f + 1) * P], DQF[:, f, :], SCALE) for f in range(KT)]
              + [(lambda c, f=f: TK[:, c, f * P:(f + 1) * P], DKF[:, f, :], 1.0) for f in range(KT)],
              lam_act, lam_dve, zero_halves),
        (diff_pe, diff_act, diff_dve, None),
        tm_stage("nq", nq, TQ, loads=lambda act: (load_table(act, TABN), cmp_dma(act)),
                 beside=(subln_act, subln_dve)),
        split_fm(OD, YDH, YDL, gain=PCOL[:, C_SUB:C_SUB + 1]),
        tm_stage("nkv", nkv, T3, rope=(heads_of(TQ), 16, RABN, "nq", TABN, 32, TMPN)),
        (cmp_pe, cmp_act, cmp_dve, None),
        rope_stage([(heads_of(T3, 512, 768), 4, RABKS, "ks"), (heads_of(T3, 1024, 1280), 4, RABKW, "kw")],
                   TABKN, TMPK, 48, load=True),
        to_fm([(lambda c, f=f: TQ[:, c, f * P:(f + 1) * P], QF[:, f, :], SCALE) for f in range(KT)]
              + [(lambda c, b=b, j=j: T3[:, c, 512 + 512 * b + j * P:512 + 512 * b + (j + 1) * P],
                  (KF[b][:, 2 * j, :], KF[b][:, 2 * j + 1, :]), 1.0) for b in range(2) for j in range(2)],
              pool_too=zero_rows),
        (cattn_pe, cattn_act, cattn_dve, cattn_pool),
        (nsa_pe, nsa_act, nsa_dve, None),
        split_fm(ON, YNH, YNL),
        (merge_pe, merge_act, merge_dve, None),
        (lambda e: kmajor_pe(e, "out2", MXH, MXL), lambda e: split_only(hi, e, "out2"),
         lambda e: split_only(lo, e, "out2"), None),
        (lambda e: ssq_pe(e, r1), lambda e: rms_act(e, r1, C_ML2), lambda e: rms_dve(e, r1, C_ML2, True), None, AHEAD),
        mlp_up("mupa", ua, after=r1) + (AHEAD,),
        (lambda e: kmajor_pe(e, "mdna", MH, ML, (ua.relu, ua.at.relu + 2 + 16)), lambda e: split_only(hi, e, "mdna"),
         lambda e: split_only(lo, e, "mdna"), None),
        mlp_up("mupb", ub, add=fin.half) + (AHEAD,),
        (lambda e: kmajor_pe(e, "mdnb", MH, ML, (ub.relu, ub.at.relu + 2 + 16)), lambda e: split_only(hi, e, "mdnb"),
         lambda e: split_only(lo, e, "mdnb"), None),
    ]
    plan.append((finish_pe, None, finish_dve, None))
    STAGES = {k: [p[j] for p in plan] for j, k in enumerate(("pe", "act", "dve", "pool"))}

    block = ctx.enter_context(nc.Block())

    @block.sync
    def _(sp):
        for name, U, bodies, src in STREAM:
            b = first[name]

            def body(i):
                for u in range(U):
                    slot = u % 2
                    s = src(i, u)
                    if not (b + u < 2 and isinstance(i, int)):
                        sp.wait_ge(lo_ready, b + u - 1 + U * i)
                    dst = RAW[:, slot, :].rearrange("p (k c) -> p k c", k=s.shape[1])
                    sp.dma_start(dst, s).then_inc(raw_loaded[slot], 16)
            start = 0
            if b == 0:
                body(0)
                start = 1
            with sp.Fori(start, bodies) as i:
                body(i)
        sp.wait_ge(stage_end, 4 * len(plan))
        sp.dma_start(out[0].rearrange("(c p) f -> p c f", p=P), OT[:, :, :]).then_inc(fin.st, 16)
        sp.wait_ge(fin.st, 16)

    @block.gpsimd
    def _(pool):
        stages(pool, "pool")

    @block.scalar
    def _(act):
        setup_dma(act)
        stages(act, "act")

    @block.vector
    def _(dve):
        stages(dve, "dve")

    @block.tensor
    def _(pe):
        stages(pe, "pe")

    ctx.close()


def constants():
    half = HD // 2
    inv = np.float32(10000.0) ** (-np.arange(half, dtype=np.float32) / np.float32(half))

    def table(pos):
        ang = pos.astype(np.float32)[:, None] * inv[None, :]
        c, s = np.cos(ang), np.sin(ang)
        return np.stack([np.concatenate([c, c], 1), np.concatenate([-s, s], 1)], 1).astype(np.float32)

    tok = table(np.arange(SEQ)).reshape(NC_, P, 2, HD).transpose(1, 0, 2, 3)
    centres = np.zeros((32, 2, HD), np.float32)
    centres[:NCMP] = table(np.arange(NCMP) * CMP_STRIDE + (CMP_BLOCK - 1) / 2.0)
    return {"rope_tok": np.ascontiguousarray(tok), "rope_cmp": np.ascontiguousarray(np.tile(centres, (NSA_G, 1, 1)))}


def kernel(**inputs):
    from concourse import bacc
    from concourse.bass_utils import run_bass_kernel_spmd

    nc = bacc.Bacc("TRN2", target_bir_lowering=False, num_devices=1)
    arrays, aps = {}, {}
    for name, value in {**inputs, **constants()}.items():
        a = np.ascontiguousarray(value)
        arrays[f"in_{name}"] = a
        aps[name] = nc.dram_tensor(f"in_{name}", a.shape, mybir.dt.from_np(a.dtype), kind="ExternalInput").ap()
    out = nc.dram_tensor("out", (1, SEQ, DM), F32, kind="ExternalOutput").ap()
    build(nc, aps, out)
    r = run_bass_kernel_spmd(nc, [arrays], core_ids=[0])
    return r.results[0]["out"]
```
